# Optimizing a Trainium2 kernel written in Bass

```python
import math
import jax, jax.numpy as jnp
from jax import lax
import numpy as np

D_MODEL = 1024
BATCH = 1
SEQ = 1024
DEPTH = 1
DEC_BATCH = 8
DEC_SEQ = 8
PAST_LEN = 1024
PAGE_SIZE = 128

HEAD_DIM = 64
ATTN_SCALE = HEAD_DIM ** -0.5
BLOCK = 128
A_Q_HEADS = 4
A_KV_HEADS = 2
A_GROUP = A_Q_HEADS // A_KV_HEADS
A_WINDOW = 128
B_HEADS = 6
B_BRANCHES = ((128, 1), (512, 4), (2048, 16))
B_SPAN = 2048
C_WIDTH = 6 * HEAD_DIM
CONV_WIDTH = 3
A_Q_W = A_Q_HEADS * HEAD_DIM
A_KV_W = A_KV_HEADS * HEAD_DIM
B_W = B_HEADS * HEAD_DIM
MIX_WIDTH = A_Q_W + B_W + C_WIDTH
IN_WIDTH = A_Q_W + 2 * A_KV_W + 3 * B_W + 3 * C_WIDTH
N_BUCKETS = 32
MAX_DISTANCE = 2048
N_ATT_HEADS = A_Q_HEADS + B_HEADS
N_GROUPS = 4
EXPERTS_PER_GROUP = 4
N_EXPERTS = N_GROUPS * EXPERTS_PER_GROUP
TOP_K = 2
EXPERT_FF = 512
RMS_EPS = 1e-6
NEG_INF = -1e30

kernel_name = 'hybrid_swa_dilated_shortconv_hmoe_step'

def rmsnorm(x, g):
    xf = x.astype(jnp.float32)
    y = xf * lax.rsqrt(jnp.mean(xf * xf, axis=-1, keepdims=True) + RMS_EPS)
    return (y * g.astype(jnp.float32)).astype(x.dtype)

def rel_bucket(dist):
    d = jnp.maximum(dist, 0)
    max_exact = N_BUCKETS // 2
    df = jnp.maximum(d, max_exact).astype(jnp.float32)
    large = max_exact + (jnp.log(df / max_exact) / math.log(MAX_DISTANCE / max_exact)
                         * (N_BUCKETS - max_exact)).astype(jnp.int32)
    large = jnp.minimum(large, N_BUCKETS - 1)
    return jnp.where(d < max_exact, d, large)

def rel_bias(table, dist, n_kv, n_group):
    b = table.astype(jnp.float32)[rel_bucket(dist)]
    return jnp.moveaxis(b, -1, 0).reshape(n_kv, n_group, *dist.shape)

def band_attention(q, k, v, max_dist, dist_scale, table):
    Bt, N, Hk, G, dh = q.shape
    nb = N // BLOCK
    qb = q.reshape(Bt, nb, BLOCK, Hk, G, dh)

    def band(x):
        xp = jnp.pad(x, ((0, 0), (BLOCK, 0), (0, 0), (0, 0))).reshape(Bt, nb + 1, BLOCK, Hk, dh)
        return jnp.concatenate([xp[:, :-1], xp[:, 1:]], axis=2)

    kb, vb = band(k), band(v)
    i = jnp.arange(BLOCK)[:, None]
    j = jnp.arange(2 * BLOCK)[None, :]
    dist = i + BLOCK - j
    key_idx = jnp.arange(nb)[:, None, None] * BLOCK + j[None] - BLOCK
    valid = (dist >= 0) & (dist <= max_dist) & (key_idx >= 0)
    bias = rel_bias(table, dist * dist_scale, Hk, G)
    logits = jnp.einsum('bnihgd,bnjhd->bnhgij', qb, kb).astype(jnp.float32) * ATTN_SCALE + bias
    logits = jnp.where(valid[None, :, None, None], logits, NEG_INF)
    lse = jax.nn.logsumexp(logits, axis=-1)
    p = jnp.exp(logits - lse[..., None])
    o = jnp.einsum('bnhgij,bnjhd->bnihgd', p.astype(v.dtype), vb).reshape(Bt, N, Hk, G, dh)
    lse = jnp.moveaxis(lse, -1, 2).reshape(Bt, N, Hk, G)
    return o, lse

def gather_attention(q, k_all, v_all, idx, dist, table):
    Hk, G = q.shape[2], q.shape[3]
    valid = idx >= 0
    safe = jnp.maximum(idx, 0)
    kg = k_all[:, safe]
    vg = v_all[:, safe]
    bias = rel_bias(table, dist, Hk, G)
    logits = jnp.einsum('bthgd,btmhd->bhgtm', q, kg).astype(jnp.float32) * ATTN_SCALE + bias
    logits = jnp.where(valid, logits, NEG_INF)
    lse = jax.nn.logsumexp(logits, axis=-1)
    p = jnp.exp(logits - lse[..., None])
    o = jnp.einsum('bhgtm,btmhd->bthgd', p.astype(vg.dtype), vg)
    return o, jnp.moveaxis(lse, -1, 1)

def apply_sinks(o, lse, sinks):
    s = sinks.astype(jnp.float32).reshape(A_KV_HEADS, A_GROUP)
    return o * jax.nn.sigmoid(lse - s)[..., None].astype(o.dtype)

def combine_branches(outs, lses):
    w = jax.nn.softmax(jnp.stack(lses), axis=0)
    o = jnp.sum(w[..., None] * jnp.stack(outs).astype(jnp.float32), axis=0)
    return o.astype(outs[0].dtype)

def to_strided(x, r, Sp):
    Bn, S = x.shape[:2]
    x = jnp.pad(x, ((0, 0), (0, Sp - S)) + ((0, 0),) * (x.ndim - 2))
    x = x.reshape(Bn, Sp // r, r, *x.shape[2:])
    return jnp.swapaxes(x, 1, 2).reshape(Bn * r, Sp // r, *x.shape[3:])

def from_strided(y, Bn, r, S):
    N, rest = y.shape[1], y.shape[2:]
    y = jnp.swapaxes(y.reshape(Bn, r, N, *rest), 1, 2)
    return y.reshape(Bn, N * r, *rest)[:, :S]

def dilated_prompt(q, k, v, table):
    Bn, S = q.shape[:2]
    outs, lses = [], []
    for w, r in B_BRANCHES:
        span = r * BLOCK
        Sp = -(-S // span) * span
        o, lse = band_attention(to_strided(q, r, Sp)[:, :, :, None], to_strided(k, r, Sp),
                                to_strided(v, r, Sp), w // r, r, table)
        outs.append(from_strided(o, Bn, r, S))
        lses.append(from_strided(lse, Bn, r, S))
    return combine_branches(outs, lses)

def dilated_sample(q, k_all, v_all, L, table):
    T = q.shape[1]
    t = jnp.arange(T)[:, None]
    outs, lses = [], []
    for w, r in B_BRANCHES:
        m = jnp.arange(w // r + 1)[None, :]
        idx = L + t - r * m
        dist = jnp.broadcast_to(r * m, idx.shape)
        o, lse = gather_attention(q[:, :, :, None], k_all, v_all, idx, dist, table)
        outs.append(o)
        lses.append(lse)
    return combine_branches(outs, lses)

def causal_conv(up, w):
    T = up.shape[1] - (CONV_WIDTH - 1)
    y = w[0] * up[:, 0:T]
    for j in range(1, CONV_WIDTH):
        y = y + w[j] * up[:, j:j + T]
    return y

def split_in(z):
    sizes = (A_Q_W, A_KV_W, A_KV_W, B_W, B_W, B_W, C_WIDTH, C_WIDTH, C_WIDTH)
    return jnp.split(z, np.cumsum(sizes)[:-1].tolist(), axis=-1)

def heads(x, n):
    return x.reshape(x.shape[0], x.shape[1], n, HEAD_DIM)

def mixer_prompt(h, w_in, conv_w, sinks, table):
    Bn, S = h.shape[:2]
    qa, ka, va, qb, kb, vb, xc, bg, cg = split_in(h @ w_in)
    qa = qa.reshape(Bn, S, A_KV_HEADS, A_GROUP, HEAD_DIM)
    ka, va = heads(ka, A_KV_HEADS), heads(va, A_KV_HEADS)
    oa, lse_a = band_attention(qa, ka, va, A_WINDOW, 1, table[:, :A_Q_HEADS])
    oa = apply_sinks(oa, lse_a, sinks)
    qb, kb, vb = heads(qb, B_HEADS), heads(kb, B_HEADS), heads(vb, B_HEADS)
    ob = dilated_prompt(qb, kb, vb, table[:, A_Q_HEADS:])
    up = jnp.pad(cg * xc, ((0, 0), (CONV_WIDTH - 1, 0), (0, 0)))
    oc = bg * causal_conv(up, conv_w)
    mix = jnp.concatenate([oa.reshape(Bn, S, A_Q_W), ob.reshape(Bn, S, B_W), oc], axis=-1)
    la, lb = min(A_WINDOW, S), min(B_SPAN, S)
    state = (ka[:, S - la:], va[:, S - la:], kb[:, S - lb:], vb[:, S - lb:], up[:, -(CONV_WIDTH - 1):])
    return mix, state

def mixer_sample(h, ca_k, ca_v, cb_k, cb_v, conv_state, w_in, conv_w, sinks, table):
    Bn, T = h.shape[:2]
    qa, ka, va, qb, kb, vb, xc, bg, cg = split_in(h @ w_in)
    qa = qa.reshape(Bn, T, A_KV_HEADS, A_GROUP, HEAD_DIM)
    ka, va = heads(ka, A_KV_HEADS), heads(va, A_KV_HEADS)
    La = ca_k.shape[1]
    t = jnp.arange(T)[:, None]
    m = jnp.arange(A_WINDOW + 1)[None, :]
    idx = La + t - m
    dist = jnp.broadcast_to(m, idx.shape)
    oa, lse_a = gather_attention(qa, jnp.concatenate([ca_k, ka], axis=1),
                                 jnp.concatenate([ca_v, va], axis=1), idx, dist, table[:, :A_Q_HEADS])
    oa = apply_sinks(oa, lse_a, sinks)
    qb, kb, vb = heads(qb, B_HEADS), heads(kb, B_HEADS), heads(vb, B_HEADS)
    ob = dilated_sample(qb, jnp.concatenate([cb_k, kb], axis=1), jnp.concatenate([cb_v, vb], axis=1),
                        cb_k.shape[1], table[:, A_Q_HEADS:])
    u = cg * xc
    up = jnp.concatenate([conv_state.astype(u.dtype), u], axis=1)
    oc = bg * causal_conv(up, conv_w)
    mix = jnp.concatenate([oa.reshape(Bn, T, A_Q_W), ob.reshape(Bn, T, B_W), oc], axis=-1)
    state = (ka, va, kb, vb, up[:, -(CONV_WIDTH - 1):])
    return mix, state

def hier_moe(h, w_group, b_group, w_router, b_router, w_gate, w_up, w_down):
    lead = h.shape[:-1]
    x = h.reshape(-1, D_MODEL)
    g_logits = (x @ w_group).astype(jnp.float32) + b_group.astype(jnp.float32)
    g_prob = jax.nn.softmax(g_logits, axis=-1)
    _, g_idx = lax.top_k(g_logits, 1)
    g_w = jnp.take_along_axis(g_prob, g_idx, axis=-1)
    e_logits = ((x @ w_router).astype(jnp.float32) + b_router.astype(jnp.float32)
                ).reshape(-1, N_GROUPS, EXPERTS_PER_GROUP)
    e_in = jnp.take_along_axis(e_logits, g_idx[:, :, None], axis=1)[:, 0]
    e_val, e_idx = lax.top_k(e_in, TOP_K)
    e_w = jax.nn.softmax(e_val, axis=-1) * g_w
    expert = g_idx * EXPERTS_PER_GROUP + e_idx
    combine = jnp.einsum('nk,nke->ne', e_w, jax.nn.one_hot(expert, N_EXPERTS, dtype=jnp.float32))
    hid = jax.nn.silu(jnp.einsum('nd,edf->nef', x, w_gate)) * jnp.einsum('nd,edf->nef', x, w_up)
    hid = hid * combine[..., None].astype(hid.dtype)
    y = jnp.einsum('nef,efd->nd', hid, w_down)
    return y.reshape(*lead, D_MODEL)

def setup_inputs(seed: int = 0) -> dict:
    key = jax.random.key(seed)
    ks = jax.random.split(key, 24)
    nrm = jax.random.normal
    La = min(A_WINDOW, PAST_LEN)
    Lb = min(B_SPAN, PAST_LEN)
    return {
        'x_prompt': nrm(ks[0], (BATCH, SEQ, D_MODEL), jnp.float32),
        'x_sample': nrm(ks[1], (DEC_BATCH, DEC_SEQ, D_MODEL), jnp.float32),
        'cache_a_k': nrm(ks[2], (DEPTH, DEC_BATCH, La, A_KV_HEADS, HEAD_DIM), jnp.float32),
        'cache_a_v': nrm(ks[3], (DEPTH, DEC_BATCH, La, A_KV_HEADS, HEAD_DIM), jnp.float32),
        'cache_b_k': nrm(ks[4], (DEPTH, DEC_BATCH, Lb, B_HEADS, HEAD_DIM), jnp.float32),
        'cache_b_v': nrm(ks[5], (DEPTH, DEC_BATCH, Lb, B_HEADS, HEAD_DIM), jnp.float32),
        'state_conv': nrm(ks[6], (DEPTH, DEC_BATCH, CONV_WIDTH - 1, C_WIDTH), jnp.float32),
        'rel_bias_table': 0.5 * nrm(ks[7], (N_BUCKETS, N_ATT_HEADS), jnp.float32),
        'w_in': nrm(ks[8], (DEPTH, D_MODEL, IN_WIDTH), jnp.float32) * D_MODEL ** -0.5,
        'w_out': nrm(ks[9], (DEPTH, MIX_WIDTH, D_MODEL), jnp.float32) * MIX_WIDTH ** -0.5,
        'conv_w': nrm(ks[10], (DEPTH, CONV_WIDTH, C_WIDTH), jnp.float32) * CONV_WIDTH ** -0.5,
        'attn_sinks': nrm(ks[11], (DEPTH, A_Q_HEADS), jnp.float32),
        'norm_mix': 1.0 + 0.05 * nrm(ks[12], (DEPTH, D_MODEL), jnp.float32),
        'norm_ffn': 1.0 + 0.05 * nrm(ks[13], (DEPTH, D_MODEL), jnp.float32),
        'w_group': nrm(ks[14], (DEPTH, D_MODEL, N_GROUPS), jnp.float32) * D_MODEL ** -0.5,
        'b_group': 0.01 * nrm(ks[15], (DEPTH, N_GROUPS), jnp.float32),
        'w_router': nrm(ks[16], (DEPTH, D_MODEL, N_EXPERTS), jnp.float32) * D_MODEL ** -0.5,
        'b_router': 0.01 * nrm(ks[17], (DEPTH, N_EXPERTS), jnp.float32),
        'w_gate': nrm(ks[18], (DEPTH, N_EXPERTS, D_MODEL, EXPERT_FF), jnp.float32) * D_MODEL ** -0.5,
        'w_up': nrm(ks[19], (DEPTH, N_EXPERTS, D_MODEL, EXPERT_FF), jnp.float32) * D_MODEL ** -0.5,
        'w_down': nrm(ks[20], (DEPTH, N_EXPERTS, EXPERT_FF, D_MODEL), jnp.float32) * EXPERT_FF ** -0.5,
        'norm_final': 1.0 + 0.05 * nrm(ks[21], (D_MODEL,), jnp.float32),
    }

def reference(x_prompt, x_sample, cache_a_k, cache_a_v, cache_b_k, cache_b_v, state_conv,
              rel_bias_table, w_in, w_out, conv_w, attn_sinks, norm_mix, norm_ffn,
              w_group, b_group, w_router, b_router, w_gate, w_up, w_down, norm_final):
    yp, ys = x_prompt, x_sample
    st_p = [[] for _ in range(5)]
    st_s = [[] for _ in range(5)]
    for l in range(DEPTH):
        mp, sp = mixer_prompt(rmsnorm(yp, norm_mix[l]), w_in[l], conv_w[l], attn_sinks[l], rel_bias_table)
        ms, ss = mixer_sample(rmsnorm(ys, norm_mix[l]), cache_a_k[l], cache_a_v[l], cache_b_k[l],
                              cache_b_v[l], state_conv[l], w_in[l], conv_w[l], attn_sinks[l], rel_bias_table)
        yp = yp + mp @ w_out[l]
        ys = ys + ms @ w_out[l]
        yp = yp + hier_moe(rmsnorm(yp, norm_ffn[l]), w_group[l], b_group[l], w_router[l], b_router[l],
                           w_gate[l], w_up[l], w_down[l])
        ys = ys + hier_moe(rmsnorm(ys, norm_ffn[l]), w_group[l], b_group[l], w_router[l], b_router[l],
                           w_gate[l], w_up[l], w_down[l])
        for i in range(5):
            st_p[i].append(sp[i])
            st_s[i].append(ss[i])
    y_prompt = rmsnorm(yp, norm_final)
    y_sample = rmsnorm(ys, norm_final)
    ak_p, av_p, bk_p, bv_p, cv_p = [jnp.stack(s) for s in st_p]
    ak_s, av_s, bk_s, bv_s, cv_s = [jnp.stack(s) for s in st_s]
    return (y_prompt, y_sample, ak_p, av_p, bk_p, bv_p, cv_p, ak_s, av_s, bk_s, bv_s, cv_s)


_drawn_inputs = setup_inputs


def setup_inputs(seed=0):
    import zlib

    import numpy as np

    out = dict(_drawn_inputs(seed))
    spreads = {}
    factors = {'attn_sinks': 8.0, 'b_group': 37.515, 'b_router': 10.596}
    for name, (base, spread) in spreads.items():
        noise = np.random.default_rng([zlib.crc32(name.encode()), seed]).standard_normal(out[name].shape)
        drawn = base * np.exp(spread * noise) if base else spread * noise
        out[name] = __import__('jax').numpy.asarray(drawn.astype(out[name].dtype))
    for name, factor in factors.items():
        out[name] = (out[name] * factor).astype(out[name].dtype)
    return out
```

```python
from contextlib import ExitStack
import math

import numpy as np

import concourse.bass as bass
from concourse import mybir

F32 = mybir.dt.float32
F32R = mybir.dt.float32r
I32 = mybir.dt.int32
U32 = mybir.dt.uint32
BF16 = mybir.dt.bfloat16
ALU = mybir.AluOpType
ACT = mybir.ActivationFunctionType
AX = mybir.AxisListType

P = 128
D = 1024
KD = D // P
SEQ = 1024
NB, NT = 8, 8
PAST = 1024
TOK = SEQ + NB * NT
QT_N = SEQ // P
TT = QT_N + 1
DH = 64
A_H, B_H = 4, 6
A_WIN = 128
BRANCHES = ((128, 1), (512, 4), (2048, 16))
BW = B_H * DH
VW = 2 * DH + BW
CH = BW // P
EPS = 1e-6
MASK = -1e30
SCALE = DH ** -0.5
NBUCK = 32
FAR = PAST + NT - 1
GW = FAR + P + 1
GPITCH = GW - 1
XA = SEQ - 2 * P
FARK, NEARK = 256, 512
SK = FARK + NEARK + NT
SKT = (FARK + NEARK) // P
AK = A_WIN + NT
NG, EPG = 4, 4
NE = NG * EPG
FF = 512
FT = FF // P
MAXB = 32
PIECES = ((0, 384), (384, 384), (768, 320))

W_IN_COL = {"qa": 0, "va": 384, "qb": 512, "kb": 896, "vb": 1280, "xc": 1664, "bg": 2048, "cg": 2432}
GROUPS = ("qb", "kb", "qa", "xc", "cg", "bg")


def tokens(t):
    return P if t < QT_N else NB * NT


def bias_rows():
    d = FAR - np.arange(GW)
    dist = np.maximum(d, 0)
    half = NBUCK // 2
    df = np.maximum(dist, half).astype(np.float32)
    large = half + (np.log(df / half) / math.log(2048 / half) * (NBUCK - half)).astype(np.int32)
    bucket = np.where(dist < half, dist, np.minimum(large, NBUCK - 1))
    out = np.zeros((NBUCK + 1, 2, GW), np.float32)
    branches = (((A_WIN, 1),), BRANCHES)
    for kind in range(2):
        seen = sum(((d >= 0) & (d <= w) & (d % r == 0)).astype(np.int64) for w, r in branches[kind])
        out[bucket, kind, np.arange(GW)] = seen > 0
        out[NBUCK, kind] = np.where(seen > 0, np.log(np.maximum(seen, 1)), MASK)
    return out


class Pools:

    def __init__(self, nc, stack):
        self.nc, self.stack = nc, stack

    def sb(self, name, shape, dt=F32):
        return self.stack.enter_context(self.nc.sbuf_tensor(name, shape, dt))

    def ps(self, name, shape, dt=F32):
        return self.stack.enter_context(self.nc.psum_tensor(name, shape, dt))

    def sem(self, name):
        return self.stack.enter_context(self.nc.semaphore(name))


def stepper(eng, sem):
    count = [0]

    def step(ins):
        count[0] += 1
        ins.then_inc(sem, 1)
        eng.wait_ge(sem, count[0])

    return step


def project_in(nc, io, keep):
    mixT, KT, V, ident = keep["mixT"], keep["KT"], keep["V"], keep["ident"]
    with ExitStack() as stack:
        p = Pools(nc, stack)
        xT_hi = p.sb("xT_hi", [P, KD, TOK], F32R)
        xT_rest = p.sb("xT_rest", [P, KD, TOK], F32R)
        w = keep["stage"][:, :].rearrange("p (s c) -> p s c", s=2)
        w_hi = p.sb("w_hi", [P, 2, KD * VW], F32R)
        w_rest = keep["w_rest"]
        smallT = p.sb("smallT", [P, CH, 19])
        V_flat = V[:, :, :].rearrange("p t c -> p (t c)")
        norm_g, scratch = V_flat[:, 0:D], V_flat[:, D:2 * D]
        bias_out = V_flat[:, 2 * D:2 * D + 2 * GW].rearrange("p (s y) -> p s y", s=2)
        UW = 2 + SEQ + NB * (NT + 2)
        U = V_flat[:, 0:CH * UW].rearrange("p (c t) -> p c t", c=CH)
        KT_flat = KT[:, :, :].rearrange("p k t -> p (k t)")
        HEADS = A_H + B_H
        table_cols = KT_flat[0:NBUCK + 1, 0:HEADS * P].rearrange("p (h c) -> p h c", h=HEADS)
        table = KT_flat[0:NBUCK + 1, HEADS * P:HEADS * P + HEADS]
        small = KT_flat[0:19, (HEADS + 1) * P:(HEADS + 1) * P + BW]
        onehot = KT_flat[0:NBUCK + 1, (HEADS + 4) * P:(HEADS + 4) * P + 2 * GW].rearrange("p (k y) -> p k y", k=2)
        XC = mixT[:, 8 - CH:8, :]
        xin = XC.rearrange("p c t -> p (c t)")
        stats = p.sb("stats", [P, TT, 3])
        eps = p.sb("eps", [P, 1])
        k_rows = w[:, 1, 0:2 * BW].rearrange("p (s c) -> p s c", s=2)
        conv_last = p.sb("conv_last", [P, CH, 18])
        conv_rows = p.sb("conv_rows", [18, BW])
        bank = [p.ps(f"bank{i}", [P, 512]) for i in range(8)]
        x_tile = [xin[:, D * i:D * (i + 1)] for i in range(3)]

        x_loaded = [p.sem(f"x_loaded{i}") for i in range(3)]
        xT_hi_made = p.sem("xT_hi_made")
        xT_rest_made = p.sem("xT_rest_made")
        w_hi_made = p.sem("w_hi_made")
        w_rest_made = p.sem("w_rest_made")
        w_loaded = [p.sem(f"w_loaded{i}") for i in range(2)]
        small_loaded = p.sem("small_loaded")
        g_loaded = p.sem("g_loaded")
        const_ready = p.sem("const_ready")
        pool_step = p.sem("pool_step")
        squared = p.sem("squared")
        rooted = p.sem("rooted")
        dve_step = p.sem("dve_step")
        normed = p.sem("normed")
        turned = p.sem("turned")
        bias_made = p.sem("bias_made")
        bias_act = p.sem("bias_act")
        bias_dve = p.sem("bias_dve")
        bias_stored = [p.sem(f"bias_stored{i}") for i in range(2)]
        small_turned = p.sem("small_turned")
        projected = p.sem("projected")
        act_out = p.sem("act_out")
        dve_out = p.sem("dve_out")
        v_made = p.sem("v_made")
        v_copied = p.sem("v_copied")
        k_turned = p.sem("k_turned")
        k_copied = p.sem("k_copied")
        k_stored = [p.sem(f"k_stored{i}") for i in range(2)]
        last_picked = p.sem("last_picked")
        last_turned = p.sem("last_turned")
        last_copied = p.sem("last_copied")
        stored = p.sem("stored")

        W_GROUPS = GROUPS + ("v",)
        act_pieces = {g: (0, 2) if g in ("qb", "kb", "qa", "xc") else () for g in GROUPS}
        dve_pieces = {g: tuple(i for i in range(3) if i not in act_pieces[g]) for g in GROUPS}

        def total(pieces, n):
            return sum(len(pieces[GROUPS[m // CH]]) for m in range(n + 1))

        K_JOBS = [("b", t) for t in range(TT)] + [("a", QT_N - 1), ("a", TT - 1)]

        WAITS = {"qa": 5, "v": 2}

        def w_part(buf, n, c):
            width = VW if W_GROUPS[n] == "v" else BW
            return buf[:, n % 2, KD // 2 * width * c:KD // 2 * width * (c + 1)]

        def w_tiles(buf, n):
            width = VW if W_GROUPS[n] == "v" else BW
            return buf[:, n % 2, 0:KD * width].rearrange("p (k c) -> p k c", k=KD)

        def w_count(n):
            return 16 * sum(WAITS.get(W_GROUPS[m], 1) for m in range(n % 2, n + 1, 2))

        block = stack.enter_context(nc.Block())

        @block.sync
        def _(sp):
            for t in range(3):
                sp.dma_start(x_tile[t], io["x"][t]).then_inc(x_loaded[t], 16)
            sp.dma_start(norm_g[:, :], io["norm_mix"].partition_broadcast(P)).then_inc(g_loaded, 16)
            sp.dma_start(onehot, io["bias_rows"]).then_inc(small_loaded, 16)
            sp.dma_start(table[0:NBUCK, :], io["table"]).then_inc(small_loaded, 16)
            sp.dma_start(small[0:16, :], io["state_conv"]).then_inc(small_loaded, 16)
            sp.dma_start(small[16:19, :], io["conv_w"]).then_inc(small_loaded, 16)

            def load_w(n):
                g, s = W_GROUPS[n], n % 2
                if n >= 2:
                    sp.wait_ge(projected, CH * (n - 1))
                if g == "v":
                    dst = w[:, s, :].rearrange("p (k c) -> p k c", k=KD)
                    sp.dma_start(dst[:, :, 0:P], io["w_in"][:, :, 384:512]).then_inc(w_loaded[s], 16)
                    sp.dma_start(dst[:, :, P:VW], io["w_in"][:, :, 1280:1664]).then_inc(w_loaded[s], 16)
                    return
                dst = w[:, s, 0:KD * BW].rearrange("p (k c) -> p k c", k=KD)
                c = W_IN_COL[g]
                if g == "qa":
                    for h in range(A_H):
                        at = P * (h % 2) + DH * (h // 2)
                        sp.dma_start(dst[:, :, at:at + DH], io["w_in"][:, :, DH * h:DH * h + DH]).then_inc(w_loaded[s], 16)
                    sp.dma_start(dst[:, :, 256:384], io["w_in"][:, :, 256:384]).then_inc(w_loaded[s], 16)
                else:
                    sp.dma_start(dst, io["w_in"][:, :, c:c + BW]).then_inc(w_loaded[s], 16)

            for t in range(3, TT):
                sp.wait_ge(turned, 2 * (t - 2))
                sp.dma_start(x_tile[t % 3][0:tokens(t), :], io["x"][t]).then_inc(x_loaded[t % 3], 16)
                if t == 5:
                    load_w(0)
            load_w(1)
            for h in range(HEADS):
                sp.wait_ge(bias_act, h + 1)
                sp.wait_ge(bias_dve, h + 1)
                sp.dma_start(io["bias"][h], bias_out[:, h % 2, :]).then_inc(bias_stored[h % 2], 16)
            for n in range(2, len(W_GROUPS)):
                load_w(n)
            for t in range(TT):
                sp.wait_ge(v_copied, t + 1)
                if t == QT_N - 1:
                    sp.dma_start(io["a_v_prompt"], V[:, t, 0:P]).then_inc(stored, 16)
                if t == QT_N:
                    sp.dma_start(io["a_v_sample"], V[0:NB * NT, t, 0:P]).then_inc(stored, 16)
                    sp.dma_start(io["b_v_sample"], V[0:NB * NT, t, P:VW]).then_inc(stored, 16)
                else:
                    sp.dma_start(io["b_v_prompt"][t], V[:, t, P:VW]).then_inc(stored, 16)
            sp.wait_ge(last_copied, 1)
            sp.dma_start(io["conv_prompt"], conv_rows[0:2, :]).then_inc(stored, 16)
            sp.dma_start(io["conv_sample"], conv_rows[2:18, :]).then_inc(stored, 16)
            for n, (kind, t) in enumerate(K_JOBS):
                sp.wait_ge(k_copied, n + 1)
                rows = k_rows[0:tokens(t), n % 2, 0:BW if kind == "b" else P]
                to = (io["b_k_sample"] if t == QT_N else io["b_k_prompt"][t]) if kind == "b" else \
                    (io["a_k_sample"] if t == QT_N else io["a_k_prompt"])
                sp.dma_start(to, rows).then_inc(k_stored[n % 2], 16)
            sp.wait_ge(stored, 16 * (TT + 2 + 2))
            sp.wait_ge(k_stored[0], 16 * 6)
            sp.wait_ge(k_stored[1], 16 * 5)
            for s in range(2):
                sp.wait_ge(bias_stored[s], 16 * HEADS // 2)

        @block.gpsimd
        def _(pool):
            nc.gpsimd.memset(ident[:, :], 0.0).then_inc(pool_step, 1)
            pool.wait_ge(pool_step, 1)
            nc.gpsimd.affine_select(out=ident[:, :], in_=ident[:, :], compare_op=ALU.not_equal, fill=1.0,
                                    base=0, pattern=[[-1, P]], channel_multiplier=1).then_inc(const_ready, 1)
            pool.wait_ge(const_ready, 1)
            nc.gpsimd.memset(eps[:, :], EPS).then_inc(const_ready, 1)
            pool.wait_ge(const_ready, 2)
            nc.gpsimd.memset(table[NBUCK:NBUCK + 1, :], 1.0).then_inc(const_ready, 1)
            pool.wait_ge(const_ready, 3)
            pool.wait_ge(small_loaded, 64)
            nc.gpsimd.tensor_copy(table_cols[:, :, :], table[:, :].unsqueeze(2).to_broadcast([NBUCK + 1, HEADS, P])).then_inc(const_ready, 1)

        @block.scalar
        def _(act):
            def root(t):
                n = tokens(t)
                act.wait_ge(squared, t + 1)
                nc.scalar.activation(stats[0:n, t, 1:2], stats[0:n, t, 0:1], ACT.Sqrt, bias=eps[0:n, :],
                                     scale=1.0 / D).then_inc(rooted, 1)

            def x_hi(t):
                m = tokens(t)
                for c in range(2):
                    act.wait_ge(turned, 2 * t + c + 1)
                    nc.scalar.activation(xT_hi[:, 4 * c:4 * c + 4, P * t:P * t + m],
                                         bank[2 * (t % 2) + c][:, :].rearrange("p (k c) -> p k c", k=4)[:, :, 0:m],
                                         ACT.Copy).then_inc(xT_hi_made, 1)

            def split_w(n):
                act.wait_ge(w_loaded[n % 2], w_count(n))
                for c in range(2):
                    nc.scalar.activation(w_part(w_hi, n, c), w_part(w, n, c), ACT.Copy).then_inc(w_hi_made, 1)

            act.wait_ge(const_ready, 2)
            for t in range(TT):
                n = tokens(t)
                act.wait_ge(x_loaded[t % 3], 16 * (t // 3 + 1))
                if t:
                    act.wait_ge(squared, t)
                nc.scalar.activation(scratch[0:n, :], x_tile[t % 3][0:n, :], ACT.Square,
                                     accum_out=stats[0:n, t, 0:1]).then_inc(squared, 1)
                root(t)
                if t >= 1:
                    x_hi(t - 1)
            x_hi(TT - 1)
            split_w(0)
            for h in range(HEADS):
                act.wait_ge(bias_made, h + 1)
                if h >= 2:
                    act.wait_ge(bias_stored[h % 2], 16 * (h // 2))
                nc.scalar.activation(bias_out[:, h % 2, 0:512], bank[3 * (h % 2)][:, :], ACT.Copy).then_inc(bias_act, 1)
            for n in range(CH * len(GROUPS)):
                g, j = GROUPS[n // CH], n % CH
                if g == "xc" and j == 0:
                    act.wait_ge(xT_rest_made, 2 * TT)
                for i in act_pieces[g]:
                    c, m = PIECES[i]
                    act.wait_ge(projected, n + 1)
                    src = bank[3 * (n % 2) + i][:, 0:m]
                    if g == "qb" or (g == "qa" and j < 2):
                        tile = 2 + j if g == "qb" else j
                        nc.scalar.activation(mixT[:, tile, c:c + m], src, ACT.Copy, scale=SCALE).then_inc(act_out, 1)
                    elif g == "xc":
                        nc.scalar.activation(XC[:, j, c:c + m], src, ACT.Copy).then_inc(act_out, 1)
                    else:
                        tile = 1 + j if g == "kb" else 0
                        nc.scalar.activation(KT[:, tile, c:c + m], src, ACT.Copy).then_inc(act_out, 1)
                if j == 0:
                    act.wait_ge(projected, n + 1)
                    split_w(n // CH + 1)
            act.wait_ge(last_picked, 1)
            for t in range(TT):
                act.wait_ge(v_made, t + 1)
                nc.scalar.activation(V[0:tokens(t), t, :], bank[6 + t % 2][0:tokens(t), :], ACT.Copy).then_inc(v_copied, 1)
            for n, (kind, t) in enumerate(K_JOBS):
                act.wait_ge(k_turned, n + 1)
                if n >= 2:
                    act.wait_ge(k_stored[n % 2], 16 * (n // 2))
                c, m = (BW if kind == "b" else P), tokens(t)
                nc.scalar.activation(k_rows[0:m, n % 2, 0:c], bank[n % 2][0:m, 0:c], ACT.Copy).then_inc(k_copied, 1)

        @block.vector
        def _(dve):
            step = stepper(dve, dve_step)

            def x_rest(t):
                n = tokens(t)
                for c in range(2):
                    dve.wait_ge(xT_hi_made, 2 * t + c + 1)
                    cols = (slice(None), slice(4 * c, 4 * c + 4), slice(P * t, P * t + n))
                    nc.vector.tensor_tensor(xT_rest[cols], bank[2 * (t % 2) + c][:, :].rearrange("p (k c) -> p k c", k=4)[:, :, 0:n],
                                            xT_hi[cols].bitcast(F32), ALU.subtract).then_inc(xT_rest_made, 1)

            def rest_w(n):
                for c in range(2):
                    dve.wait_ge(w_hi_made, 2 * n + c + 1)
                    nc.vector.tensor_tensor(w_part(w_rest, n, c), w_part(w, n, c), w_part(w_hi, n, c).bitcast(F32),
                                            ALU.subtract).then_inc(w_rest_made, 1)

            dve.wait_ge(g_loaded, 16)
            for t in range(TT):
                n = tokens(t)
                dve.wait_ge(rooted, t + 1)
                step(nc.vector.reciprocal(stats[0:n, t, 2:3], stats[0:n, t, 1:2]))
                nc.vector.scalar_tensor_tensor(out=x_tile[t % 3][0:n, :], in0=x_tile[t % 3][0:n, :],
                                               scalar=stats[0:n, t, 2:3], in1=norm_g[0:n, :],
                                               op0=ALU.mult, op1=ALU.mult).then_inc(normed, 1)
                if t:
                    x_rest(t - 1)
            x_rest(TT - 1)
            rest_w(0)
            for h in range(HEADS):
                dve.wait_ge(bias_made, h + 1)
                if h >= 2:
                    dve.wait_ge(bias_stored[h % 2], 16 * (h // 2))
                nc.vector.tensor_copy(bias_out[:, h % 2, 512:1024], bank[3 * (h % 2) + 1][:, :])
                nc.vector.tensor_copy(bias_out[:, h % 2, 1024:GW], bank[3 * (h % 2) + 2][:, 0:GW - 1024]).then_inc(bias_dve, 1)
            dve.wait_ge(small_turned, 1)
            step(nc.vector.tensor_copy(smallT[:, :, :], bank[6][:, 0:CH * 32].rearrange("p (c s) -> p c s", c=CH)[:, :, 0:19]))

            def begin_u():
                for i in range(2):
                    dve.wait_ge(bias_stored[i], 16 * HEADS // 2)
                step(nc.vector.memset(U[:, :, 0:2], 0.0))
                for j in range(CH):
                    step(nc.vector.tensor_copy(U[:, j, 2 + SEQ:].rearrange("p (b t) -> p b t", b=NB)[:, :, 0:2],
                                               smallT[:, j, 0:16].rearrange("p (b s) -> p b s", b=NB)))

            def u_cols(j, c, m, shift):
                out = []
                if c < SEQ:
                    m1 = min(m, SEQ - c)
                    out.append((U[:, j, c + shift:c + shift + m1], lambda a: a[:, 0:m1], m1))
                if c + m > SEQ:
                    m1 = max(0, SEQ - c)
                    v = U[:, j, 2 + SEQ:].rearrange("p (b t) -> p b t", b=NB)[:, :, shift:shift + NT]
                    out.append((v, lambda a: a[:, m1:m].rearrange("p (b t) -> p b t", b=NB), m - m1))
                return out

            for n in range(CH * len(GROUPS)):
                g, j = GROUPS[n // CH], n % CH
                if g == "cg" and j == 0:
                    begin_u()
                    dve.wait_ge(act_out, total(act_pieces, CH * 4 - 1))
                for i in dve_pieces[g]:
                    c, m = PIECES[i]
                    dve.wait_ge(projected, n + 1)
                    src = bank[3 * (n % 2) + i][:, 0:m]
                    if g == "qb" or (g == "qa" and j < 2):
                        tile = 2 + j if g == "qb" else j
                        nc.vector.tensor_scalar(mixT[:, tile, c:c + m], src, SCALE, None, ALU.mult).then_inc(dve_out, 1)
                    elif g == "cg":
                        for to, pick, _ in u_cols(j, c, m, 2):
                            ins = nc.vector.tensor_tensor(to, pick(src), pick(XC[:, j, c:c + m]), ALU.mult)
                        ins.then_inc(dve_out, 1)
                    elif g == "bg":
                        nc.vector.tensor_tensor(mixT[:, 5 + j, c:c + m], src, XC[:, j, c:c + m], ALU.mult).then_inc(dve_out, 1)
                    elif g == "xc":
                        nc.vector.tensor_copy(XC[:, j, c:c + m], src).then_inc(dve_out, 1)
                    else:
                        tile = 1 + j if g == "kb" else 0
                        nc.vector.tensor_copy(KT[:, tile, c:c + m], src).then_inc(dve_out, 1)
                if j == 0:
                    rest_w(n // CH + 1)
                if g == "cg":
                    dve.wait_ge(dve_out, total(dve_pieces, n))
                    for c, m in ((0, SEQ), (SEQ, NB * NT)):
                        for k in range(3):
                            (src, pick, _), = u_cols(j, c, m, k)
                            y = pick(XC[:, j, c:c + m])
                            tap = smallT[:, j, 16 + k:17 + k]
                            if k == 0:
                                step(nc.vector.tensor_scalar(y, src, tap, None, ALU.mult))
                            else:
                                step(nc.vector.scalar_tensor_tensor(out=y, in0=src, scalar=tap, in1=y,
                                                                    op0=ALU.mult, op1=ALU.add))
                    if j == CH - 1:
                        nc.vector.tensor_copy(conv_last[:, :, 0:2], U[:, :, SEQ:SEQ + 2])
                        nc.vector.tensor_copy(conv_last[:, :, 2:18].rearrange("p c (b s) -> p c b s", b=NB),
                                              U[:, :, 2 + SEQ:].rearrange("p c (b t) -> p c b t", b=NB)[:, :, :, NT:NT + 2]).then_inc(last_picked, 1)
            dve.wait_ge(last_turned, 1)
            nc.vector.tensor_copy(conv_rows[:, :], bank[5][0:18, 0:BW]).then_inc(last_copied, 1)

        @block.tensor
        def _(pe):
            pe.wait_ge(const_ready, 2)
            for t in range(TT):
                n = tokens(t)
                pe.wait_ge(normed, t + 1)
                if t >= 2:
                    pe.wait_ge(xT_rest_made, 2 * t - 2)
                for k in range(KD):
                    ins = nc.tensor.transpose(bank[2 * (t % 2) + k // 4][:, P * (k % 4):P * (k % 4) + n],
                                              x_tile[t % 3][0:n, P * k:P * k + P], ident[0:n, 0:n])
                    if k == 3:
                        ins.then_inc(turned, 1)
                ins.then_inc(turned, 1)
            pe.wait_ge(small_loaded, 64)
            for c in range(CH):
                ins = nc.tensor.transpose(bank[6][:, 32 * c:32 * c + 19], small[:, P * c:P * c + P], ident[0:19, 0:19])
            ins.then_inc(small_turned, 1)
            pe.wait_ge(const_ready, 4)
            pe.wait_ge(xT_rest_made, 2 * TT)
            for h in range(HEADS):
                if h >= 2:
                    pe.wait_ge(bias_act, h - 1)
                    pe.wait_ge(bias_dve, h - 1)
                kind = int(h >= A_H)
                for i, (c, m) in enumerate(((0, 512), (512, 512), (1024, GW - 1024))):
                    ins = nc.tensor.matmul(bank[3 * (h % 2) + i][:, 0:m], table_cols[:, h, :], onehot[:, kind, c:c + m],
                                           start=True, stop=True)
                ins.then_inc(bias_made, 1)
            pe.wait_ge(bias_act, HEADS)
            pe.wait_ge(bias_dve, HEADS)
            for n in range(CH * len(GROUPS)):
                g, j = GROUPS[n // CH], n % CH
                if j == 0:
                    pe.wait_ge(w_rest_made, 2 * (n // CH) + 2)
                if n >= 2:
                    pe.wait_ge(act_out, total(act_pieces, n - 2))
                    pe.wait_ge(dve_out, total(dve_pieces, n - 2))
                cols = slice(P * j, P * j + P)
                for k in range(KD):
                    passes = ((w_hi, xT_hi), (w_hi, xT_rest), (w_rest, xT_hi))
                    for x, (wt, xt) in enumerate(passes):
                        for i, (c, m) in enumerate(PIECES):
                            ins = nc.tensor.matmul(bank[3 * (n % 2) + i][:, 0:m], w_tiles(wt, n // CH)[:, k, cols], xt[:, k, c:c + m],
                                                   start=(k == 0 and x == 0), stop=(k == KD - 1 and x == 2))
                ins.then_inc(projected, 1)
            n = len(GROUPS)
            pe.wait_ge(w_rest_made, 2 * n + 2)
            for t in range(TT):
                if t >= 2:
                    pe.wait_ge(v_copied, t - 1)
                for k in range(KD):
                    cols = slice(P * t, P * t + tokens(t))
                    for x, (wt, xt) in enumerate(((w_hi, xT_hi), (w_rest, xT_hi), (w_hi, xT_rest))):
                        ins = nc.tensor.matmul(bank[6 + t % 2][0:tokens(t), :], xt[:, k, cols], w_tiles(wt, n)[:, k, :],
                                               start=(k == 0 and x == 0), stop=(k == KD - 1 and x == 2))
                ins.then_inc(v_made, 1)
            last = CH * len(GROUPS) - 1
            pe.wait_ge(act_out, total(act_pieces, last))
            pe.wait_ge(dve_out, total(dve_pieces, last))
            pe.wait_ge(last_picked, 1)
            for c in range(CH):
                ins = nc.tensor.transpose(bank[5][0:18, P * c:P * c + P], conv_last[:, c, :], ident[:, :])
            ins.then_inc(last_turned, 1)
            for n, (kind, t) in enumerate(K_JOBS):
                if n >= 2:
                    pe.wait_ge(k_copied, n - 1)
                for j in range(CH if kind == "b" else 1):
                    tile = 1 + j if kind == "b" else 0
                    ins = nc.tensor.transpose(bank[n % 2][0:tokens(t), P * j:P * j + P],
                                              KT[:, tile, P * t:P * t + tokens(t)], ident[:, :])
                ins.then_inc(k_turned, 1)


def attend(nc, io, keep):
    mixT, KT, V, ident = keep["mixT"], keep["KT"], keep["V"], keep["ident"]
    HEADS = A_H + B_H
    A_ORDER = (0, 2, 1, 3)
    UNITS = QT_N * HEADS
    PAIRS = NB // 2
    with ExitStack() as stack:
        p = Pools(nc, stack)
        stage = keep["stage"]
        bias_b = stage[:, 0:B_H * SEQ].rearrange("p (h x) -> p h x", h=B_H)
        bias_a = stage[:, B_H * SEQ:B_H * SEQ + A_H * 2 * P].rearrange("p (h x) -> p h x", h=A_H)
        w_out = stage[:, :].rearrange("p (k c) -> p k c", k=KD)
        negs = p.sb("negs", [P, 2, SEQ])
        probs = p.sb("probs", [P, 2, SEQ])
        probsT = p.sb("probsT", [P, 2, KD, P])
        heads_out = p.sb("heads_out", [P, 2, HEADS * DH])
        COLS = UNITS + PAIRS + 2
        neg_max = p.sb("neg_max", [P, COLS])
        denom = p.sb("denom", [P, COLS])
        sink_e = p.sb("sink_e", [P, COLS])
        recip = p.sb("recip", [P, COLS])
        sinks = p.sb("sinks", [P, A_H])
        sink_col = p.sb("sink_col", [A_H, 1])
        sink_pick = p.sb("sink_pick", [A_H, P])
        sink_rows = p.sb("sink_rows", [P, 1])
        bias_sb = p.sb("bias_sb", [P, SK])
        bias_sa = p.sb("bias_sa", [P, AK])
        k_cache = p.sb("k_cache", [P, 2, SKT, BW])
        V_flat = V[:, :, :].rearrange("p t c -> p (t c)")
        v_cache = [p.sb("v_cache", [P, SKT, BW]), V_flat[:, 0:SKT * BW].rearrange("p (t c) -> p t c", t=SKT)]
        va_cache = V_flat[:, SKT * BW:SKT * BW + NB * P].rearrange("p (b c) -> p b c", b=NB)
        kT_s = p.sb("kT_s", [P, 2, CH, SK])
        ka_cache = p.sb("ka_cache", [P, NB, P])
        kaT_s = p.sb("kaT_s", [P, NB, AK])
        v_new = p.sb("v_new", [NT, 4, BW])
        va_new = p.sb("va_new", [NT, NB, P])
        q_blk = p.sb("q_blk", [P, NB, CH, DH])
        qa_blk = p.sb("qa_blk", [P, NB, NT * A_H])
        score = [p.ps(f"score{i}", [P, SEQ]) for i in range(2)]
        turn = [p.ps(f"turn{i}", [P, 512]) for i in range(2)]
        value = [p.ps(f"value{i}", [P, 512]) for i in range(2)]

        w_out_loaded = p.sem("w_out_loaded")
        bias_loaded = [p.sem(f"bias_loaded{i}") for i in range(QT_N)]
        sinks_loaded = p.sem("sinks_loaded")
        sbias_loaded = p.sem("sbias_loaded")
        sbias_copied = p.sem("sbias_copied")
        a_loaded = p.sem("a_loaded")
        va_loaded = p.sem("va_loaded")
        k_loaded = [p.sem(f"k_loaded{i}") for i in range(2)]
        v_loaded = [p.sem(f"v_loaded{i}") for i in range(2)]
        last_v_loaded = [p.sem(f"last_v_loaded{i}") for i in range(2)]
        blanks = p.sem("blanks")
        q_blocked = p.sem("q_blocked")
        new_k = p.sem("new_k")
        scored = p.sem("scored")
        biased = p.sem("biased")
        exped = p.sem("exped")
        act_step = p.sem("act_step2")
        dve_step = p.sem("dve_step2")
        turned = p.sem("turned2")
        act_turned = p.sem("act_turned")
        dve_turned = p.sem("dve_turned")
        valued = p.sem("valued")
        scaled = p.sem("scaled")
        sink_spread = p.sem("sink_spread")
        sink_ready = p.sem("sink_ready")

        def place(u):
            return (4, 0, 5, 1, 6, 2, 7, 3, 8, 9)[u % HEADS]

        def unit(u):
            i, s = u // HEADS, place(u)
            if s < A_H:
                first = max(0, i - 1)
                return i, first, i + 1 - first, True, A_ORDER[s]
            return i, 0, i + 1, False, s - A_H

        groups = []

        def add(what, *rest):
            groups.append((what, *rest))

        for u in range(UNITS + 1):
            if u < UNITS:
                for k in range(0, unit(u)[2], 4):
                    add("probs", u, k, min(4, unit(u)[2] - k))
            if u and u % HEADS == 0:
                add("out", u // HEADS - 1, 0, 4)
                add("out", u // HEADS - 1, 4, 1)
        for x in range(2):
            add("ka", x)
        def add_keys(r):
            for b in (2 * r, 2 * r + 1):
                for k in range(SKT if r < PAIRS else 0):
                    add("ks", b, k)

        add_keys(0)
        for x in range(2):
            add("aprobs", x)
        for r in range(PAIRS):
            add_keys(r + 1)
            add("sprobs", r, 0, 4)
            add("sprobs", r, 4, 3)

        def wait_taken(eng, upto):
            if upto >= 0:
                eng.wait_ge(act_turned, upto // 2 + 1)
            if upto >= 1:
                eng.wait_ge(dve_turned, (upto + 1) // 2)

        def groups_of(*key):
            return [n for n, g in enumerate(groups) if g[:len(key)] == key]

        def take(eng, n):
            g = groups[n]
            src = turn[n % 2]
            eng.wait_ge(turned, n + 1)
            if g[0] == "probs":
                u, k, c = g[1:]
                if u >= 2:
                    eng.wait_ge(valued, u - 1)
                out, src = probsT[:, u % 2, k:k + c, :], src[:, 0:P * c].rearrange("p (k c) -> p k c", c=P)
            elif g[0] == "out":
                i, k, c = g[1:]
                out, src = mixT[:, k:k + c, P * i:P * i + P], src[:, 0:P * c].rearrange("p (k c) -> p k c", c=P)
            elif g[0] == "ka":
                out, src = kaT_s[:, 4 * g[1]:4 * g[1] + 4, 0:P], src[:, :].rearrange("p (b c) -> p b c", c=P)
            elif g[0] == "aprobs":
                eng.wait_ge(valued, UNITS)
                x = g[1]
                eng_copy(eng, n, probsT[:, x, 0, :], src[:, 0:P], False)
                out, src = probsT[0:NT, x, 1, :], src[0:NT, P:2 * P]
            elif g[0] == "ks":
                b, k = g[1:]
                if b >= 2:
                    eng.wait_ge(scored, UNITS + b)
                out, src = kT_s[:, b % 2, :, P * k:P * k + P], src[:, 0:BW].rearrange("p (g c) -> p g c", c=P)
            else:
                r, k, c = g[1:]
                eng.wait_ge(valued, UNITS + 1 + (r - 1 if r >= 1 else 0))
                full = min(c, SKT - k)
                if full < c:
                    eng_copy(eng, n, probsT[0:NT, r % 2, SKT, :], src[0:NT, P * full:P * c], False)
                out, src = probsT[:, r % 2, k:k + full, :], src[:, 0:P * full].rearrange("p (k c) -> p k c", c=P)
            eng_copy(eng, n, out, src, True)

        def eng_copy(eng, n, out, src, last):
            if n % 2 == 0:
                ins = nc.scalar.activation(out, src, ACT.Copy)
            else:
                ins = nc.vector.tensor_copy(out, src)
            if last:
                ins.then_inc(act_turned if n % 2 == 0 else dve_turned, 1)

        def take_all(eng, parity, *key):
            for n in groups_of(*key):
                if n % 2 == parity:
                    take(eng, n)

        def v_place(b):
            if b >= NB - 2:
                return k_cache[:, b % 2, :, :], last_v_loaded[b % 2]
            return v_cache[b % 2], v_loaded[b % 2]

        block = stack.enter_context(nc.Block())

        @block.sync
        def _(sp):
            for i in range(QT_N):
                lo = SEQ - P * (i + 1)
                for h in range(B_H):
                    sp.dma_start(bias_b[:, h, lo:lo + P], io["bias_skewed"][A_H + h][:, lo:lo + P]).then_inc(bias_loaded[i], 16)
                if i < 2:
                    for h in range(A_H):
                        sp.dma_start(bias_a[:, h, P * (1 - i):P * (2 - i)], io["bias_skewed"][h][:, lo:lo + P]).then_inc(bias_loaded[i], 16)
                if i == 0:
                    sp.dma_start(sinks[:, :], io["sinks"].partition_broadcast(P)).then_inc(sinks_loaded, 16)
                    sp.dma_start(sink_col[:, :], io["sinks"].rearrange("(h o) -> h o", o=1)).then_inc(sinks_loaded, 16)
                    sp.dma_start(sink_pick[:, :], io["sink_pick"]).then_inc(sinks_loaded, 16)
            sp.dma_start(ka_cache[:, :, :], io["cache_a_k"]).then_inc(a_loaded, 16)
            sp.dma_start(va_new[:, :, :], io["a_v_new"]).then_inc(a_loaded, 16)
            sp.wait_ge(blanks, 1)
            for t in range(NT):
                sp.dma_start(bias_sb[B_H * t:B_H * t + B_H, 0:FARK],
                             io["bias_row"][A_H:HEADS, NT - 1 - t:NT - 1 - t + SEQ // 2].rearrange("h (a r) -> h a r", r=16)[:, :, 0:NT]).then_inc(sbias_loaded, 16)
                near = NT - 1 - t + SEQ // 2
                sp.dma_start(bias_sb[B_H * t:B_H * t + B_H, FARK:SK],
                             io["bias_row"][A_H:HEADS, near:near + NEARK + NT]).then_inc(sbias_loaded, 16)
                a0 = FAR - A_WIN - t
                sp.dma_start(bias_sa[A_H * t:A_H * t + A_H, :], io["bias_row"][0:A_H, a0:a0 + AK]).then_inc(sbias_loaded, 16)
            sp.wait_ge(sbias_loaded, 16 * 3 * NT)
            sp.dma_start(bias_sb[DH:P, :], bias_sb[0:DH, :]).then_inc(sbias_copied, 16)
            for x in range(1, 4):
                sp.dma_start(bias_sa[32 * x:32 * x + 32, :], bias_sa[0:32, :]).then_inc(sbias_copied, 16)

            def load_k(b):
                if b >= 2:
                    sp.wait_ge(turned, groups_of("ks", b - 2)[-1] + 1)
                for k in range(2):
                    sp.dma_start(k_cache[:, b % 2, k, :], io["cache_b_k_far"][b][k]).then_inc(k_loaded[b % 2], 16)
                sp.dma_start(k_cache[:, b % 2, 2:SKT, :], io["cache_b_k_near"][b]).then_inc(k_loaded[b % 2], 16)

            def load_v(b):
                if b == 1:
                    sp.wait_ge(valued, UNITS)
                    sp.dma_start(va_cache[:, :, :], io["cache_a_v"]).then_inc(va_loaded, 16)
                if 2 <= b < NB - 2:
                    sp.wait_ge(valued, UNITS + 1 + b // 2)
                if b >= NB - 2:
                    sp.wait_ge(turned, groups_of("ks", b)[-1] + 1)
                to, loaded = v_place(b)
                for k in range(2):
                    sp.dma_start(to[:, k, :], io["cache_b_v_far"][b][k]).then_inc(loaded, 16)
                sp.dma_start(to[:, 2:SKT, :], io["cache_b_v_near"][b]).then_inc(loaded, 16)
                sp.dma_start(v_new[:, b % 4, :], io["b_v_new"][b]).then_inc(loaded, 16)

            for b in (0, 1):
                load_k(b)
            for b in (0, 1):
                load_v(b)
            for b in (2, 3):
                load_k(b)
            sp.wait_ge(biased, UNITS)
            for j in range(2):
                for hh in range(2):
                    r0 = DH * (2 * hh + j)
                    sp.dma_start(w_out[DH * hh:DH * hh + DH, j, :], io["w_out"][r0:r0 + DH, :]).then_inc(w_out_loaded, 16)
            sp.dma_start(w_out[:, 2:KD, :], io["w_out"][2 * P:, :].rearrange("(k p) c -> p k c", p=P)).then_inc(w_out_loaded, 16)
            for r in range(1, PAIRS):
                if r + 1 < PAIRS:
                    load_k(2 * r + 2)
                    load_k(2 * r + 3)
                load_v(2 * r)
                load_v(2 * r + 1)
            sp.wait_ge(w_out_loaded, 80)

        @block.gpsimd
        def _(pool):
            nc.gpsimd.memset(bias_sb[:, :], 0.0).then_inc(blanks, 1)
            pool.wait_ge(blanks, 1)
            nc.gpsimd.memset(q_blk[:, :, :, :], 0.0).then_inc(blanks, 1)
            pool.wait_ge(blanks, 2)
            nc.gpsimd.memset(qa_blk[:, :, :], 0.0).then_inc(blanks, 1)
            pool.wait_ge(blanks, 3)
            done = 0
            for h in range(B_H):
                half, g = DH * (h % 2), h // 2
                nc.gpsimd.tensor_copy(q_blk[half:half + DH, :, g, 0:NT * B_H].rearrange("p b (t h) -> p b t h", h=B_H)[:, :, :, h],
                                      mixT[half:half + DH, 2 + g, SEQ:TOK].rearrange("p (b t) -> p b t", b=NB)).then_inc(q_blocked, 1)
                done += 1
                pool.wait_ge(q_blocked, done)
            for h in range(A_H):
                half = DH * (h // 2)
                nc.gpsimd.tensor_copy(qa_blk[half:half + DH, :, :].rearrange("p b (t h) -> p b t h", h=A_H)[:, :, :, h],
                                      mixT[half:half + DH, h % 2, SEQ:TOK].rearrange("p (b t) -> p b t", b=NB)).then_inc(q_blocked, 1)
                done += 1
                pool.wait_ge(q_blocked, done)
            nc.gpsimd.tensor_copy(kaT_s[:, :, P:AK], KT[:, 0, SEQ:TOK].rearrange("p (b t) -> p b t", b=NB)).then_inc(new_k, 1)

        @block.scalar
        def _(act):
            sinks_added = 0

            def exp(u, col, n, rows_sink, sink_bias):
                nonlocal sinks_added
                nc.scalar.activation(probs[:, u % 2, 0:n], negs[:, u % 2, 0:n], ACT.Exp, bias=neg_max[:, col:col + 1],
                                     scale=-1.0, accum_out=denom[:, col:col + 1]).then_inc(exped, 1)
                if rows_sink is not None:
                    nc.scalar.activation(sink_e[:, col:col + 1], rows_sink, ACT.Exp,
                                         bias=neg_max[:, col:col + 1]).then_inc(act_step, 1)

            def exp_unit(u):
                i, first, k, window, h = unit(u)
                act.wait_ge(biased, u + 1)
                if u >= 2:
                    act.wait_ge(turned, groups_of("probs", u - 2)[-1] + 1)
                exp(u, u, P * k, sinks[:, h:h + 1] if window else None, None)

            act.wait_ge(sinks_loaded, 48)
            exp_unit(0)
            for u in range(UNITS):
                if u % HEADS == 1 and u > HEADS:
                    take_all(act, 0, "out", u // HEADS - 1)
                take_all(act, 0, "probs", u)
                if u + 1 < UNITS:
                    exp_unit(u + 1)
            take_all(act, 0, "out", QT_N - 1)
            take_all(act, 0, "ka")
            act.wait_ge(sink_ready, 1)
            act.wait_ge(turned, groups_of("probs", UNITS - 1)[-1] + 1)
            for x in range(2):
                act.wait_ge(biased, UNITS + x + 1)
                exp(x, UNITS + PAIRS + x, AK, sink_rows[:, :], None)
            for b in (0, 1):
                take_all(act, 0, "ks", b)
            take_all(act, 0, "aprobs")
            for r in range(PAIRS):
                take_all(act, 0, "ks", 2 * r + 2)
                act.wait_ge(biased, UNITS + 2 + r + 1)
                if r < 2:
                    act.wait_ge(turned, groups_of("aprobs", r)[-1] + 1)
                else:
                    act.wait_ge(turned, groups_of("sprobs", r - 2)[-1] + 1)
                exp(r, UNITS + r, SK, None, None)
                take_all(act, 0, "ks", 2 * r + 3)
                take_all(act, 0, "sprobs", r)

        @block.vector
        def _(dve):
            step = stepper(dve, dve_step)

            def bias(u):
                i, first, k, window, h = unit(u)
                if u % HEADS == 0:
                    dve.wait_ge(bias_loaded[i], 16 * (HEADS if i < 2 else B_H))
                dve.wait_ge(scored, u + 1)
                if u >= 2:
                    dve.wait_ge(exped, u - 1)
                n = P * k
                table = bias_a[:, h, 2 * P - n:2 * P] if window else bias_b[:, h, SEQ - n:SEQ]
                nc.vector.tensor_tensor_reduce(negs[:, u % 2, 0:n], score[u % 2][:, 0:n], table, -1.0, 0.0 - MASK,
                                               ALU.add, ALU.min, neg_max[:, u:u + 1]).then_inc(biased, 1)

            windows_seen = 0

            def scale(u):
                nonlocal windows_seen
                i, first, k, window, h = unit(u)
                dve.wait_ge(exped, u + 1)
                if window:
                    windows_seen += 1
                    dve.wait_ge(act_step, windows_seen)
                    step(nc.vector.tensor_tensor(denom[:, u:u + 1], denom[:, u:u + 1], sink_e[:, u:u + 1], ALU.add))
                step(nc.vector.reciprocal(recip[:, u:u + 1], denom[:, u:u + 1]))
                if i >= 2 and u % HEADS == 0:
                    dve.wait_ge(turned, groups_of("out", i - 2)[-1] + 1)
                s = place(u)
                dve.wait_ge(valued, u + 1)
                nc.vector.tensor_scalar(heads_out[:, i % 2, DH * s:DH * s + DH], value[u % 2][:, 0:DH],
                                        recip[:, u:u + 1], None, ALU.mult).then_inc(scaled, 1)

            bias(0)
            for u in range(UNITS):
                if u + 1 < UNITS:
                    bias(u + 1)
                if u % HEADS == 1 and u > HEADS:
                    take_all(dve, 1, "out", u // HEADS - 1)
                take_all(dve, 1, "probs", u)
                if u:
                    scale(u - 1)
            scale(UNITS - 1)
            take_all(dve, 1, "out", QT_N - 1)
            take_all(dve, 1, "ka")
            dve.wait_ge(sink_spread, 1)
            nc.vector.tensor_copy(sink_rows[:, :], value[1][:, 0:1]).then_inc(sink_ready, 1)
            dve.wait_ge(sbias_copied, 64)
            dve.wait_ge(exped, UNITS)
            dve.wait_ge(scored, UNITS + 1)
            for x in range(2):
                nc.vector.tensor_tensor_reduce(negs[:, x, 0:AK], score[0][:, AK * x:AK * x + AK], bias_sa[:, :], -1.0, 0.0 - MASK,
                                               ALU.add, ALU.min, neg_max[:, UNITS + PAIRS + x:UNITS + PAIRS + x + 1]).then_inc(biased, 1)

            def take_keys(b):
                if b < NB:
                    if b >= 2:
                        dve.wait_ge(scored, UNITS + b)
                    nc.vector.tensor_copy(kT_s[:, b % 2, :, P * SKT:SK], KT[:, 1:4, SEQ + NT * b:SEQ + NT * b + NT]).then_inc(new_k, 1)
                    take_all(dve, 1, "ks", b)

            take_keys(0)
            for x in range(2):
                col = UNITS + PAIRS + x
                dve.wait_ge(exped, UNITS + x + 1)
                dve.wait_ge(act_step, windows_seen + x + 1)
                step(nc.vector.tensor_tensor(denom[:, col:col + 1], denom[:, col:col + 1], sink_e[:, col:col + 1], ALU.add))
                step(nc.vector.reciprocal(recip[:, col:col + 1], denom[:, col:col + 1]))
                nc.vector.tensor_scalar(probs[:, x, 0:AK], probs[:, x, 0:AK], recip[:, col:col + 1], None, ALU.mult).then_inc(scaled, 1)
            take_keys(1)
            take_all(dve, 1, "aprobs")
            for r in range(PAIRS):
                col = UNITS + r
                dve.wait_ge(scored, UNITS + 1 + 2 * r + 2)
                dve.wait_ge(exped, UNITS + 2 + (r - 1 if r >= 2 else 0))
                nc.vector.tensor_tensor_reduce(negs[:, r % 2, 0:SK], score[(r + 1) % 2][:, 0:SK], bias_sb[:, :], -1.0, 0.0 - MASK,
                                               ALU.add, ALU.min, neg_max[:, col:col + 1]).then_inc(biased, 1)
                take_keys(2 * r + 2)
                dve.wait_ge(exped, UNITS + 2 + r + 1)
                step(nc.vector.reciprocal(recip[:, col:col + 1], denom[:, col:col + 1]))
                nc.vector.tensor_scalar(probs[:, r % 2, 0:SK], probs[:, r % 2, 0:SK], recip[:, col:col + 1], None, ALU.mult).then_inc(scaled, 1)
                take_keys(2 * r + 3)
                take_all(dve, 1, "sprobs", r)
            dve.wait_ge(valued, UNITS + 1 + PAIRS)
            for hh in range(2):
                rows = slice(DH * hh, DH * hh + DH)
                for g in range(CH):
                    nc.vector.tensor_copy(mixT[rows, 2 + g, SEQ:TOK].rearrange("p (b t) -> p b t", b=NB),
                                          value[0][rows, 0:NB * CH * 16].rearrange("p (b g t h) -> p b g t h", b=NB, g=CH, h=2)[:, :, g, :, hh])
                for j in range(2):
                    nc.vector.tensor_copy(mixT[rows, j, SEQ:TOK].rearrange("p (b t) -> p b t", b=NB),
                                          value[1][rows, 0:NB * 32].rearrange("p (b t h) -> p b t h", b=NB, h=A_H)[:, :, :, 2 * hh + j])

        @block.tensor
        def _(pe):
            def bank_for(n):
                wait_taken(pe, n - 2)
                return turn[n % 2]

            def scores(u):
                i, first, k, window, h = unit(u)
                half = DH * (h // 2 if window else h % 2)
                qt = h % 2 if window else 2 + h // 2
                kt = 0 if window else 1 + h // 2
                if u >= 2:
                    pe.wait_ge(biased, u - 1)
                for c in range(0, k, 4):
                    m = P * min(4, k - c)
                    ins = nc.tensor.matmul(score[u % 2][:, P * c:P * c + m], mixT[half:half + DH, qt, P * i:P * i + P],
                                           KT[half:half + DH, kt, P * (first + c):P * (first + c) + m], start=True, stop=True)
                ins.then_inc(scored, 1)

            def turn_probs(u):
                pe.wait_ge(exped, u + 1)
                for n in groups_of("probs", u):
                    _, _, k, c = groups[n]
                    bank = bank_for(n)
                    for x in range(c):
                        ins = nc.tensor.transpose(bank[:, P * x:P * x + P], probs[:, u % 2, P * (k + x):P * (k + x) + P], ident[:, :])
                    ins.then_inc(turned, 1)

            def values(u):
                i, first, k, window, h = unit(u)
                wait_taken(pe, groups_of("probs", u)[-1])
                if u >= 2:
                    pe.wait_ge(scaled, u - 1)
                c0 = DH * (h // 2) if window else P + DH * h
                for x in range(k):
                    ins = nc.tensor.matmul(value[u % 2][:, 0:DH], probsT[:, u % 2, x, :], V[:, first + x, c0:c0 + DH],
                                           start=(x == 0), stop=(x == k - 1))
                ins.then_inc(valued, 1)

            def turn_out(i):
                pe.wait_ge(scaled, HEADS * (i + 1))
                for n in groups_of("out", i):
                    _, _, k, c = groups[n]
                    bank = bank_for(n)
                    for x in range(c):
                        ins = nc.tensor.transpose(bank[:, P * x:P * x + P], heads_out[:, i % 2, P * (k + x):P * (k + x) + P], ident[:, :])
                    ins.then_inc(turned, 1)

            scores(0)
            for u in range(UNITS):
                if u + 1 < UNITS:
                    scores(u + 1)
                turn_probs(u)
                if u:
                    values(u - 1)
                if u and u % HEADS == 0:
                    turn_out(u // HEADS - 1)
            values(UNITS - 1)
            turn_out(QT_N - 1)

            pe.wait_ge(a_loaded, 32)
            for x, n in enumerate(groups_of("ka")):
                bank = bank_for(n)
                for b in range(4):
                    ins = nc.tensor.transpose(bank[:, P * b:P * b + P], ka_cache[:, 4 * x + b, :], ident[:, :])
                ins.then_inc(turned, 1)
            pe.wait_ge(scaled, UNITS)
            pe.wait_ge(sinks_loaded, 48)
            nc.tensor.matmul(value[1][:, 0:1], sink_pick[:, :], sink_col[:, :], start=True, stop=True).then_inc(sink_spread, 1)
            wait_taken(pe, groups_of("ka")[-1])
            pe.wait_ge(q_blocked, HEADS)
            pe.wait_ge(new_k, 1)
            pe.wait_ge(biased, UNITS)
            for b in range(NB):
                at = 32 * (b % 4)
                ins = nc.tensor.matmul(score[0][at:at + 32, AK * (b // 4):AK * (b // 4) + AK], qa_blk[:, b, :], kaT_s[:, b, :],
                                       start=True, stop=True)
            ins.then_inc(scored, 1)

            def keys(r):
                if r == PAIRS:
                    return
                buf = score[(r + 1) % 2]
                if r:
                    pe.wait_ge(biased, UNITS + 2 + r - 1)
                for b in (2 * r, 2 * r + 1):
                    pe.wait_ge(k_loaded[b % 2], 48 * (r + 1))
                    for n in groups_of("ks", b):
                        bank = bank_for(n)
                        for g in range(CH):
                            ins = nc.tensor.transpose(bank[:, P * g:P * g + P], k_cache[:, b % 2, groups[n][2], P * g:P * g + P], ident[:, :])
                        ins.then_inc(turned, 1)
                    wait_taken(pe, groups_of("ks", b)[-1])
                    pe.wait_ge(new_k, 2 + b)
                    at = DH * (b % 2)
                    for c, m in ((0, 512), (512, SK - 512)):
                        for g in range(CH):
                            ins = nc.tensor.matmul(buf[at:at + DH, c:c + m], q_blk[:, b, g, :], kT_s[:, b % 2, g, c:c + m],
                                                   start=(g == 0), stop=(g == CH - 1))
                    ins.then_inc(scored, 1)

            keys(0)
            for x, n in enumerate(groups_of("aprobs")):
                pe.wait_ge(scaled, UNITS + x + 1)
                bank = bank_for(n)
                nc.tensor.transpose(bank[:, 0:P], probs[:, x, 0:P], ident[:, :])
                nc.tensor.transpose(bank[0:NT, P:2 * P], probs[:, x, P:AK], ident[:, :]).then_inc(turned, 1)
            wait_taken(pe, groups_of("aprobs")[-1])
            pe.wait_ge(sink_ready, 1)
            pe.wait_ge(va_loaded, 16)
            for b in range(NB):
                out = value[1][:, 32 * b:32 * b + 32]
                cols = slice(32 * (b % 4), 32 * (b % 4) + 32)
                nc.tensor.matmul(out, va_cache[:, b, :], probsT[:, b // 4, 0, cols], start=True, stop=False)
                ins = nc.tensor.matmul(out, va_new[:, b, :], probsT[0:NT, b // 4, 1, cols], start=False, stop=True)
            ins.then_inc(valued, 1)

            for r in range(PAIRS):
                keys(r + 1)
                pe.wait_ge(scaled, UNITS + 2 + r + 1)
                for n in groups_of("sprobs", r):
                    bank = bank_for(n)
                    _, _, k, c = groups[n]
                    for x in range(k, k + c):
                        m = P if x < SKT else NT
                        ins = nc.tensor.transpose(bank[0:m, P * (x - k):P * (x - k) + P], probs[:, r % 2, P * x:P * x + m], ident[:, :])
                    ins.then_inc(turned, 1)
                wait_taken(pe, groups_of("sprobs", r)[-1])
                for b in (2 * r, 2 * r + 1):
                    v_all, loaded = v_place(b)
                    pe.wait_ge(loaded, 64 if r == PAIRS - 1 else 64 * (r + 1))
                    for g in range(CH):
                        out = value[0][:, 16 * (CH * b + g):16 * (CH * b + g) + 16]
                        at = DH * (b % 2) + 2 * g
                        for x in range(SKT + 1):
                            cached = x < SKT
                            lhs = v_all[:, x, P * g:P * g + P] if cached else v_new[:, b % 4, P * g:P * g + P]
                            rows = probsT[:, r % 2, x, :] if cached else probsT[0:NT, r % 2, SKT, :]
                            rhs = rows[:, DH * (b % 2):DH * (b % 2) + NT * B_H].rearrange("p (t h) -> p t h", h=B_H)[:, :, 2 * g:2 * g + 2]
                            ins = nc.tensor.matmul(out, lhs, rhs, start=(x == 0), stop=not cached)
                ins.then_inc(valued, 1)


def mix_out(nc, io, keep):
    mixT, ident = keep["mixT"], keep["ident"]
    ends, slot_ids, slot_w = keep["ends"], keep["slot_ids"], keep["slot_w"]
    moe = keep["moe"]
    with ExitStack() as stack:
        p = Pools(nc, stack)
        w_out = keep["stage"][:, :].rearrange("p (k c) -> p k c", k=KD)
        norm_g = p.sb("norm_g2", [P, D])
        x1 = p.sb("x1", [P, 3, D])
        hn = p.sb("hn", [P, 2, D])
        hT = p.sb("hT", [P, 2, KD, P])
        squares = p.sb("squares", [P, D])
        stats = p.sb("stats2", [P, TT, 3])
        eps = p.sb("eps2", [P, 1])
        w_route = p.sb("w_route", [P, KD, NG + NE])
        b_route = p.sb("b_route", [P, NG + NE])
        logits = p.sb("logits", [P, TT, NG + NE])
        g_pad = p.sb("g_pad", [P, TT, 8])
        g_top = p.sb("g_top", [P, TT, 8])
        g_index = p.sb("g_index", [P, TT, 8], U32)
        g_index_f = p.sb("g_index_f", [P, TT])
        g_shift = p.sb("g_shift", [P, TT, NG])
        g_exp = p.sb("g_exp", [P, TT, NG])
        g_sum = p.sb("g_sum", [P, TT])
        g_weight = p.sb("g_weight", [P, TT])
        chosen = p.sb("chosen", [P, TT, NG])
        e_in = p.sb("e_in", [P, TT, NE])
        e_top = p.sb("e_top", [P, TT, 8])
        e_index = p.sb("e_index", [P, TT, 8], U32)
        e_index_f = p.sb("e_index_f", [P, TT, 2])
        e_gap = p.sb("e_gap", [P, TT])
        e_exp = p.sb("e_exp", [P, TT])
        e_norm = p.sb("e_norm", [P, TT])
        iota_f = p.sb("iota_f", [P, NE])
        pick = p.sb("pick", [P, 2, TT, NE])
        picks = p.sb("picks", [P, TT, NE], BF16)
        below = p.sb("below", [P, P], BF16)
        ones = p.sb("ones", [P, P], BF16)
        before = p.sb("before", [P, TT + 1, NE])
        place = p.sb("place", [P, TT, NE])
        slot_f = p.sb("slot_f", [P, TT, 2])
        blocks = p.sb("blocks", [P, NE])
        blocks_i = p.sb("blocks_i", [P, NE], I32)
        scan = p.sb("scan", [P, 5, NE])
        ends_f = p.sb("ends_f", [P, NE + 1])
        slot_i = p.sb("slot_i", [P, TT, 2], I32)
        block_f = p.sb("block_f", [P, TT, 2])
        row_f = p.sb("row_f", [P, TT, 2])
        weight = p.sb("weight", [P, TT, 2])
        token_no = p.sb("token_no", [P, TT])
        spare_no = p.sb("spare_no", [P, 1])
        iota_p = p.sb("iota_p", [P, P])
        occupied = p.sb("occupied", [P, MAXB])
        row_pick = keep["stage"][:, D * KD // 2:D * KD // 2 + 2 * TT * P].rearrange("p (t k x) -> p t k x", t=TT, k=2)
        block_pick = keep["stage"][:, D * KD // 2 + 2 * TT * P:D * KD // 2 + 2 * TT * (P + 2 * MAXB)].rearrange("p (t k v x) -> p t k v x", t=TT, k=2, v=2)
        zeros = p.sb("zeros", [P, 128])
        y = [[p.ps(f"y{i}{j}", [P, 512]) for j in range(2)] for i in range(2)]
        turn = [p.ps(f"turn3{i}", [P, 512]) for i in range(2)]
        route = p.ps("route", [P, 512])
        count = p.ps("count", [P, 512])

        r_loaded = p.sem("r_loaded")
        x_loaded = [p.sem(f"x1_loaded{i}") for i in range(3)]
        consts = p.sem("consts3")
        mixed = p.sem("mixed3")
        added = p.sem("added")
        squared = p.sem("squared3")
        rooted = p.sem("rooted3")
        normed = p.sem("normed3")
        x_stored = [p.sem(f"x_stored{i}") for i in range(3)]
        h_stored = [p.sem(f"h_stored{i}") for i in range(2)]
        turned = p.sem("turned3")
        hT_act = p.sem("hT_act")
        hT_dve = p.sem("hT_dve")
        routed = p.sem("routed")
        dve_step = p.sem("dve_step3")
        shifted = p.sem("shifted")
        g_exped = p.sem("g_exped")
        gapped = p.sem("gapped")
        e_exped = p.sem("e_exped")
        picked = p.sem("picked")
        counted = p.sem("counted")
        slotted = p.sem("slotted")
        slots_summed = p.sem("slots_summed")
        spare_stored = p.sem("spare_stored")

        SPLIT_FROM = 5

        block = stack.enter_context(nc.Block())

        @block.sync
        def _(sp):
            for t in range(3):
                sp.dma_start(x1[:, t, :], io["x"][t]).then_inc(x_loaded[t], 16)
            sp.dma_start(norm_g[:, :], io["norm_ffn"].partition_broadcast(P)).then_inc(r_loaded, 16)
            sp.dma_start(w_route[:, :, 0:NG], io["w_group"]).then_inc(r_loaded, 16)
            sp.dma_start(w_route[:, :, NG:], io["w_router"]).then_inc(r_loaded, 16)
            sp.dma_start(b_route[:, 0:NG], io["b_group"].partition_broadcast(P)).then_inc(r_loaded, 16)
            sp.dma_start(b_route[:, NG:], io["b_router"].partition_broadcast(P)).then_inc(r_loaded, 16)
            for which in moe.names:
                moe.load(sp, which, 0, 0)
            sp.wait_ge(consts, 9)
            sp.dma_start(io["x1"][TOK:, :].rearrange("p (k f) -> p k f", f=P), zeros[:, :].unsqueeze(1).to_broadcast([P, KD, P])).then_inc(spare_stored, 16)
            sp.dma_start(io["h"][TOK:, :].rearrange("p (k f) -> p k f", f=P), zeros[:, :].unsqueeze(1).to_broadcast([P, KD, P])).then_inc(spare_stored, 16)
            for t in range(TT):
                n = tokens(t)
                sp.wait_ge(added, t + 1)
                sp.dma_start(io["x1"][P * t:P * t + n, :], x1[0:n, t % 3, :]).then_inc(x_stored[t % 3], 16)
                sp.wait_ge(normed, t + 1)
                sp.dma_start(io["h"][P * t:P * t + n, :], hn[0:n, t % 2, :]).then_inc(h_stored[t % 2], 16)
                if t + 3 < TT:
                    sp.wait_ge(x_stored[t % 3], 16 * (t // 3 + 1))
                    sp.dma_start(x1[0:tokens(t + 3), t % 3, :], io["x"][t + 3]).then_inc(x_loaded[t % 3], 16)
            sp.wait_ge(mixed, TT)
            for which in moe.names:
                moe.load(sp, which, 1, 1)
            for s in range(3):
                sp.wait_ge(x_stored[s], 16 * (TT // 3))
            sp.wait_ge(h_stored[0], 16 * 5)
            sp.wait_ge(h_stored[1], 16 * 4)
            sp.wait_ge(spare_stored, 32)

        @block.gpsimd
        def _(pool):
            exact = {"allow_small_or_imprecise_dtypes": True}
            nc.gpsimd.memset(eps[:, :], EPS).then_inc(consts, 1)
            pool.wait_ge(consts, 1)
            nc.gpsimd.iota(spare_no[:, :], pattern=[[0, 1]], base=TOK + 1, channel_multiplier=1, **exact).then_inc(consts, 1)
            pool.wait_ge(consts, 2)
            nc.gpsimd.iota(token_no[:, :], pattern=[[P, TT]], base=1, channel_multiplier=1, **exact).then_inc(consts, 1)
            pool.wait_ge(consts, 3)
            nc.gpsimd.memset(token_no[NB * NT:P, QT_N:TT], 0.0).then_inc(consts, 1)
            pool.wait_ge(consts, 4)
            nc.gpsimd.iota(iota_f[:, :], pattern=[[1, NE]], base=0, channel_multiplier=0, **exact).then_inc(consts, 1)
            pool.wait_ge(consts, 5)
            nc.gpsimd.iota(iota_p[:, :], pattern=[[1, P]], base=0, channel_multiplier=0, **exact).then_inc(consts, 1)
            pool.wait_ge(consts, 6)
            nc.gpsimd.memset(ones[:, :], 1.0).then_inc(consts, 1)
            pool.wait_ge(consts, 7)
            nc.gpsimd.affine_select(out=below[:, :], in_=ones[:, :], compare_op=ALU.is_gt, fill=0.0, base=0,
                                    pattern=[[1, P]], channel_multiplier=-1).then_inc(consts, 1)
            pool.wait_ge(consts, 8)
            nc.gpsimd.memset(zeros[:, :], 0.0).then_inc(consts, 1)

        @block.scalar
        def _(act):
            act.wait_ge(consts, 1)
            for t in range(TT):
                n = tokens(t)
                act.wait_ge(added, t + 1)
                if t:
                    act.wait_ge(squared, t)
                nc.scalar.activation(squares[0:n, :], x1[0:n, t % 3, :], ACT.Square, accum_out=stats[0:n, t, 0:1]).then_inc(squared, 1)
                act.wait_ge(squared, t + 1)
                nc.scalar.activation(stats[0:n, t, 1:2], stats[0:n, t, 0:1], ACT.Sqrt, bias=eps[0:n, :], scale=1.0 / D).then_inc(rooted, 1)
                act.wait_ge(turned, 2 * t + 1)
                if t >= 2:
                    act.wait_ge(routed, t - 1)
                nc.scalar.activation(hT[:, t % 2, 0:4, 0:n], turn[0][:, :].rearrange("p (k c) -> p k c", k=4)[:, :, 0:n], ACT.Copy).then_inc(hT_act, 1)
                if t >= SPLIT_FROM:
                    moe.split_hi(act, *moe.steps[t - SPLIT_FROM][:1], 0, 0, moe.steps[t - SPLIT_FROM][1])
            act.wait_ge(shifted, 1)
            nc.scalar.activation(g_exp[:, :, :], g_shift[:, :, :], ACT.Exp).then_inc(g_exped, 1)
            act.wait_ge(gapped, 1)
            nc.scalar.activation(e_exp[:, :], e_gap[:, :], ACT.Exp).then_inc(e_exped, 1)

        @block.vector
        def _(dve):
            step = stepper(dve, dve_step)
            step(nc.vector.memset(logits[:, :, :], 0.0))
            step(nc.vector.memset(g_pad[:, :, :], MASK))
            dve.wait_ge(r_loaded, 80)

            def after_route(t):
                n = tokens(t)
                dve.wait_ge(routed, t + 1)
                step(nc.vector.tensor_tensor(logits[0:n, t, :], route[0:n, 32 * t:32 * t + NG + NE], b_route[0:n, :], ALU.add))

            for t in range(TT):
                n = tokens(t)
                dve.wait_ge(x_loaded[t % 3], 16 * (t // 3 + 1))
                dve.wait_ge(mixed, t + 1)
                for j in range(2):
                    xs = x1[0:n, t % 3, 512 * j:512 * j + 512]
                    ins = nc.vector.tensor_tensor(xs, y[t % 2][j][0:n, :], xs, ALU.add)
                ins.then_inc(added, 1)
                dve.wait_ge(rooted, t + 1)
                step(nc.vector.reciprocal(stats[0:n, t, 2:3], stats[0:n, t, 1:2]))
                if t >= 2:
                    dve.wait_ge(h_stored[t % 2], 16 * (t // 2))
                    dve.wait_ge(turned, 2 * t - 2)
                nc.vector.scalar_tensor_tensor(out=hn[0:n, t % 2, :], in0=x1[0:n, t % 3, :], scalar=stats[0:n, t, 2:3],
                                               in1=norm_g[0:n, :], op0=ALU.mult, op1=ALU.mult).then_inc(normed, 1)
                if t:
                    after_route(t - 1)
                dve.wait_ge(turned, 2 * t + 2)
                if t >= 2:
                    dve.wait_ge(routed, t - 1)
                nc.vector.tensor_copy(hT[:, t % 2, 4:8, 0:n], turn[1][:, :].rearrange("p (k c) -> p k c", k=4)[:, :, 0:n]).then_inc(hT_dve, 1)
                if t >= SPLIT_FROM:
                    moe.split_rest(dve, *moe.steps[t - SPLIT_FROM][:1], 0, 0, moe.steps[t - SPLIT_FROM][1])
            after_route(TT - 1)

            step(nc.vector.tensor_copy(g_pad[:, :, 0:NG], logits[:, :, 0:NG]))
            for t in range(TT):
                ins = nc.vector.max(g_top[:, t, :], g_pad[:, t, :])
            step(ins)
            for t in range(TT):
                ins = nc.vector.max_index(g_index[:, t, :], g_top[:, t, :], g_pad[:, t, :])
            step(ins)
            nc.vector.tensor_tensor(g_shift[:, :, :], logits[:, :, 0:NG], g_top[:, :, 0:1].to_broadcast([P, TT, NG]), ALU.subtract).then_inc(shifted, 1)
            step(nc.vector.tensor_copy(g_index_f[:, :], g_index[:, :, 0]))
            dve.wait_ge(consts, 8)
            step(nc.vector.tensor_tensor(chosen[:, :, :], iota_f[:, 0:NG].unsqueeze(1).to_broadcast([P, TT, NG]),
                                         g_index_f[:, :].unsqueeze(2).to_broadcast([P, TT, NG]), ALU.is_equal))
            step(nc.vector.tensor_scalar(chosen[:, :, :], chosen[:, :, :], -1.0, -MASK, ALU.add, ALU.mult))
            for g in range(NG):
                ins = nc.vector.tensor_tensor(e_in[:, :, EPG * g:EPG * g + EPG], logits[:, :, NG + EPG * g:NG + EPG * g + EPG],
                                              chosen[:, :, g:g + 1].to_broadcast([P, TT, EPG]), ALU.add)
            step(ins)
            for t in range(TT):
                ins = nc.vector.max(e_top[:, t, :], e_in[:, t, :])
            step(ins)
            for t in range(TT):
                ins = nc.vector.max_index(e_index[:, t, :], e_top[:, t, :], e_in[:, t, :])
            nc.vector.tensor_tensor(e_gap[:, :], e_top[:, :, 1], e_top[:, :, 0], ALU.subtract).then_inc(gapped, 1)
            step(ins)
            step(nc.vector.tensor_copy(e_index_f[:, :, :], e_index[:, :, 0:2]))
            for k in range(2):
                ins = nc.vector.tensor_tensor(pick[:, k, :, :], iota_f[:, :].unsqueeze(1).to_broadcast([P, TT, NE]),
                                              e_index_f[:, :, k:k + 1].to_broadcast([P, TT, NE]), ALU.is_equal)
            step(ins)
            step(nc.vector.memset(pick[NB * NT:P, :, QT_N, :], 0.0))
            nc.vector.tensor_tensor(picks[:, :, :], pick[:, 0, :, :], pick[:, 1, :, :], ALU.add).then_inc(picked, 1)
            dve.wait_ge(g_exped, 1)
            step(nc.vector.tensor_reduce(g_sum[:, :], g_exp[:, :, :], AX.X, ALU.add))
            step(nc.vector.reciprocal(g_weight[:, :], g_sum[:, :]))
            dve.wait_ge(e_exped, 1)
            step(nc.vector.tensor_scalar(e_norm[:, :], e_exp[:, :], 1.0, None, ALU.add))
            step(nc.vector.reciprocal(e_norm[:, :], e_norm[:, :]))
            step(nc.vector.tensor_tensor(weight[:, :, 0], e_norm[:, :], g_weight[:, :], ALU.mult))
            step(nc.vector.tensor_tensor(weight[:, :, 1], weight[:, :, 0], e_exp[:, :], ALU.mult))
            step(nc.vector.memset(weight[NB * NT:P, QT_N, :], 0.0))
            dve.wait_ge(counted, 1)
            total = count[:, 256:256 + TT * NE].rearrange("p (t e) -> p t e", e=NE)
            step(nc.vector.memset(before[:, 0, :], 0.0))
            for t in range(TT):
                step(nc.vector.tensor_tensor(before[:, t + 1, :], total[:, t, :], before[:, t, :], ALU.add))
            step(nc.vector.tensor_scalar(blocks[:, :], before[:, TT, :], float(P - 1), None, ALU.add))
            step(nc.vector.tensor_copy(blocks_i[:, :], blocks[:, :]))
            step(nc.vector.tensor_scalar(blocks_i[:, :], blocks_i[:, :], 7, None, ALU.arith_shift_right))
            step(nc.vector.tensor_copy(blocks[:, :], blocks_i[:, :]))
            step(nc.vector.tensor_scalar(scan[:, 0, :], blocks[:, :], 1.0, None, ALU.max))
            for i in range(4):
                d = 1 << i
                nc.vector.tensor_copy(scan[:, i + 1, 0:d], scan[:, i, 0:d])
                step(nc.vector.tensor_tensor(scan[:, i + 1, d:NE], scan[:, i, d:NE], scan[:, i, 0:NE - d], ALU.add))
            step(nc.vector.memset(ends_f[:, 0:1], 0.0))
            step(nc.vector.tensor_copy(ends_f[:, 1:NE + 1], scan[:, 4, :]))
            step(nc.vector.tensor_copy(ends[:, :], ends_f[:, :]))
            step(nc.vector.tensor_scalar(blocks[:, :], ends_f[:, 0:NE], float(P), None, ALU.mult))
            step(nc.vector.tensor_tensor(place[:, :, :], count[:, 0:TT * NE].rearrange("p (t e) -> p t e", e=NE),
                                         before[:, 0:TT, :], ALU.add))
            step(nc.vector.tensor_tensor(place[:, :, :], place[:, :, :], blocks[:, :].unsqueeze(1).to_broadcast([P, TT, NE]), ALU.add))
            for k in range(2):
                step(nc.vector.tensor_tensor(pick[:, k, :, :], pick[:, k, :, :], place[:, :, :], ALU.mult))
                step(nc.vector.tensor_reduce(slot_f[:, :, k], pick[:, k, :, :], AX.X, ALU.add))
            step(nc.vector.tensor_copy(slot_i[:, :, :], slot_f[:, :, :]))
            step(nc.vector.tensor_scalar(slot_i[:, :, :], slot_i[:, :, :], 7, None, ALU.arith_shift_right))
            step(nc.vector.tensor_copy(block_f[:, :, :], slot_i[:, :, :]))
            step(nc.vector.scalar_tensor_tensor(out=row_f[:, :, :], in0=block_f[:, :, :], scalar=-float(P), in1=slot_f[:, :, :],
                                                op0=ALU.mult, op1=ALU.add))
            all_slots = [P, TT, 2, MAXB]
            step(nc.vector.tensor_tensor(block_pick[:, :, :, 0, :], iota_p[:, 0:MAXB].unsqueeze(1).unsqueeze(1).to_broadcast(all_slots),
                                         block_f[:, :, :].unsqueeze(3).to_broadcast(all_slots), ALU.is_equal))
            step(nc.vector.tensor_tensor(block_pick[:, :, :, 1, :], block_pick[:, :, :, 0, :],
                                         weight[:, :, :].unsqueeze(3).to_broadcast(all_slots), ALU.mult))
            step(nc.vector.tensor_tensor(block_pick[:, :, :, 0, :], block_pick[:, :, :, 0, :],
                                         token_no[:, :].unsqueeze(2).unsqueeze(2).to_broadcast(all_slots), ALU.mult))
            for t in range(0, TT, 3):
                part = [P, 3, 2, P]
                nc.vector.tensor_tensor(row_pick[:, t:t + 3, :, :], iota_p[:, :].unsqueeze(1).unsqueeze(1).to_broadcast(part),
                                        row_f[:, t:t + 3, :].unsqueeze(3).to_broadcast(part), ALU.is_equal).then_inc(slotted, 1)
            dve.wait_ge(slots_summed, 1)
            numbers = y[0][0][:, 0:MAXB]
            step(nc.vector.tensor_copy(slot_w[:, :], y[0][0][:, MAXB:2 * MAXB]))
            step(nc.vector.tensor_scalar(occupied[:, :], numbers, 1.0, None, ALU.min))
            step(nc.vector.tensor_scalar(occupied[:, :], occupied[:, :], -1.0, 1.0, ALU.mult, ALU.add))
            step(nc.vector.scalar_tensor_tensor(out=occupied[:, :], in0=occupied[:, :], scalar=spare_no[:, 0:1], in1=numbers,
                                                op0=ALU.mult, op1=ALU.add))
            step(nc.vector.memset(slot_ids[:, MAXB:], 0))
            step(nc.vector.tensor_scalar(slot_ids[:, 0:MAXB], occupied[:, :], -1.0, None, ALU.add))

        @block.tensor
        def _(pe):
            def mix(t):
                n = tokens(t)
                if t >= 2:
                    pe.wait_ge(added, t - 1)
                for k in range(KD):
                    for j in range(2):
                        ins = nc.tensor.matmul(y[t % 2][j][0:n, :], mixT[:, k, P * t:P * t + n], w_out[:, k, 512 * j:512 * j + 512],
                                               start=(k == 0), stop=(k == KD - 1))
                ins.then_inc(mixed, 1)

            def turn_h(t):
                n = tokens(t)
                pe.wait_ge(normed, t + 1)
                if t:
                    pe.wait_ge(hT_act, t)
                    pe.wait_ge(hT_dve, t)
                for k in range(KD):
                    ins = nc.tensor.transpose(turn[k // 4][:, P * (k % 4):P * (k % 4) + n], hn[0:n, t % 2, P * k:P * k + P], ident[0:n, 0:n])
                    if k == 3:
                        ins.then_inc(turned, 1)
                ins.then_inc(turned, 1)

            def router(t):
                n = tokens(t)
                pe.wait_ge(hT_act, t + 1)
                pe.wait_ge(hT_dve, t + 1)
                if t:
                    pe.wait_ge(dve_step, 3 + 2 * t)
                for k in range(KD):
                    ins = nc.tensor.matmul(route[0:n, 32 * t:32 * t + NG + NE], hT[:, t % 2, k, 0:n], w_route[:, k, :],
                                           start=(k == 0), stop=(k == KD - 1))
                ins.then_inc(routed, 1)

            mix(0)
            mix(1)
            pe.wait_ge(r_loaded, 80)
            for t in range(TT):
                turn_h(t)
                if t + 2 < TT:
                    mix(t + 2)
                router(t)
            pe.wait_ge(consts, 8)
            pe.wait_ge(picked, 1)
            flat = picks[:, :, :].rearrange("p t e -> p (t e)")
            nc.tensor.matmul(count[:, 0:TT * NE], below[:, :], flat, start=True, stop=True)
            nc.tensor.matmul(count[:, 256:256 + TT * NE], ones[:, :], flat, start=True, stop=True).then_inc(counted, 1)
            for t in range(TT):
                if t % 3 == 0:
                    pe.wait_ge(slotted, t // 3 + 1)
                for k in range(2):
                    ins = nc.tensor.matmul(y[0][0][:, 0:2 * MAXB], row_pick[:, t, k, :], block_pick[:, t, k, :, :].rearrange("p v x -> p (v x)"),
                                           start=(t == 0 and k == 0), stop=(t == TT - 1 and k == 1))
            ins.then_inc(slots_summed, 1)


class ExpertWeights:

    names = ("gate", "up", "down")
    steps = [(which, c) for which in names for c in range(2)]

    def __init__(self, nc, io, p):
        self.nc, self.io = nc, io
        tiles = {"gate": KD, "up": KD, "down": FT}
        self.shape = {n: [P, tiles[n], KD * FF // tiles[n]] for n in self.names}
        self.half_tiles = {n: tiles[n] // 2 for n in self.names}
        self.raw, self.rest, self.hi = ({n: [None, None] for n in self.names} for _ in range(3))
        self.loaded = {n: [p.sem(f"{n}_loaded{i}") for i in range(2)] for n in self.names}
        self.hi_made, self.rest_made = p.sem("weights_hi"), p.sem("weights_rest")

    def place(self, p, half):
        with ExitStack() as freed:
            for n in self.names:
                self.raw[n][half] = Pools(self.nc, freed).sb(f"w_{n}{half}", self.shape[n])
        for n in self.names:
            self.rest[n][half] = p.sb(f"{n}_rest{half}", self.shape[n], F32R)

    def place_hi(self, p, which, half):
        self.hi[which][half] = p.sb(f"{which}_hi{half}", self.shape[which], F32R)

    def load(self, sp, which, e, half):
        src = self.io["w_" + which]
        src = src[e:e + 1] if type(e) is int else src[bass.ds(e, 1)]
        sp.dma_start(self.raw[which][half][:, :, :], src.rearrange("o (k p) f -> p (o k) f", p=P)).then_inc(self.loaded[which][half], 16)

    def rows(self, which, c):
        return slice(self.half_tiles[which] * c, self.half_tiles[which] * (c + 1))

    def split_hi(self, act, which, pair, half, c):
        if c == 0:
            act.wait_ge(self.loaded[which][half], 16 * pair + 16)
        k = self.rows(which, c)
        self.nc.scalar.activation(self.hi[which][half][:, k, :], self.raw[which][half][:, k, :], ACT.Copy).then_inc(self.hi_made, 1)

    def split_rest(self, dve, which, pair, half, c):
        dve.wait_ge(self.hi_made, 12 * pair + 6 * half + self.steps.index((which, c)) + 1)
        k = self.rows(which, c)
        self.nc.vector.tensor_tensor(self.rest[which][half][:, k, :], self.raw[which][half][:, k, :],
                                     self.hi[which][half][:, k, :].bitcast(F32), ALU.subtract).then_inc(self.rest_made, 1)


def experts(nc, io, keep):
    ident, ends, slot_ids, slot_w = keep["ident"], keep["ends"], keep["slot_ids"], keep["slot_w"]
    moe = keep["moe"]
    FIRST = 0
    with ExitStack() as stack:
        p = Pools(nc, stack)
        landing = p.sb("landing", [P, D])
        rows = p.sb("rows", [P, D])
        row_id = p.sb("row_id", [P, 1], I32)
        out_id = p.sb("out_id", [P, 1], I32)
        rowsT_hi = p.sb("rowsT_hi", [P, KD, P], F32R)
        rowsT_lo = p.sb("rowsT_lo", [P, KD, P], F32R)
        moe.place_hi(p, "down", 0)
        moe.hi["down"][1] = moe.hi["down"][0]
        moe.place_hi(p, "up", 1)
        silu = keep["silu"]
        hid = p.sb("hid", [P, FF])
        hidT_hi = p.sb("hidT_hi", [P, FT, P], F32R)
        hidT_lo = p.sb("hidT_lo", [P, FT, P], F32R)
        y_out = p.sb("y_out", [P, D])
        turn = [p.ps(f"turn5{i}", [P, 512]) for i in range(2)]
        gate = p.ps("gate", [P, FF])
        up = p.ps("up", [P, FF])
        hturn = p.ps("hturn", [P, 512])
        y = [p.ps(f"y5{i}", [P, 512]) for i in range(2)]

        rows_ready = p.sem("rows_ready")
        gathered = p.sem("gathered")
        gather_id = p.sem("gather_id")
        id_copied = p.sem("id_copied")
        turned = p.sem("turned5")
        rowsT_hi_made = p.sem("rowsT_hi_made")
        rowsT_lo_made = p.sem("rowsT_lo_made")
        gated = p.sem("gated")
        silued = p.sem("silued")
        upped = p.sem("upped")
        hid_ready = p.sem("hid_ready")
        hid_turned = p.sem("hid_turned")
        hidT_hi_made = p.sem("hidT_hi_made")
        hidT_lo_made = p.sem("hidT_lo_made")
        downed = p.sem("downed")
        y_act = p.sem("y_act")
        y_dve = p.sem("y_dve")
        y_stored = p.sem("y_stored")
        gather_begun = p.sem("gather_begun")
        add_begun = p.sem("add_begun")
        expert_begun = p.sem("expert_begun")

        def expert_loops(eng, block_step):
            def one(pair, half, last):
                e = 2 * pair + half if pair is not FIRST or half else FIRST
                here = (pair, half)
                following = None if last else ((pair, 1) if half == 0 else (pair + 1, 0))
                first = eng.value_load(ends[0:1, bass.ds(e, 1)], min_val=0, max_val=MAXB - 1)
                after = eng.value_load(ends[0:1, bass.ds(e + 1, 1)], min_val=1, max_val=MAXB)
                block_step(FIRST if e is FIRST else first, here, following)
                with eng.If(first + 1 < after):
                    with eng.Fori(first + 1, after) as b:
                        block_step(b)

            one(0, 0, False)
            one(0, 1, False)
            with eng.Fori(1, NE // 2 - 1) as pair:
                one(pair, 0, False)
                one(pair, 1, False)
            one(NE // 2 - 1, 0, False)
            one(NE // 2 - 1, 1, True)

        block = stack.enter_context(nc.Block())

        @block.sync
        def _(sp):
            with sp.Fori(1, NE // 2) as pair:
                for half in range(2):
                    end = sp.value_load(ends[0:1, bass.ds(2 * pair + half - 1, 1)], min_val=1, max_val=MAXB)
                    sp.wait_ge(gated, end)
                    moe.load(sp, "gate", 2 * pair + half, half)
                    sp.wait_ge(upped, end)
                    moe.load(sp, "up", 2 * pair + half, half)
                    sp.wait_ge(downed, end)
                    moe.load(sp, "down", 2 * pair + half, half)

        @block.gpsimd
        def _(pool):
            def gather(b):
                if b is not FIRST:
                    pool.wait_ge(rows_ready, b)
                nc.gpsimd.tensor_copy(row_id[:, :], slot_ids[:, bass.ds(b, 1)]).then_inc(gather_id, 1)
                pool.wait_ge(gather_id, b + 1)
                nc.gpsimd.sem_inc(gather_begun, 1)
                nc.gpsimd.indirect_dma_start(out=landing[:, :], out_offset=None, in_=io["h"],
                                             in_offset=bass.IndirectOffsetOnAxis(ap=row_id[:, :], axis=0)).then_inc(gathered, 16)

            gather(FIRST)
            gather(1)
            gather(2)
            total = pool.value_load(ends[0:1, NE:NE + 1], min_val=NE, max_val=MAXB)

            def block_step(b):
                if b is not FIRST:
                    pool.wait_ge(y_stored, 16 * b)
                nc.gpsimd.tensor_copy(out_id[:, :], slot_ids[:, bass.ds(b, 1)]).then_inc(id_copied, 1)
                pool.wait_ge(id_copied, b + 1)
                pool.wait_ge(y_act, b + 1)
                pool.wait_ge(y_dve, b + 1)
                nc.gpsimd.sem_inc(add_begun, 1)
                nc.gpsimd.indirect_dma_start(out=io["x1"], out_offset=bass.IndirectOffsetOnAxis(ap=out_id[:, :], axis=0),
                                             in_=y_out[:, :], in_offset=None, compute_op=ALU.add).then_inc(y_stored, 16)
                gather(b + 3)

            block_step(FIRST)
            with pool.Fori(1, total) as b:
                block_step(b)
            pool.wait_ge(y_stored, 16 * total)
            pool.wait_ge(gathered, 16 * total + 48)

        @block.scalar
        def _(act):
            def rows_hi(b, c):
                act.wait_ge(turned, 2 * b + c + 1)
                nc.scalar.activation(rowsT_hi[:, 4 * c:4 * c + 4, :], turn[c][:, :].rearrange("p (k c) -> p k c", k=4), ACT.Copy).then_inc(rowsT_hi_made, 1)

            def block_step(b, here=None, following=None):
                if here:
                    if b is not FIRST:
                        act.wait_ge(downed, b)
                    moe.split_hi(act, "down", *here, 0)
                    moe.split_hi(act, "down", *here, 1)
                if following:
                    moe.split_hi(act, "gate", *following, 0)
                act.wait_ge(gated, b + 1)
                nc.scalar.activation(silu[:, :], gate[:, :], ACT.Silu).then_inc(silued, 1)
                if following:
                    moe.split_hi(act, "gate", *following, 1)
                    moe.split_hi(act, "up", *following, 0)
                rows_hi(b + 1, 0)
                act.wait_ge(hid_turned, b + 1)
                nc.scalar.activation(hidT_hi[:, :, :], hturn[:, :].rearrange("p (k c) -> p k c", k=FT), ACT.Copy).then_inc(hidT_hi_made, 1)
                rows_hi(b + 1, 1)
                if following:
                    moe.split_hi(act, "up", *following, 1)
                act.wait_ge(downed, b + 1)
                if b is not FIRST:
                    act.wait_ge(y_stored, 16 * b)
                nc.scalar.activation(y_out[:, 0:512], y[0][:, :], ACT.Copy, scale=slot_w[:, bass.ds(b, 1)]).then_inc(y_act, 1)

            rows_hi(FIRST, 0)
            rows_hi(FIRST, 1)
            expert_loops(act, block_step)

        @block.vector
        def _(dve):
            def fetch(b):
                if b is not FIRST:
                    dve.wait_ge(turned, 2 * b)
                dve.wait_ge(gathered, 16 * b + 16)
                nc.vector.tensor_copy(rows[:, :], landing[:, :]).then_inc(rows_ready, 1)

            def rows_lo(b, c):
                dve.wait_ge(rowsT_hi_made, 2 * b + c + 1)
                hi = rowsT_hi[:, 4 * c:4 * c + 4, :]
                nc.vector.tensor_tensor(rowsT_lo[:, 4 * c:4 * c + 4, :], turn[c][:, :].rearrange("p (k c) -> p k c", k=4),
                                        hi.bitcast(F32), ALU.subtract).then_inc(rowsT_lo_made, 1)

            def block_step(b, here=None, following=None):
                if here:
                    moe.split_rest(dve, "down", *here, 0)
                    moe.split_rest(dve, "down", *here, 1)
                if following:
                    moe.split_rest(dve, "gate", *following, 0)
                dve.wait_ge(silued, b + 1)
                dve.wait_ge(upped, b + 1)
                nc.vector.tensor_tensor(hid[:, :], up[:, :], silu[:, :], ALU.mult).then_inc(hid_ready, 1)
                rows_lo(b + 1, 0)
                dve.wait_ge(hidT_hi_made, b + 1)
                nc.vector.tensor_tensor(hidT_lo[:, :, :], hturn[:, :].rearrange("p (k c) -> p k c", k=FT),
                                        hidT_hi[:, :, :].bitcast(F32), ALU.subtract).then_inc(hidT_lo_made, 1)
                rows_lo(b + 1, 1)
                if following:
                    moe.split_rest(dve, "gate", *following, 1)
                    moe.split_rest(dve, "up", *following, 0)
                    moe.split_rest(dve, "up", *following, 1)
                dve.wait_ge(downed, b + 1)
                if b is not FIRST:
                    dve.wait_ge(y_stored, 16 * b)
                nc.vector.tensor_scalar(y_out[:, 512:D], y[1][:, :], slot_w[:, bass.ds(b, 1)], None, ALU.mult).then_inc(y_dve, 1)
                fetch(b + 2)

            fetch(FIRST)
            rows_lo(FIRST, 0)
            rows_lo(FIRST, 1)
            fetch(1)
            expert_loops(dve, block_step)

        @block.tensor
        def _(pe):
            def turn_rows(c):
                for k in range(4):
                    ins = nc.tensor.transpose(turn[c][:, P * k:P * k + P], rows[:, P * (4 * c + k):P * (4 * c + k + 1)], ident[:, :])
                ins.then_inc(turned, 1)

            def project(out, b, hi, rest, made):
                pe.wait_ge(rowsT_hi_made, 2 * b + 2)
                pe.wait_ge(moe.rest_made, made)
                for k in range(KD):
                    nc.tensor.matmul(out[:, :], rowsT_hi[:, k, :], hi[:, k, :], start=(k == 0), stop=False)
                    nc.tensor.matmul(out[:, :], rowsT_hi[:, k, :], rest[:, k, :], start=False, stop=False)
                pe.wait_ge(rowsT_lo_made, 2 * b + 2)
                for k in range(KD):
                    ins = nc.tensor.matmul(out[:, :], rowsT_lo[:, k, :], hi[:, k, :], start=False, stop=(k == KD - 1))
                return ins

            pe.wait_ge(rows_ready, 1)
            turn_rows(0)
            turn_rows(1)
            with pe.Fori(0, NE // 2) as pair:
                for half in range(2):
                    first = pe.value_load(ends[0:1, bass.ds(2 * pair + half, 1)], min_val=0, max_val=MAXB - 1)
                    after = pe.value_load(ends[0:1, bass.ds(2 * pair + half + 1, 1)], min_val=1, max_val=MAXB)
                    done = 12 * pair + 6 * half
                    pe.wait_ge(moe.rest_made, done + 2)
                    nc.tensor.sem_inc(expert_begun, 1)
                    with pe.Fori(first, after) as b:
                        project(gate, b, moe.hi["gate"][half], moe.rest["gate"][half], done + 2).then_inc(gated, 1)
                        project(up, b, moe.hi["up"][half], moe.rest["up"][half], done + 4).then_inc(upped, 1)
                        pe.wait_ge(rows_ready, b + 2)
                        turn_rows(0)
                        pe.wait_ge(hid_ready, b + 1)
                        for k in range(FT):
                            ins = nc.tensor.transpose(hturn[:, P * k:P * k + P], hid[:, P * k:P * k + P], ident[:, :])
                        ins.then_inc(hid_turned, 1)
                        turn_rows(1)
                        pe.wait_ge(hidT_hi_made, b + 1)
                        pe.wait_ge(moe.rest_made, done + 6)
                        for k in range(FT):
                            for j in range(2):
                                cols = slice(512 * j, 512 * j + 512)
                                nc.tensor.matmul(y[j][:, :], hidT_hi[:, k, :], moe.hi["down"][half][:, k, cols], start=(k == 0), stop=False)
                                nc.tensor.matmul(y[j][:, :], hidT_hi[:, k, :], moe.rest["down"][half][:, k, cols], start=False, stop=False)
                        pe.wait_ge(hidT_lo_made, b + 1)
                        for k in range(FT):
                            for j in range(2):
                                ins = nc.tensor.matmul(y[j][:, :], hidT_lo[:, k, :], moe.hi["down"][half][:, k, 512 * j:512 * j + 512],
                                                       start=False, stop=(k == FT - 1))
                        ins.then_inc(downed, 1)


def finish(nc, io, keep):
    with ExitStack() as stack:
        p = Pools(nc, stack)
        R = 9
        x1 = p.sb("x1f", [P, R, D])
        squares = p.sb("squaresf", [P, D])
        norm_g = p.sb("norm_gf", [P, D])
        stats = p.sb("statsf", [P, TT, 3])
        eps = p.sb("epsf", [P, 1])
        eps_set = p.sem("eps_setf")
        g_loaded = p.sem("g_loadedf")
        x_loaded = [p.sem(f"x_loadedf{i}") for i in range(R)]
        y_stored = [p.sem(f"out_storedf{i}") for i in range(R)]
        squared = p.sem("squaredf")
        rooted = p.sem("rootedf")
        dve_step = p.sem("dve_stepf")
        scaled = p.sem("scaledf")
        block = stack.enter_context(nc.Block())

        @block.sync
        def _(sp):
            sp.dma_start(norm_g[:, :], io["norm_final"].partition_broadcast(P)).then_inc(g_loaded, 16)
            for t in range(TT):
                if t >= R:
                    sp.wait_ge(y_stored[t % R], 16 * (t // R))
                n = tokens(t)
                sp.dma_start(x1[0:n, t % R, :], io["x1"][P * t:P * t + n, :]).then_inc(x_loaded[t % R], 16)
            for s in range(R):
                sp.wait_ge(y_stored[s], 16 * (TT // R))

        @block.scalar
        def _(act):
            act.wait_ge(eps_set, 1)
            for t in range(TT):
                n = tokens(t)
                act.wait_ge(x_loaded[t % R], 16 * (t // R + 1))
                if t:
                    act.wait_ge(squared, t)
                nc.scalar.activation(squares[0:n, :], x1[0:n, t % R, :], ACT.Square, accum_out=stats[0:n, t, 0:1]).then_inc(squared, 1)
                act.wait_ge(squared, t + 1)
                nc.scalar.activation(stats[0:n, t, 1:2], stats[0:n, t, 0:1], ACT.Sqrt, bias=eps[0:n, :], scale=1.0 / D).then_inc(rooted, 1)
                act.wait_ge(scaled, t + 1)
                act.dma_start(io["y"][t], x1[0:n, t % R, :]).then_inc(y_stored[t % R], 16)

        @block.vector
        def _(dve):
            step = stepper(dve, dve_step)
            nc.vector.memset(eps[:, :], EPS).then_inc(eps_set, 1)
            dve.wait_ge(g_loaded, 16)

            for t in range(TT):
                n = tokens(t)
                x = x1[0:n, t % R, :]
                dve.wait_ge(rooted, t + 1)
                step(nc.vector.reciprocal(stats[0:n, t, 2:3], stats[0:n, t, 1:2]))
                nc.vector.scalar_tensor_tensor(out=x, in0=x, scalar=stats[0:n, t, 2:3], in1=norm_g[0:n, :],
                                               op0=ALU.mult, op1=ALU.mult).then_inc(scaled, 1)


def constants():
    return {"bias_rows": bias_rows(), "sink_pick": np.tile(np.eye(A_H, dtype=np.float32), (1, P // A_H))}


def program(nc, ins, outs, upto=9):
    io = {k: ins[k] for k in ("norm_mix", "norm_ffn", "norm_final", "bias_rows")}
    xp = ins["x_prompt"].rearrange("o (t p) d -> (o t) p d", p=P)
    xs = ins["x_sample"].rearrange("b t d -> (b t) d")
    io["x"] = [xp[t] for t in range(QT_N)] + [xs]
    io["table"] = ins["rel_bias_table"]
    io["w_in"] = ins["w_in"].rearrange("l (k p) c -> p (l k) c", p=P)
    io["state_conv"] = ins["state_conv"].rearrange("l b s c -> (l b s) c")
    io["conv_w"] = ins["conv_w"].rearrange("l s c -> (l s) c")
    io["norm_mix"] = ins["norm_mix"].rearrange("l d -> (l d)")
    io["a_k_prompt"] = outs["a_k_prompt"].rearrange("l b t h d -> (l b t) (h d)")
    io["a_v_prompt"] = outs["a_v_prompt"].rearrange("l b t h d -> (l b t) (h d)")
    for n in "kv":
        rows = outs[f"b_{n}_prompt"].rearrange("l b (t p) h d -> (l b t) p (h d)", p=P)
        io[f"b_{n}_prompt"] = [rows[t] for t in range(QT_N)]
        io[f"a_{n}_sample"] = outs[f"a_{n}_sample"].rearrange("l b t h d -> (l b t) (h d)")
        io[f"b_{n}_sample"] = outs[f"b_{n}_sample"].rearrange("l b t h d -> (l b t) (h d)")
    io["conv_prompt"] = outs["conv_prompt"].rearrange("l b s c -> (l b s) c")
    io["conv_sample"] = outs["conv_sample"].rearrange("l b s c -> (l b s) c")
    bias = nc.dram_tensor("bias_scratch", (A_H + B_H, P * GW + P), F32, kind="Internal").ap()
    io["bias"] = [bias[h, 0:P * GW].rearrange("(p y) -> p y", p=P) for h in range(A_H + B_H)]
    io["bias_skewed"] = [bias[h, P + 7:P + 7 + P * GPITCH].rearrange("(p y) -> p y", p=P) for h in range(A_H + B_H)]
    io["bias_row"] = bias
    io["sinks"] = ins["attn_sinks"].rearrange("l h -> (l h)")
    io["sink_pick"] = ins["sink_pick"]
    for n in "kv":
        io[f"cache_a_{n}"] = ins[f"cache_a_{n}"].rearrange("l b t h d -> t (l b) (h d)")
        rows = ins[f"cache_b_{n}"].rearrange("l b t h d -> (l b) t (h d)")
        io[f"cache_b_{n}_far"] = [[rows[b, 256 * k:256 * k + 256].rearrange("(a r) c -> a r c", r=16)[:, 0:NT, :]
                                   for k in range(2)] for b in range(NB)]
        io[f"cache_b_{n}_near"] = [rows[b, SEQ // 2:SEQ].rearrange("(k p) c -> p k c", p=P) for b in range(NB)]
    io["a_v_new"] = outs["a_v_sample"].rearrange("l b t h d -> t (l b) (h d)")
    vn = outs["b_v_sample"].rearrange("l b t h d -> (l b) t (h d)")
    io["b_v_new"] = [vn[b] for b in range(NB)]
    io["w_out"] = ins["w_out"].rearrange("l r c -> (l r) c")
    for n in ("norm_ffn", "b_group", "b_router"):
        io[n] = ins[n].rearrange("l d -> (l d)")
    for n in ("w_group", "w_router"):
        io[n] = ins[n].rearrange("l (k p) c -> p (l k) c", p=P)
    for n in ("w_gate", "w_up", "w_down"):
        io[n] = ins[n].rearrange("l e r c -> (l e) r c")
    yp = outs["y_prompt"].rearrange("o (t p) d -> (o t) p d", p=P)
    io["y"] = [yp[t] for t in range(QT_N)] + [outs["y_sample"].rearrange("b t d -> (b t) d")]
    io["x1"] = nc.dram_tensor("x1_rows", (TOK + P, D), F32, kind="Internal").ap()
    io["h"] = nc.dram_tensor("h_rows", (TOK + P, D), F32, kind="Internal").ap()
    with ExitStack() as stack:
        p = Pools(nc, stack)
        keep = {"ident": p.sb("ident", [P, P]), 
                "ends": p.sb("ends", [P, NE + 1], I32), "slot_ids": p.sb("slot_ids", [P, MAXB + 3], I32),
                "slot_w": p.sb("slot_w", [P, MAXB])}
        moe = keep["moe"] = ExpertWeights(nc, io, p)
        with ExitStack() as later:
            q = Pools(nc, later)
            moe.place(q, 1)
            moe.place_hi(q, "gate", 1)
            keep["silu"] = q.sb("silu", [P, FF])
        keep["mixT"] = p.sb("mixT", [P, 8, TOK])
        with ExitStack() as before:
            keep["w_rest"] = Pools(nc, before).sb("w_rest", [P, 2, KD * VW], F32R)
        keep["stage"] = p.sb("stage", [P, KD * D])
        with ExitStack() as heads:
            r = Pools(nc, heads)
            keep["KT"] = r.sb("KT", [P, 4, TOK])
            keep["V"] = r.sb("V", [P, TT, VW])
            project_in(nc, io, keep)
            if upto >= 2:
                attend(nc, io, keep)
        moe.place(p, 0)
        moe.place_hi(p, "gate", 0)
        moe.place_hi(p, "up", 0)
        if upto >= 3:
            mix_out(nc, io, keep)
        if upto >= 5:
            experts(nc, io, keep)
            finish(nc, io, keep)


_OUTS = [("y_prompt", (1, SEQ, D)), ("y_sample", (NB, NT, D)),
         ("a_k_prompt", (1, 1, A_WIN, 2, DH)), ("a_v_prompt", (1, 1, A_WIN, 2, DH)),
         ("b_k_prompt", (1, 1, SEQ, B_H, DH)), ("b_v_prompt", (1, 1, SEQ, B_H, DH)),
         ("conv_prompt", (1, 1, 2, BW)),
         ("a_k_sample", (1, NB, NT, 2, DH)), ("a_v_sample", (1, NB, NT, 2, DH)),
         ("b_k_sample", (1, NB, NT, B_H, DH)), ("b_v_sample", (1, NB, NT, B_H, DH)),
         ("conv_sample", (1, NB, 2, BW))]
_INS = ["x_prompt", "x_sample", "cache_a_k", "cache_a_v", "cache_b_k", "cache_b_v", "state_conv", "rel_bias_table",
        "w_in", "w_out", "conv_w", "attn_sinks", "norm_mix", "norm_ffn", "w_group", "b_group", "w_router", "b_router",
        "w_gate", "w_up", "w_down", "norm_final"]


def kernel(**inputs):
    import numpy as _np
    import concourse.bacc as _bacc
    from concourse import mybir as _mybir
    from concourse.bass_utils import run_bass_kernel_spmd as _run

    nc = _bacc.Bacc("TRN2", target_bir_lowering=False, num_devices=1)
    arrays = {name: _np.ascontiguousarray(inputs[name]) for name in _INS}
    arrays |= constants()
    ins = {n: nc.dram_tensor(f"in_{n}", a.shape, _mybir.dt.from_np(a.dtype), kind="ExternalInput").ap()
           for n, a in arrays.items()}
    outs = {n: nc.dram_tensor(f"out_{n}", shape, _mybir.dt.float32, kind="ExternalOutput").ap() for n, shape in _OUTS}
    program(nc, ins, outs)
    r = _run(nc, [{f"in_{n}": a for n, a in arrays.items()}], core_ids=[0])
    return tuple(r.results[0][f"out_{n}"] for n, _ in _OUTS)
```

```python
from contextlib import ExitStack
import math

import numpy as np

import concourse.bass as bass
from concourse import mybir

F32 = mybir.dt.float32
F32R = mybir.dt.float32r
I32 = mybir.dt.int32
U32 = mybir.dt.uint32
BF16 = mybir.dt.bfloat16
ALU = mybir.AluOpType
ACT = mybir.ActivationFunctionType
AX = mybir.AxisListType

P = 128
D = 1024
KD = D // P
SEQ = 1024
NB, NT = 8, 8
PAST = 1024
TOK = SEQ + NB * NT
QT_N = SEQ // P
TT = QT_N + 1
DH = 64
A_H, B_H = 4, 6
A_WIN = 128
BRANCHES = ((128, 1), (512, 4), (2048, 16))
BW = B_H * DH
VW = 2 * DH + BW
CH = BW // P
EPS = 1e-6
MASK = -1e30
SCALE = DH ** -0.5
NBUCK = 32
FAR = PAST + NT - 1
GW = FAR + P + 1
GPITCH = GW - 1
FARK, NEARK = 256, 512
SK = FARK + NEARK + NT
SKT = (FARK + NEARK) // P
AK = A_WIN + NT
NG, EPG = 4, 4
NE = NG * EPG
FF = 512
FT = FF // P
MAXB = 32
PIECES = ((0, 384), (384, 384), (768, 320))

W_IN_COL = {"qa": 0, "va": 384, "qb": 512, "kb": 896, "vb": 1280, "xc": 1664, "bg": 2048, "cg": 2432}
GROUPS = ("qb", "kb", "qa", "xc", "cg", "bg")


def tokens(t):
    return P if t < QT_N else NB * NT


def bias_rows():
    d = FAR - np.arange(GW)
    dist = np.maximum(d, 0)
    half = NBUCK // 2
    df = np.maximum(dist, half).astype(np.float32)
    large = half + (np.log(df / half) / math.log(2048 / half) * (NBUCK - half)).astype(np.int32)
    bucket = np.where(dist < half, dist, np.minimum(large, NBUCK - 1))
    out = np.zeros((NBUCK + 1, 2, GW), np.float32)
    branches = (((A_WIN, 1),), BRANCHES)
    for kind in range(2):
        seen = sum(((d >= 0) & (d <= w) & (d % r == 0)).astype(np.int64) for w, r in branches[kind])
        out[bucket, kind, np.arange(GW)] = seen > 0
        out[NBUCK, kind] = np.where(seen > 0, np.log(np.maximum(seen, 1)), MASK)
    return out


class Pools:

    def __init__(self, nc, stack):
        self.nc, self.stack = nc, stack

    def sb(self, name, shape, dt=F32):
        return self.stack.enter_context(self.nc.sbuf_tensor(name, shape, dt))

    def ps(self, name, shape, dt=F32):
        return self.stack.enter_context(self.nc.psum_tensor(name, shape, dt))

    def sem(self, name):
        return self.stack.enter_context(self.nc.semaphore(name))


def stepper(eng, sem):
    count = [0]

    def step(ins):
        count[0] += 1
        ins.then_inc(sem, 1)
        eng.wait_ge(sem, count[0])

    return step


def project_in(nc, io, keep):
    mixT, KT, V, ident = keep["mixT"], keep["KT"], keep["V"], keep["ident"]
    with ExitStack() as stack:
        p = Pools(nc, stack)
        xT_hi = p.sb("xT_hi", [P, KD, TOK], F32R)
        xT_rest = p.sb("xT_rest", [P, KD, TOK], F32R)
        w = keep["stage"][:, :].rearrange("p (s c) -> p s c", s=2)
        w_hi = p.sb("w_hi", [P, 2, KD * VW], F32R)
        w_rest = keep["w_rest"]
        KR = 5
        smallT = p.sb("smallT", [P, CH, 19])
        V_flat = V[:, :, :].rearrange("p t c -> p (t c)")
        norm_g, scratch = V_flat[:, 0:D], V_flat[:, D:2 * D]
        bias_out = [V_flat[0:n, 2 * D + GW * k:2 * D + GW * k + GW] for k, n in enumerate((A_H, B_H))]
        UW = 2 + SEQ + NB * (NT + 2)
        U = V_flat[:, 0:CH * UW].rearrange("p (c t) -> p c t", c=CH)
        KT_flat = KT[:, :, :].rearrange("p k t -> p (k t)")
        HEADS = A_H + B_H
        table = KT_flat[0:NBUCK + 1, HEADS * P:HEADS * P + HEADS]
        small = KT_flat[0:19, (HEADS + 1) * P:(HEADS + 1) * P + BW]
        onehot = KT_flat[0:NBUCK + 1, (HEADS + 4) * P:(HEADS + 4) * P + 2 * GW].rearrange("p (k y) -> p k y", k=2)
        XC = mixT[:, 8 - CH:8, :]
        xin = XC.rearrange("p c t -> p (c t)")
        stats = p.sb("stats", [P, TT, 3])
        eps = p.sb("eps", [P, 1])
        k_rows = w[:, 1, 0:KR * BW].rearrange("p (s c) -> p s c", s=KR)
        conv_last = p.sb("conv_last", [P, CH, 18])
        conv_rows = p.sb("conv_rows", [18, BW])
        bank = [p.ps(f"bank{i}", [P, 512]) for i in range(8)]
        x_tile = [xin[:, D * i:D * (i + 1)] for i in range(3)]

        x_loaded = [p.sem(f"x_loaded{i}") for i in range(3)]
        xT_hi_made = p.sem("xT_hi_made")
        xT_rest_made = p.sem("xT_rest_made")
        w_hi_made = p.sem("w_hi_made")
        w_rest_made = p.sem("w_rest_made")
        w_loaded = [p.sem(f"w_loaded{i}") for i in range(2)]
        small_loaded = p.sem("small_loaded")
        g_loaded = p.sem("g_loaded")
        const_ready = p.sem("const_ready")
        pool_step = p.sem("pool_step")
        squared = p.sem("squared")
        rooted = p.sem("rooted")
        dve_step = p.sem("dve_step")
        normed = p.sem("normed")
        turned = p.sem("turned")
        bias_made = p.sem("bias_made")
        bias_act = p.sem("bias_act")
        bias_dve = p.sem("bias_dve")
        bias_stored = p.sem("bias_stored")
        small_turned = p.sem("small_turned")
        projected = p.sem("projected")
        act_out = p.sem("act_out")
        dve_out = p.sem("dve_out")
        v_made = p.sem("v_made")
        v_copied = p.sem("v_copied")
        k_turned = p.sem("k_turned")
        k_copied = p.sem("k_copied")
        k_stored = [p.sem(f"k_stored{i}") for i in range(KR)]
        last_picked = p.sem("last_picked")
        last_turned = p.sem("last_turned")
        last_copied = p.sem("last_copied")
        stored = p.sem("stored")

        W_GROUPS = GROUPS + ("v",)
        act_pieces = {g: (0, 2) if g in ("qb", "kb", "qa", "xc") else () for g in GROUPS}
        dve_pieces = {g: tuple(i for i in range(3) if i not in act_pieces[g]) for g in GROUPS}

        def total(pieces, n):
            return sum(len(pieces[GROUPS[m // CH]]) for m in range(n + 1))

        K_JOBS = [("b", t) for t in range(TT)] + [("a", QT_N - 1), ("a", TT - 1)]

        WAITS = {"qa": 5, "v": 2}

        def w_part(buf, n, c):
            width = VW if W_GROUPS[n] == "v" else BW
            return buf[:, n % 2, KD // 2 * width * c:KD // 2 * width * (c + 1)]

        def w_tiles(buf, n):
            width = VW if W_GROUPS[n] == "v" else BW
            return buf[:, n % 2, 0:KD * width].rearrange("p (k c) -> p k c", k=KD)

        def w_count(n):
            return 16 * sum(WAITS.get(W_GROUPS[m], 1) for m in range(n % 2, n + 1, 2))

        K_AFTER = [[t] for t in range(TT - 2)] + [[TT - 2, TT - 1], [TT, TT + 1]]

        block = stack.enter_context(nc.Block())

        @block.sync
        def _(sp):
            for t in range(3):
                sp.dma_start(x_tile[t], io["x"][t]).then_inc(x_loaded[t], 16)
            sp.dma_start(norm_g[:, :], io["norm_mix"].partition_broadcast(P)).then_inc(g_loaded, 16)
            sp.dma_start(onehot, io["bias_rows"]).then_inc(small_loaded, 16)
            sp.dma_start(table[0:NBUCK, :], io["table"]).then_inc(small_loaded, 16)
            sp.dma_start(small[0:16, :], io["state_conv"]).then_inc(small_loaded, 16)
            sp.dma_start(small[16:19, :], io["conv_w"]).then_inc(small_loaded, 16)

            def load_w(n):
                g, s = W_GROUPS[n], n % 2
                if n >= 2:
                    sp.wait_ge(projected, CH * (n - 1))
                if g == "v":
                    dst = w[:, s, :].rearrange("p (k c) -> p k c", k=KD)
                    sp.dma_start(dst[:, :, 0:P], io["w_in"][:, :, 384:512]).then_inc(w_loaded[s], 16)
                    sp.dma_start(dst[:, :, P:VW], io["w_in"][:, :, 1280:1664]).then_inc(w_loaded[s], 16)
                    return
                dst = w[:, s, 0:KD * BW].rearrange("p (k c) -> p k c", k=KD)
                c = W_IN_COL[g]
                if g == "qa":
                    for h in range(A_H):
                        at = P * (h % 2) + DH * (h // 2)
                        sp.dma_start(dst[:, :, at:at + DH], io["w_in"][:, :, DH * h:DH * h + DH]).then_inc(w_loaded[s], 16)
                    sp.dma_start(dst[:, :, 256:384], io["w_in"][:, :, 256:384]).then_inc(w_loaded[s], 16)
                else:
                    sp.dma_start(dst, io["w_in"][:, :, c:c + BW]).then_inc(w_loaded[s], 16)

            for t in range(3, TT):
                sp.wait_ge(turned, 2 * (t - 2))
                sp.dma_start(x_tile[t % 3][0:tokens(t), :], io["x"][t]).then_inc(x_loaded[t % 3], 16)
                if t == 5:
                    load_w(0)
            load_w(1)
            for k, heads in enumerate(((0, A_H), (A_H, HEADS))):
                sp.wait_ge(bias_act, k + 1)
                sp.wait_ge(bias_dve, k + 1)
                for h in range(*heads):
                    row = bias_out[k][h - heads[0]:h - heads[0] + 1, :]
                    sp.dma_start(io["bias"][h].unsqueeze(0), row.unsqueeze(1).to_broadcast([1, P, GW])).then_inc(bias_stored, 16)
            for n in range(2, len(W_GROUPS)):
                load_w(n)
            def store_k(n):
                kind, t = K_JOBS[n]
                sp.wait_ge(k_copied, n + 1)
                rows = k_rows[0:tokens(t), n % KR, 0:BW if kind == "b" else P]
                to = (io["b_k_sample"] if t == QT_N else io["b_k_prompt"][t]) if kind == "b" else \
                    (io["a_k_sample"] if t == QT_N else io["a_k_prompt"])
                sp.dma_start(to, rows).then_inc(k_stored[n % KR], 16)

            for t in range(TT):
                sp.wait_ge(v_copied, t + 1)
                if t == QT_N - 1:
                    sp.dma_start(io["a_v_prompt"], V[:, t, 0:P]).then_inc(stored, 16)
                if t == QT_N:
                    sp.dma_start(io["a_v_sample"], V[0:NB * NT, t, 0:P]).then_inc(stored, 16)
                    sp.dma_start(io["b_v_sample"], V[0:NB * NT, t, P:VW]).then_inc(stored, 16)
                else:
                    sp.dma_start(io["b_v_prompt"][t], V[:, t, P:VW]).then_inc(stored, 16)
                if t == 0:
                    sp.wait_ge(last_copied, 1)
                    sp.dma_start(io["conv_prompt"], conv_rows[0:2, :]).then_inc(stored, 16)
                    sp.dma_start(io["conv_sample"], conv_rows[2:18, :]).then_inc(stored, 16)
                for n in K_AFTER[t]:
                    store_k(n)
            sp.wait_ge(stored, 16 * (TT + 2 + 2))
            for s in range(KR):
                sp.wait_ge(k_stored[s], 16 * len(range(s, len(K_JOBS), KR)))
            sp.wait_ge(bias_stored, 16 * HEADS)

        @block.gpsimd
        def _(pool):
            nc.gpsimd.memset(ident[:, :], 0.0).then_inc(pool_step, 1)
            pool.wait_ge(pool_step, 1)
            nc.gpsimd.affine_select(out=ident[:, :], in_=ident[:, :], compare_op=ALU.not_equal, fill=1.0,
                                    base=0, pattern=[[-1, P]], channel_multiplier=1).then_inc(const_ready, 1)
            pool.wait_ge(const_ready, 1)
            nc.gpsimd.memset(eps[:, :], EPS).then_inc(const_ready, 1)
            pool.wait_ge(const_ready, 2)
            nc.gpsimd.memset(table[NBUCK:NBUCK + 1, :], 1.0).then_inc(const_ready, 1)

        @block.scalar
        def _(act):
            def root(t):
                n = tokens(t)
                act.wait_ge(squared, t + 1)
                nc.scalar.activation(stats[0:n, t, 1:2], stats[0:n, t, 0:1], ACT.Sqrt, bias=eps[0:n, :],
                                     scale=1.0 / D).then_inc(rooted, 1)

            def x_hi(t):
                m = tokens(t)
                for c in range(2):
                    act.wait_ge(turned, 2 * t + c + 1)
                    nc.scalar.activation(xT_hi[:, 4 * c:4 * c + 4, P * t:P * t + m],
                                         bank[2 * (t % 2) + c][:, :].rearrange("p (k c) -> p k c", k=4)[:, :, 0:m],
                                         ACT.Copy).then_inc(xT_hi_made, 1)

            def split_w(n):
                act.wait_ge(w_loaded[n % 2], w_count(n))
                for c in range(2):
                    nc.scalar.activation(w_part(w_hi, n, c), w_part(w, n, c), ACT.Copy).then_inc(w_hi_made, 1)

            act.wait_ge(const_ready, 2)
            for t in range(TT):
                n = tokens(t)
                act.wait_ge(x_loaded[t % 3], 16 * (t // 3 + 1))
                if t:
                    act.wait_ge(squared, t)
                nc.scalar.activation(scratch[0:n, :], x_tile[t % 3][0:n, :], ACT.Square,
                                     accum_out=stats[0:n, t, 0:1]).then_inc(squared, 1)
                root(t)
                if t >= 1:
                    x_hi(t - 1)
            x_hi(TT - 1)
            split_w(0)
            for k in range(2):
                act.wait_ge(bias_made, k + 1)
                n = (A_H, B_H)[k]
                nc.scalar.activation(bias_out[k][:, 0:512], bank[3 * k][0:n, :], ACT.Copy).then_inc(bias_act, 1)
            for n in range(CH * len(GROUPS)):
                g, j = GROUPS[n // CH], n % CH
                if g == "xc" and j == 0:
                    act.wait_ge(xT_rest_made, 2 * TT)
                for i in act_pieces[g]:
                    c, m = PIECES[i]
                    act.wait_ge(projected, n + 1)
                    src = bank[3 * (n % 2) + i][:, 0:m]
                    if g == "qb" or (g == "qa" and j < 2):
                        tile = 2 + j if g == "qb" else j
                        nc.scalar.activation(mixT[:, tile, c:c + m], src, ACT.Copy, scale=SCALE).then_inc(act_out, 1)
                    elif g == "xc":
                        nc.scalar.activation(XC[:, j, c:c + m], src, ACT.Copy).then_inc(act_out, 1)
                    else:
                        tile = 1 + j if g == "kb" else 0
                        nc.scalar.activation(KT[:, tile, c:c + m], src, ACT.Copy).then_inc(act_out, 1)
                if j == 0:
                    act.wait_ge(projected, n + 1)
                    split_w(n // CH + 1)
            act.wait_ge(last_picked, 1)
            for t in range(TT):
                act.wait_ge(v_made, t + 1)
                nc.scalar.activation(V[0:tokens(t), t, :], bank[6 + t % 2][0:tokens(t), :], ACT.Copy).then_inc(v_copied, 1)
                for n in K_AFTER[t]:
                    kind, tile = K_JOBS[n]
                    act.wait_ge(k_turned, n + 1)
                    if n >= KR:
                        act.wait_ge(k_stored[n % KR], 16 * (n // KR))
                    c, m = (BW if kind == "b" else P), tokens(tile)
                    nc.scalar.activation(k_rows[0:m, n % KR, 0:c], bank[n % KR][0:m, 0:c], ACT.Copy).then_inc(k_copied, 1)

        @block.vector
        def _(dve):
            step = stepper(dve, dve_step)

            def x_rest(t):
                n = tokens(t)
                for c in range(2):
                    dve.wait_ge(xT_hi_made, 2 * t + c + 1)
                    cols = (slice(None), slice(4 * c, 4 * c + 4), slice(P * t, P * t + n))
                    nc.vector.tensor_tensor(xT_rest[cols], bank[2 * (t % 2) + c][:, :].rearrange("p (k c) -> p k c", k=4)[:, :, 0:n],
                                            xT_hi[cols].bitcast(F32), ALU.subtract).then_inc(xT_rest_made, 1)

            def rest_w(n):
                for c in range(2):
                    dve.wait_ge(w_hi_made, 2 * n + c + 1)
                    nc.vector.tensor_tensor(w_part(w_rest, n, c), w_part(w, n, c), w_part(w_hi, n, c).bitcast(F32),
                                            ALU.subtract).then_inc(w_rest_made, 1)

            dve.wait_ge(g_loaded, 16)
            for t in range(TT):
                n = tokens(t)
                dve.wait_ge(rooted, t + 1)
                step(nc.vector.reciprocal(stats[0:n, t, 2:3], stats[0:n, t, 1:2]))
                nc.vector.scalar_tensor_tensor(out=x_tile[t % 3][0:n, :], in0=x_tile[t % 3][0:n, :],
                                               scalar=stats[0:n, t, 2:3], in1=norm_g[0:n, :],
                                               op0=ALU.mult, op1=ALU.mult).then_inc(normed, 1)
                if t:
                    x_rest(t - 1)
            x_rest(TT - 1)
            rest_w(0)
            for k in range(2):
                dve.wait_ge(bias_made, k + 1)
                n = (A_H, B_H)[k]
                nc.vector.tensor_copy(bias_out[k][:, 512:1024], bank[3 * k + 1][0:n, :])
                nc.vector.tensor_copy(bias_out[k][:, 1024:GW], bank[3 * k + 2][0:n, 0:GW - 1024]).then_inc(bias_dve, 1)
            dve.wait_ge(small_turned, 1)
            step(nc.vector.tensor_copy(smallT[:, :, :], bank[6][:, 0:CH * 32].rearrange("p (c s) -> p c s", c=CH)[:, :, 0:19]))

            def begin_u():
                dve.wait_ge(bias_stored, 16 * HEADS)
                step(nc.vector.memset(U[:, :, 0:2], 0.0))
                for j in range(CH):
                    step(nc.vector.tensor_copy(U[:, j, 2 + SEQ:].rearrange("p (b t) -> p b t", b=NB)[:, :, 0:2],
                                               smallT[:, j, 0:16].rearrange("p (b s) -> p b s", b=NB)))

            def u_cols(j, c, m, shift):
                out = []
                if c < SEQ:
                    m1 = min(m, SEQ - c)
                    out.append((U[:, j, c + shift:c + shift + m1], lambda a: a[:, 0:m1], m1))
                if c + m > SEQ:
                    m1 = max(0, SEQ - c)
                    v = U[:, j, 2 + SEQ:].rearrange("p (b t) -> p b t", b=NB)[:, :, shift:shift + NT]
                    out.append((v, lambda a: a[:, m1:m].rearrange("p (b t) -> p b t", b=NB), m - m1))
                return out

            for n in range(CH * len(GROUPS)):
                g, j = GROUPS[n // CH], n % CH
                if g == "cg" and j == 0:
                    begin_u()
                    dve.wait_ge(act_out, total(act_pieces, CH * 4 - 1))
                for i in dve_pieces[g]:
                    c, m = PIECES[i]
                    dve.wait_ge(projected, n + 1)
                    src = bank[3 * (n % 2) + i][:, 0:m]
                    if g == "qb" or (g == "qa" and j < 2):
                        tile = 2 + j if g == "qb" else j
                        nc.vector.tensor_scalar(mixT[:, tile, c:c + m], src, SCALE, None, ALU.mult).then_inc(dve_out, 1)
                    elif g == "cg":
                        for to, pick, _ in u_cols(j, c, m, 2):
                            ins = nc.vector.tensor_tensor(to, pick(src), pick(XC[:, j, c:c + m]), ALU.mult)
                        ins.then_inc(dve_out, 1)
                    elif g == "bg":
                        nc.vector.tensor_tensor(mixT[:, 5 + j, c:c + m], src, XC[:, j, c:c + m], ALU.mult).then_inc(dve_out, 1)
                    elif g == "xc":
                        nc.vector.tensor_copy(XC[:, j, c:c + m], src).then_inc(dve_out, 1)
                    else:
                        tile = 1 + j if g == "kb" else 0
                        nc.vector.tensor_copy(KT[:, tile, c:c + m], src).then_inc(dve_out, 1)
                if j == 0:
                    rest_w(n // CH + 1)
                if g == "cg":
                    dve.wait_ge(dve_out, total(dve_pieces, n))
                    for c, m in ((0, SEQ), (SEQ, NB * NT)):
                        for k in range(3):
                            (src, pick, _), = u_cols(j, c, m, k)
                            y = pick(XC[:, j, c:c + m])
                            tap = smallT[:, j, 16 + k:17 + k]
                            if k == 0:
                                step(nc.vector.tensor_scalar(y, src, tap, None, ALU.mult))
                            else:
                                step(nc.vector.scalar_tensor_tensor(out=y, in0=src, scalar=tap, in1=y,
                                                                    op0=ALU.mult, op1=ALU.add))
                    if j == CH - 1:
                        nc.vector.tensor_copy(conv_last[:, :, 0:2], U[:, :, SEQ:SEQ + 2])
                        nc.vector.tensor_copy(conv_last[:, :, 2:18].rearrange("p c (b s) -> p c b s", b=NB),
                                              U[:, :, 2 + SEQ:].rearrange("p c (b t) -> p c b t", b=NB)[:, :, :, NT:NT + 2]).then_inc(last_picked, 1)
            dve.wait_ge(last_turned, 1)
            nc.vector.tensor_copy(conv_rows[:, :], bank[5][0:18, 0:BW]).then_inc(last_copied, 1)

        @block.tensor
        def _(pe):
            pe.wait_ge(const_ready, 2)
            for t in range(TT):
                n = tokens(t)
                pe.wait_ge(normed, t + 1)
                if t >= 2:
                    pe.wait_ge(xT_rest_made, 2 * t - 2)
                for k in range(KD):
                    ins = nc.tensor.transpose(bank[2 * (t % 2) + k // 4][:, P * (k % 4):P * (k % 4) + n],
                                              x_tile[t % 3][0:n, P * k:P * k + P], ident[0:n, 0:n])
                    if k == 3:
                        ins.then_inc(turned, 1)
                ins.then_inc(turned, 1)
            pe.wait_ge(small_loaded, 64)
            for c in range(CH):
                ins = nc.tensor.transpose(bank[6][:, 32 * c:32 * c + 19], small[:, P * c:P * c + P], ident[0:19, 0:19])
            ins.then_inc(small_turned, 1)
            pe.wait_ge(const_ready, 3)
            pe.wait_ge(xT_rest_made, 2 * TT)
            for k, heads in enumerate((slice(0, A_H), slice(A_H, HEADS))):
                for i, (c, m) in enumerate(((0, 512), (512, 512), (1024, GW - 1024))):
                    ins = nc.tensor.matmul(bank[3 * k + i][0:heads.stop - heads.start, 0:m], table[:, heads], onehot[:, k, c:c + m],
                                           start=True, stop=True)
                ins.then_inc(bias_made, 1)
            pe.wait_ge(bias_act, 2)
            pe.wait_ge(bias_dve, 2)
            for n in range(CH * len(GROUPS)):
                g, j = GROUPS[n // CH], n % CH
                if j == 0:
                    pe.wait_ge(w_rest_made, 2 * (n // CH) + 2)
                if n >= 2:
                    pe.wait_ge(act_out, total(act_pieces, n - 2))
                    pe.wait_ge(dve_out, total(dve_pieces, n - 2))
                cols = slice(P * j, P * j + P)
                for k in range(KD):
                    passes = ((w_hi, xT_hi), (w_hi, xT_rest), (w_rest, xT_hi))
                    for x, (wt, xt) in enumerate(passes):
                        for i, (c, m) in enumerate(PIECES):
                            ins = nc.tensor.matmul(bank[3 * (n % 2) + i][:, 0:m], w_tiles(wt, n // CH)[:, k, cols], xt[:, k, c:c + m],
                                                   start=(k == 0 and x == 0), stop=(k == KD - 1 and x == 2))
                ins.then_inc(projected, 1)
            def turn_k(m):
                kind, t = K_JOBS[m]
                if m >= KR:
                    pe.wait_ge(k_copied, m - KR + 1)
                for j in range(CH if kind == "b" else 1):
                    tile = 1 + j if kind == "b" else 0
                    ins = nc.tensor.transpose(bank[m % KR][0:tokens(t), P * j:P * j + P], KT[:, tile, P * t:P * t + tokens(t)], ident[:, :])
                ins.then_inc(k_turned, 1)

            n = len(GROUPS)
            pe.wait_ge(w_rest_made, 2 * n + 2)
            for t in range(TT):
                if t >= 2:
                    pe.wait_ge(v_copied, t - 1)
                for k in range(KD):
                    cols = slice(P * t, P * t + tokens(t))
                    for x, (wt, xt) in enumerate(((w_hi, xT_hi), (w_rest, xT_hi), (w_hi, xT_rest))):
                        ins = nc.tensor.matmul(bank[6 + t % 2][0:tokens(t), :], xt[:, k, cols], w_tiles(wt, n)[:, k, :],
                                               start=(k == 0 and x == 0), stop=(k == KD - 1 and x == 2))
                ins.then_inc(v_made, 1)
                if t == 0:
                    last = CH * len(GROUPS) - 1
                    pe.wait_ge(act_out, total(act_pieces, last))
                    pe.wait_ge(dve_out, total(dve_pieces, last))
                    pe.wait_ge(last_picked, 1)
                    for c in range(CH):
                        ins = nc.tensor.transpose(bank[5][0:18, P * c:P * c + P], conv_last[:, c, :], ident[:, :])
                    ins.then_inc(last_turned, 1)
                for m in K_AFTER[t]:
                    turn_k(m)

def attend(nc, io, keep):
    mixT, KT, V, ident = keep["mixT"], keep["KT"], keep["V"], keep["ident"]
    HEADS = A_H + B_H
    A_ORDER = (0, 2, 1, 3)
    UNITS = QT_N * HEADS
    DUOS = UNITS // 2
    PAIRS = NB // 2
    with ExitStack() as stack:
        p = Pools(nc, stack)
        stage = keep["stage"]
        bias_b = stage[:, 0:B_H * SEQ].rearrange("p (h x) -> p h x", h=B_H)
        bias_a = stage[:, B_H * SEQ:B_H * SEQ + A_H * 2 * P].rearrange("p (h x) -> p h x", h=A_H)
        w_out = stage[:, :].rearrange("p (k c) -> p k c", k=KD)
        negs = p.sb("negs", [P, 2, SEQ])
        probs = p.sb("probs", [P, 2, SEQ])
        probsT = p.sb("probsT", [P, 3, KD, P])
        COLS = UNITS + PAIRS + 2
        neg_max = p.sb("neg_max", [P, COLS])
        denom = p.sb("denom", [P, COLS])
        sink_e = p.sb("sink_e", [P, COLS])
        recip = p.sb("recip", [P, COLS])
        sinks = p.sb("sinks", [P, A_H])
        sink_col = p.sb("sink_col", [A_H, 1])
        sink_pick = p.sb("sink_pick", [A_H, P])
        sink_rows = p.sb("sink_rows", [P, 1])
        bias_sb = p.sb("bias_sb", [P, SK])
        bias_sa = p.sb("bias_sa", [P, AK])
        k_cache = p.sb("k_cache", [P, 2, SKT, BW])
        V_flat = V[:, :, :].rearrange("p t c -> p (t c)")
        v_cache = [p.sb("v_cache", [P, SKT, BW]), V_flat[:, 0:SKT * BW].rearrange("p (t c) -> p t c", t=SKT)]
        va_cache = V_flat[:, SKT * BW:SKT * BW + NB * P].rearrange("p (b c) -> p b c", b=NB)
        values_s = V_flat[:, SKT * BW + NB * P:SKT * BW + NB * P + BW]
        kT_s = p.sb("kT_s", [P, 2, CH, SK])
        ka_cache = p.sb("ka_cache", [P, NB, P])
        kaT_s = p.sb("kaT_s", [P, NB, AK])
        v_new = p.sb("v_new", [NT, 4, BW])
        va_new = p.sb("va_new", [NT, NB, P])
        q_blk = p.sb("q_blk", [P, NB, CH, DH])
        qa_blk = p.sb("qa_blk", [P, NB, NT * A_H])
        score = [p.ps(f"score{i}", [P, SEQ]) for i in range(2)]
        turn = [p.ps(f"turn{i}", [P, 512]) for i in range(2)]
        value = [p.ps(f"value{i}", [P, 512]) for i in range(2)]

        w_out_loaded = p.sem("w_out_loaded")
        bias_loaded = [p.sem(f"bias_loaded{i}") for i in range(QT_N)]
        sinks_loaded = p.sem("sinks_loaded")
        sbias_loaded = p.sem("sbias_loaded")
        sbias_copied = p.sem("sbias_copied")
        a_loaded = p.sem("a_loaded")
        va_loaded = p.sem("va_loaded")
        k_loaded = [p.sem(f"k_loaded{i}") for i in range(2)]
        v_loaded = [p.sem(f"v_loaded{i}") for i in range(2)]
        last_v_loaded = [p.sem(f"last_v_loaded{i}") for i in range(2)]
        blanks = p.sem("blanks")
        q_blocked = p.sem("q_blocked")
        new_k = p.sem("new_k")
        scored = p.sem("scored")
        biased = p.sem("biased")
        exped = p.sem("exped")
        act_step = p.sem("act_step2")
        dve_step = p.sem("dve_step2")
        turned = p.sem("turned2")
        act_turned = p.sem("act_turned")
        dve_turned = p.sem("dve_turned")
        valued = p.sem("valued")
        values_taken = p.sem("values_taken")
        scaled = p.sem("scaled")
        duo_taken = p.sem("duo_taken")
        sink_spread = p.sem("sink_spread")
        sink_ready = p.sem("sink_ready")

        def place(u):
            return (u + A_H) % HEADS

        def unit(u):
            i, s = u // HEADS, place(u)
            if s < A_H:
                first = max(0, i - 1)
                return i, first, i + 1 - first, True, A_ORDER[s]
            return i, 0, i + 1, False, s - A_H

        groups = []

        def add(what, *rest):
            groups.append((what, *rest))

        for u in range(UNITS):
            for k in range(0, unit(u)[2], 4):
                add("probs", u, k, min(4, unit(u)[2] - k))
        for x in range(2):
            add("ka", x)
        def add_keys(r):
            for b in (2 * r, 2 * r + 1):
                for k in range(SKT if r < PAIRS else 0):
                    add("ks", b, k)

        add_keys(0)
        for x in range(2):
            add("aprobs", x)
        for r in range(PAIRS):
            add_keys(r + 1)
            if r:
                add("sout", r - 1)
            add("sprobs", r, 0, 4)
            add("sprobs", r, 4, 3)
        add("sout", PAIRS - 1)

        def bank_key(n):
            if groups[n][0] == "ks" and n // 2 % 2:
                return "score", (groups[n][1] // 2 + 1) % 2, n % 2
            return "turn", 0, n % 2

        def bank_of(n):
            kind, s, half = bank_key(n)
            return score[s][:, 512 * half:512 * half + 512] if kind == "score" else turn[half][:, :]

        last_user, previous = {}, []
        for n in range(len(groups)):
            previous.append(last_user.get(bank_key(n), -1))
            last_user[bank_key(n)] = n

        def wait_taken(eng, upto):
            if upto >= 0:
                eng.wait_ge(act_turned, upto // 2 + 1)
            if upto >= 1:
                eng.wait_ge(dve_turned, (upto + 1) // 2)

        def groups_of(*key):
            return [n for n, g in enumerate(groups) if g[:len(key)] == key]

        def take(eng, n):
            g = groups[n]
            src = bank_of(n)
            eng.wait_ge(turned, n + 1)
            if g[0] == "probs":
                u, k, c = g[1:]
                if u >= 3:
                    eng.wait_ge(valued, (u - 1) // 2)
                out, src = probsT[:, u % 3, k:k + c, :], src[:, 0:P * c].rearrange("p (k c) -> p k c", c=P)
            elif g[0] == "ka":
                out, src = kaT_s[:, 4 * g[1]:4 * g[1] + 4, 0:P], src[:, :].rearrange("p (b c) -> p b c", c=P)
            elif g[0] == "aprobs":
                eng.wait_ge(valued, DUOS)
                x = g[1]
                eng_copy(eng, n, probsT[:, x, 0, :], src[:, 0:P], False)
                out, src = probsT[0:NT, x, 1, :], src[0:NT, P:2 * P]
            elif g[0] == "ks":
                b, k = g[1:]
                if b >= 2:
                    eng.wait_ge(scored, UNITS + b)
                out, src = kT_s[:, b % 2, :, P * k:P * k + P], src[:, 0:BW].rearrange("p (g c) -> p g c", c=P)
            elif g[0] == "sout":
                r = g[1]
                for h in range(B_H):
                    rows, c = slice(DH * (h % 2), DH * (h % 2) + DH), h // 2
                    out = mixT[rows, 2 + c, SEQ + 2 * NT * r:SEQ + 2 * NT * (r + 1)].rearrange("p (b t) -> p b t", b=2)
                    picked = src[rows, P * c:P * c + P].rearrange("p (b x) -> p b x", b=2)[:, :, 0:NT * B_H]
                    eng_copy(eng, n, out, picked.rearrange("p b (t h) -> p b t h", h=B_H)[:, :, :, h], h == B_H - 1)
                return
            else:
                r, k, c = g[1:]
                eng.wait_ge(valued, DUOS + 1 + (r - 1 if r >= 1 else 0))
                full = min(c, SKT - k)
                if full < c:
                    eng_copy(eng, n, probsT[0:NT, r % 2, SKT, :], src[0:NT, P * full:P * c], False)
                out, src = probsT[:, r % 2, k:k + full, :], src[:, 0:P * full].rearrange("p (k c) -> p k c", c=P)
            eng_copy(eng, n, out, src, True)

        def eng_copy(eng, n, out, src, last):
            if n % 2 == 0:
                ins = nc.scalar.activation(out, src, ACT.Copy)
            else:
                ins = nc.vector.tensor_copy(out, src)
            if last:
                ins.then_inc(act_turned if n % 2 == 0 else dve_turned, 1)

        def take_all(eng, parity, *key):
            for n in groups_of(*key):
                if n % 2 == parity:
                    take(eng, n)

        def v_place(b):
            if b >= NB - 2:
                return k_cache[:, b % 2, :, :], last_v_loaded[b % 2]
            return v_cache[b % 2], v_loaded[b % 2]

        block = stack.enter_context(nc.Block())

        @block.sync
        def _(sp):
            for i in range(QT_N):
                lo = SEQ - P * (i + 1)
                sp.dma_start(bias_b[:, :, lo:lo + P], io["bias_skewed"][:, A_H:HEADS, lo:lo + P]).then_inc(bias_loaded[i], 16)
                if i < 2:
                    sp.dma_start(bias_a[:, :, P * (1 - i):P * (2 - i)], io["bias_skewed"][:, 0:A_H, lo:lo + P]).then_inc(bias_loaded[i], 16)
                if i == 0:
                    sp.dma_start(sinks[:, :], io["sinks"].partition_broadcast(P)).then_inc(sinks_loaded, 16)
                    sp.dma_start(sink_col[:, :], io["sinks"].rearrange("(h o) -> h o", o=1)).then_inc(sinks_loaded, 16)
                    sp.dma_start(sink_pick[:, :], io["sink_pick"]).then_inc(sinks_loaded, 16)
            sp.dma_start(ka_cache[:, :, :], io["cache_a_k"]).then_inc(a_loaded, 16)
            sp.dma_start(va_new[:, :, :], io["a_v_new"]).then_inc(a_loaded, 16)
            sp.wait_ge(blanks, 1)
            for t in range(NT):
                sp.dma_start(bias_sb[B_H * t:B_H * t + B_H, 0:FARK],
                             io["bias_row"][A_H:HEADS, NT - 1 - t:NT - 1 - t + SEQ // 2].rearrange("h (a r) -> h a r", r=16)[:, :, 0:NT]).then_inc(sbias_loaded, 16)
                near = NT - 1 - t + SEQ // 2
                sp.dma_start(bias_sb[B_H * t:B_H * t + B_H, FARK:SK],
                             io["bias_row"][A_H:HEADS, near:near + NEARK + NT]).then_inc(sbias_loaded, 16)
                a0 = FAR - A_WIN - t
                sp.dma_start(bias_sa[A_H * t:A_H * t + A_H, :], io["bias_row"][0:A_H, a0:a0 + AK]).then_inc(sbias_loaded, 16)
            sp.wait_ge(sbias_loaded, 16 * 3 * NT)
            sp.dma_start(bias_sb[DH:P, :], bias_sb[0:DH, :]).then_inc(sbias_copied, 16)
            for x in range(1, 4):
                sp.dma_start(bias_sa[32 * x:32 * x + 32, :], bias_sa[0:32, :]).then_inc(sbias_copied, 16)

            def load_k(b):
                if b >= 2:
                    sp.wait_ge(turned, groups_of("ks", b - 2)[-1] + 1)
                for k in range(2):
                    sp.dma_start(k_cache[:, b % 2, k, :], io["cache_b_k_far"][b][k]).then_inc(k_loaded[b % 2], 16)
                sp.dma_start(k_cache[:, b % 2, 2:SKT, :], io["cache_b_k_near"][b]).then_inc(k_loaded[b % 2], 16)

            def load_v(b):
                if b == 1:
                    sp.wait_ge(valued, DUOS)
                    sp.dma_start(va_cache[:, :, :], io["cache_a_v"]).then_inc(va_loaded, 16)
                if 2 <= b < NB - 2:
                    sp.wait_ge(valued, DUOS + 1 + b // 2)
                if b >= NB - 2:
                    sp.wait_ge(turned, groups_of("ks", b)[-1] + 1)
                to, loaded = v_place(b)
                for k in range(2):
                    sp.dma_start(to[:, k, :], io["cache_b_v_far"][b][k]).then_inc(loaded, 16)
                sp.dma_start(to[:, 2:SKT, :], io["cache_b_v_near"][b]).then_inc(loaded, 16)
                sp.dma_start(v_new[:, b % 4, :], io["b_v_new"][b]).then_inc(loaded, 16)

            for b in (0, 1):
                load_k(b)
            for b in (0, 1):
                load_v(b)
            for b in (2, 3):
                load_k(b)
            sp.wait_ge(biased, UNITS)
            for j in range(2):
                for hh in range(2):
                    r0 = DH * (2 * hh + j)
                    sp.dma_start(w_out[DH * hh:DH * hh + DH, j, :], io["w_out"][r0:r0 + DH, :]).then_inc(w_out_loaded, 16)
            sp.dma_start(w_out[:, 2:KD, :], io["w_out"][2 * P:, :].rearrange("(k p) c -> p k c", p=P)).then_inc(w_out_loaded, 16)
            for r in range(1, PAIRS):
                if r + 1 < PAIRS:
                    load_k(2 * r + 2)
                    load_k(2 * r + 3)
                load_v(2 * r)
                load_v(2 * r + 1)
            sp.wait_ge(w_out_loaded, 80)

        @block.gpsimd
        def _(pool):
            nc.gpsimd.memset(bias_sb[:, :], 0.0).then_inc(blanks, 1)
            pool.wait_ge(blanks, 1)
            nc.gpsimd.memset(q_blk[:, :, :, :], 0.0).then_inc(blanks, 1)
            pool.wait_ge(blanks, 2)
            nc.gpsimd.memset(qa_blk[:, :, :], 0.0).then_inc(blanks, 1)
            pool.wait_ge(blanks, 3)
            done = 0
            for h in range(B_H):
                half, g = DH * (h % 2), h // 2
                nc.gpsimd.tensor_copy(q_blk[half:half + DH, :, g, 0:NT * B_H].rearrange("p b (t h) -> p b t h", h=B_H)[:, :, :, h],
                                      mixT[half:half + DH, 2 + g, SEQ:TOK].rearrange("p (b t) -> p b t", b=NB)).then_inc(q_blocked, 1)
                done += 1
                pool.wait_ge(q_blocked, done)
            for h in range(A_H):
                half = DH * (h // 2)
                nc.gpsimd.tensor_copy(qa_blk[half:half + DH, :, :].rearrange("p b (t h) -> p b t h", h=A_H)[:, :, :, h],
                                      mixT[half:half + DH, h % 2, SEQ:TOK].rearrange("p (b t) -> p b t", b=NB)).then_inc(q_blocked, 1)
                done += 1
                pool.wait_ge(q_blocked, done)
            nc.gpsimd.tensor_copy(kaT_s[:, :, P:AK], KT[:, 0, SEQ:TOK].rearrange("p (b t) -> p b t", b=NB)).then_inc(new_k, 1)

        @block.scalar
        def _(act):
            def exp(u, col, n, rows_sink):
                nc.scalar.activation(probs[:, u % 2, 0:n], negs[:, u % 2, 0:n], ACT.Exp, bias=neg_max[:, col:col + 1],
                                     scale=-1.0, accum_out=denom[:, col:col + 1]).then_inc(exped, 1)
                if rows_sink is not None:
                    nc.scalar.activation(sink_e[:, col:col + 1], rows_sink, ACT.Exp,
                                         bias=neg_max[:, col:col + 1]).then_inc(act_step, 1)

            def exp_unit(u):
                _, _, k, window, h = unit(u)
                act.wait_ge(biased, u + 1)
                if u >= 2:
                    act.wait_ge(turned, groups_of("probs", u - 2)[-1] + 1)
                exp(u, u, P * k, sinks[:, h:h + 1] if window else None)

            def duo_out(q):
                i, _, _, window, h = unit(2 * q)
                act.wait_ge(valued, q + 1)
                nc.scalar.activation(mixT[:, h % 2 if window else 2 + h // 2, P * i:P * i + P], value[q % 2][:, 0:P],
                                     ACT.Copy).then_inc(duo_taken, 1)

            act.wait_ge(sinks_loaded, 48)
            exp_unit(0)
            for u in range(UNITS):
                if u % 2 and u >= 3:
                    duo_out(u // 2 - 1)
                if u + 1 < UNITS:
                    exp_unit(u + 1)
                take_all(act, 0, "probs", u)
            duo_out(DUOS - 1)
            take_all(act, 0, "ka")
            act.wait_ge(sink_ready, 1)
            act.wait_ge(turned, groups_of("probs", UNITS - 1)[-1] + 1)
            for x in range(2):
                act.wait_ge(biased, UNITS + x + 1)
                exp(x, UNITS + PAIRS + x, AK, sink_rows[:, :])
            for b in (0, 1):
                take_all(act, 0, "ks", b)
            take_all(act, 0, "aprobs")
            for r in range(PAIRS):
                take_all(act, 0, "ks", 2 * r + 2)
                act.wait_ge(biased, UNITS + 2 + r + 1)
                if r < 2:
                    act.wait_ge(turned, groups_of("aprobs", r)[-1] + 1)
                else:
                    act.wait_ge(turned, groups_of("sprobs", r - 2)[-1] + 1)
                exp(r, UNITS + r, SK, None)
                take_all(act, 0, "ks", 2 * r + 3)
                take_all(act, 0, "sout", r - 1)
                take_all(act, 0, "sprobs", r)
                act.wait_ge(valued, DUOS + 1 + r + 1)
                if r:
                    act.wait_ge(turned, groups_of("sout", r - 1)[0] + 1)
                nc.scalar.activation(values_s[:, :], value[0][:, 0:BW], ACT.Copy).then_inc(values_taken, 1)
            take_all(act, 0, "sout", PAIRS - 1)

        @block.vector
        def _(dve):
            step = stepper(dve, dve_step)

            def bias(u):
                i, first, k, window, h = unit(u)
                if u % HEADS == 0:
                    dve.wait_ge(bias_loaded[i], 32 if i < 2 else 16)
                dve.wait_ge(scored, u + 1)
                if u >= 2:
                    dve.wait_ge(exped, u - 1)
                n = P * k
                table = bias_a[:, h, 2 * P - n:2 * P] if window else bias_b[:, h, SEQ - n:SEQ]
                nc.vector.tensor_tensor_reduce(negs[:, u % 2, 0:n], score[u % 2][:, 0:n], table, -1.0, 0.0 - MASK,
                                               ALU.add, ALU.min, neg_max[:, u:u + 1]).then_inc(biased, 1)

            windows_seen = 0

            def scale(u):
                nonlocal windows_seen
                i, first, k, window, h = unit(u)
                dve.wait_ge(exped, u + 1)
                if window:
                    windows_seen += 1
                    dve.wait_ge(act_step, windows_seen)
                    step(nc.vector.tensor_tensor(denom[:, u:u + 1], denom[:, u:u + 1], sink_e[:, u:u + 1], ALU.add))
                step(nc.vector.reciprocal(recip[:, u:u + 1], denom[:, u:u + 1]))
                nc.vector.tensor_scalar(probs[:, u % 2, 0:P * k], probs[:, u % 2, 0:P * k], recip[:, u:u + 1], None,
                                        ALU.mult).then_inc(scaled, 1)

            bias(0)
            scale(0)
            for u in range(UNITS):
                if u + 1 < UNITS:
                    bias(u + 1)
                take_all(dve, 1, "probs", u)
                if u + 1 < UNITS:
                    scale(u + 1)
            take_all(dve, 1, "ka")
            dve.wait_ge(sink_spread, 1)
            nc.vector.tensor_copy(sink_rows[:, :], value[1][:, 0:1]).then_inc(sink_ready, 1)
            dve.wait_ge(sbias_copied, 64)
            dve.wait_ge(exped, UNITS)
            dve.wait_ge(scored, UNITS + 1)
            for x in range(2):
                nc.vector.tensor_tensor_reduce(negs[:, x, 0:AK], score[0][:, AK * x:AK * x + AK], bias_sa[:, :], -1.0, 0.0 - MASK,
                                               ALU.add, ALU.min, neg_max[:, UNITS + PAIRS + x:UNITS + PAIRS + x + 1]).then_inc(biased, 1)

            def take_keys(b):
                if b < NB:
                    if b >= 2:
                        dve.wait_ge(scored, UNITS + b)
                    nc.vector.tensor_copy(kT_s[:, b % 2, :, P * SKT:SK], KT[:, 1:4, SEQ + NT * b:SEQ + NT * b + NT]).then_inc(new_k, 1)
                    take_all(dve, 1, "ks", b)

            take_keys(0)
            for x in range(2):
                col = UNITS + PAIRS + x
                dve.wait_ge(exped, UNITS + x + 1)
                dve.wait_ge(act_step, windows_seen + x + 1)
                step(nc.vector.tensor_tensor(denom[:, col:col + 1], denom[:, col:col + 1], sink_e[:, col:col + 1], ALU.add))
                step(nc.vector.reciprocal(recip[:, col:col + 1], denom[:, col:col + 1]))
                nc.vector.tensor_scalar(probs[:, x, 0:AK], probs[:, x, 0:AK], recip[:, col:col + 1], None, ALU.mult).then_inc(scaled, 1)
            take_keys(1)
            take_all(dve, 1, "aprobs")
            for r in range(PAIRS):
                col = UNITS + r
                dve.wait_ge(scored, UNITS + 1 + 2 * r + 2)
                dve.wait_ge(exped, UNITS + 2 + (r - 1 if r >= 2 else 0))
                nc.vector.tensor_tensor_reduce(negs[:, r % 2, 0:SK], score[(r + 1) % 2][:, 0:SK], bias_sb[:, :], -1.0, 0.0 - MASK,
                                               ALU.add, ALU.min, neg_max[:, col:col + 1]).then_inc(biased, 1)
                take_keys(2 * r + 2)
                dve.wait_ge(exped, UNITS + 2 + r + 1)
                step(nc.vector.reciprocal(recip[:, col:col + 1], denom[:, col:col + 1]))
                nc.vector.tensor_scalar(probs[:, r % 2, 0:SK], probs[:, r % 2, 0:SK], recip[:, col:col + 1], None, ALU.mult).then_inc(scaled, 1)
                take_keys(2 * r + 3)
                take_all(dve, 1, "sout", r - 1)
                take_all(dve, 1, "sprobs", r)
                if r == 0:
                    dve.wait_ge(valued, DUOS + 1)
                    for hh in range(2):
                        rows = slice(DH * hh, DH * hh + DH)
                        for j in range(2):
                            nc.vector.tensor_copy(mixT[rows, j, SEQ:TOK].rearrange("p (b t) -> p b t", b=NB),
                                                  value[1][rows, 0:NB * 32].rearrange("p (b t h) -> p b t h", b=NB, h=A_H)[:, :, :, 2 * hh + j])
            take_all(dve, 1, "sout", PAIRS - 1)

        @block.tensor
        def _(pe):
            def bank_for(n):
                wait_taken(pe, previous[n])
                return bank_of(n)

            def scores(u):
                i, first, k, window, h = unit(u)
                half = DH * (h // 2 if window else h % 2)
                qt = h % 2 if window else 2 + h // 2
                kt = 0 if window else 1 + h // 2
                if u >= 2:
                    pe.wait_ge(biased, u - 1)
                for c in range(0, k, 4):
                    m = P * min(4, k - c)
                    ins = nc.tensor.matmul(score[u % 2][:, P * c:P * c + m], mixT[half:half + DH, qt, P * i:P * i + P],
                                           KT[half:half + DH, kt, P * (first + c):P * (first + c) + m], start=True, stop=True)
                ins.then_inc(scored, 1)

            def turn_probs(u):
                pe.wait_ge(scaled, u + 1)
                for n in groups_of("probs", u):
                    _, _, k, c = groups[n]
                    bank = bank_for(n)
                    for x in range(c):
                        ins = nc.tensor.transpose(bank[:, P * x:P * x + P], probs[:, u % 2, P * (k + x):P * (k + x) + P], ident[:, :])
                    ins.then_inc(turned, 1)

            def values(q, part):
                i, first, k, window, _ = unit(2 * q)
                if part == 0:
                    wait_taken(pe, groups_of("probs", 2 * q + 1)[-1])
                    if q >= 2:
                        pe.wait_ge(duo_taken, q - 1)
                mid = (k + 1) // 2
                for x in range(mid * part, k if part else mid):
                    for u in (2 * q, 2 * q + 1):
                        h = unit(u)[4]
                        half = DH * (h // 2 if window else h % 2)
                        c0 = DH * (h // 2) if window else P + DH * h
                        ins = nc.tensor.matmul(value[q % 2][half:half + DH, 0:P], V[:, first + x, c0:c0 + DH], probsT[:, u % 3, x, :],
                                               start=(x == 0), stop=(x == k - 1))
                if k == 1 and part == 0:
                    ins.then_inc(valued, 1)
                if k > 1 and part == 1:
                    ins.then_inc(valued, 1)

            scores(0)
            for u in range(UNITS):
                if u + 1 < UNITS:
                    scores(u + 1)
                if u % 2 and u >= 3:
                    values(u // 2 - 1, 1)
                turn_probs(u)
                if u % 2 == 0 and u >= 2:
                    values(u // 2 - 1, 0)
            values(DUOS - 1, 0)
            values(DUOS - 1, 1)

            pe.wait_ge(a_loaded, 32)
            for x, n in enumerate(groups_of("ka")):
                bank = bank_for(n)
                for b in range(4):
                    ins = nc.tensor.transpose(bank[:, P * b:P * b + P], ka_cache[:, 4 * x + b, :], ident[:, :])
                ins.then_inc(turned, 1)
            pe.wait_ge(duo_taken, DUOS)
            pe.wait_ge(sinks_loaded, 48)
            nc.tensor.matmul(value[1][:, 0:1], sink_pick[:, :], sink_col[:, :], start=True, stop=True).then_inc(sink_spread, 1)
            wait_taken(pe, groups_of("ka")[-1])
            pe.wait_ge(q_blocked, HEADS)
            pe.wait_ge(new_k, 1)
            pe.wait_ge(biased, UNITS)
            for b in range(NB):
                at = 32 * (b % 4)
                ins = nc.tensor.matmul(score[0][at:at + 32, AK * (b // 4):AK * (b // 4) + AK], qa_blk[:, b, :], kaT_s[:, b, :],
                                       start=True, stop=True)
            ins.then_inc(scored, 1)

            def keys(r):
                if r == PAIRS:
                    return
                buf = score[(r + 1) % 2]
                if r:
                    pe.wait_ge(biased, UNITS + 2 + r - 1)
                for b in (2 * r, 2 * r + 1):
                    pe.wait_ge(k_loaded[b % 2], 48 * (r + 1))
                    for n in groups_of("ks", b):
                        bank = bank_for(n)
                        for g in range(CH):
                            ins = nc.tensor.transpose(bank[:, P * g:P * g + P], k_cache[:, b % 2, groups[n][2], P * g:P * g + P], ident[:, :])
                        ins.then_inc(turned, 1)
                wait_taken(pe, groups_of("ks", 2 * r + 1)[-1])
                pe.wait_ge(new_k, 2 + 2 * r + 1)
                for c, m in ((0, 512), (512, SK - 512)):
                    for g in range(CH):
                        for b in (2 * r, 2 * r + 1):
                            at = DH * (b % 2)
                            ins = nc.tensor.matmul(buf[at:at + DH, c:c + m], q_blk[:, b, g, :], kT_s[:, b % 2, g, c:c + m],
                                                   start=(g == 0), stop=(g == CH - 1))
                            if c and g == CH - 1:
                                ins.then_inc(scored, 1)

            keys(0)
            for x, n in enumerate(groups_of("aprobs")):
                pe.wait_ge(scaled, UNITS + x + 1)
                bank = bank_for(n)
                nc.tensor.transpose(bank[:, 0:P], probs[:, x, 0:P], ident[:, :])
                nc.tensor.transpose(bank[0:NT, P:2 * P], probs[:, x, P:AK], ident[:, :]).then_inc(turned, 1)
            wait_taken(pe, groups_of("aprobs")[-1])
            pe.wait_ge(sink_ready, 1)
            pe.wait_ge(va_loaded, 16)
            for b in range(NB):
                out = value[1][:, 32 * b:32 * b + 32]
                cols = slice(32 * (b % 4), 32 * (b % 4) + 32)
                nc.tensor.matmul(out, va_cache[:, b, :], probsT[:, b // 4, 0, cols], start=True, stop=False)
                ins = nc.tensor.matmul(out, va_new[:, b, :], probsT[0:NT, b // 4, 1, cols], start=False, stop=True)
            ins.then_inc(valued, 1)

            def turn_values(r):
                pe.wait_ge(values_taken, r + 1)
                (n,) = groups_of("sout", r)
                bank = bank_for(n)
                for c in range(CH):
                    ins = nc.tensor.transpose(bank[:, P * c:P * c + P], values_s[:, P * c:P * c + P], ident[:, :])
                ins.then_inc(turned, 1)

            for r in range(PAIRS):
                keys(r + 1)
                if r:
                    turn_values(r - 1)
                pe.wait_ge(scaled, UNITS + 2 + r + 1)
                for n in groups_of("sprobs", r):
                    bank = bank_for(n)
                    _, _, k, c = groups[n]
                    for x in range(k, k + c):
                        m = P if x < SKT else NT
                        ins = nc.tensor.transpose(bank[0:m, P * (x - k):P * (x - k) + P], probs[:, r % 2, P * x:P * x + m], ident[:, :])
                    ins.then_inc(turned, 1)
                wait_taken(pe, groups_of("sprobs", r)[-1])
                for b in (2 * r, 2 * r + 1):
                    pe.wait_ge(v_place(b)[1], 64 if r == PAIRS - 1 else 64 * (r + 1))
                for x in range(SKT + 1):
                    for b in (2 * r, 2 * r + 1):
                        at = slice(DH * (b % 2), DH * (b % 2) + DH)
                        if x < SKT:
                            nc.tensor.matmul(value[0][at, 0:BW], probsT[:, r % 2, x, at], v_place(b)[0][:, x, :], start=(x == 0), stop=False)
                        else:
                            ins = nc.tensor.matmul(value[0][at, 0:BW], probsT[0:NT, r % 2, SKT, at], v_new[:, b % 4, :], start=False, stop=True)
                ins.then_inc(valued, 1)
            turn_values(PAIRS - 1)


def mix_out(nc, io, keep):
    mixT, ident = keep["mixT"], keep["ident"]
    ends, slot_ids, slot_w = keep["ends"], keep["slot_ids"], keep["slot_w"]
    moe = keep["moe"]
    with ExitStack() as stack:
        p = Pools(nc, stack)
        w_out = keep["stage"][:, :].rearrange("p (k c) -> p k c", k=KD)
        w_out_rest = keep["w_rest"][:, :, :].rearrange("p s c -> p (s c)").rearrange("p (k c) -> p k c", k=KD)
        w_out_hi = keep["w_out_hi"]
        mix_hi = p.sb("mix_hi", [P, 2, KD, P], F32R)
        mix_rest = p.sb("mix_rest", [P, 2, KD, P], F32R)
        norm_g = p.sb("norm_g2", [P, D])
        x1 = p.sb("x1", [P, 3, D])
        hn = p.sb("hn", [P, 2, D])
        hT = p.sb("hT", [P, 2, KD, P])
        stats = p.sb("stats2", [P, TT, 3])
        eps = p.sb("eps2", [P, 1])
        w_route = p.sb("w_route", [P, KD, NG + NE])
        b_route = p.sb("b_route", [P, NG + NE])
        logits = p.sb("logits", [P, TT, NG + NE])
        g_pad = p.sb("g_pad", [P, TT, 8])
        g_top = p.sb("g_top", [P, TT, 8])
        g_index = p.sb("g_index", [P, TT, 8], U32)
        g_index_f = p.sb("g_index_f", [P, TT])
        g_shift = p.sb("g_shift", [P, TT, NG])
        g_exp = p.sb("g_exp", [P, TT, NG])
        g_sum = p.sb("g_sum", [P, TT])
        g_weight = p.sb("g_weight", [P, TT])
        chosen = p.sb("chosen", [P, TT, NG])
        e_in = p.sb("e_in", [P, TT, NE])
        e_top = p.sb("e_top", [P, TT, 8])
        e_index = p.sb("e_index", [P, TT, 8], U32)
        e_index_f = p.sb("e_index_f", [P, TT, 2])
        e_gap = p.sb("e_gap", [P, TT])
        e_exp = p.sb("e_exp", [P, TT])
        e_norm = p.sb("e_norm", [P, TT])
        iota_f = p.sb("iota_f", [P, NE])
        pick = p.sb("pick", [P, 2, TT, NE])
        picks = p.sb("picks", [P, TT, NE], BF16)
        below = p.sb("below", [P, P], BF16)
        ones = p.sb("ones", [P, P], BF16)
        place = p.sb("place", [P, TT, NE])
        slot_f = p.sb("slot_f", [P, TT, 2])
        blocks = p.sb("blocks", [P, NE])
        blocks_i = p.sb("blocks_i", [P, NE], I32)
        scan = p.sb("scan", [P, 5, NE])
        ends_f = p.sb("ends_f", [P, NE + 1])
        slot_i = p.sb("slot_i", [P, TT, 2], I32)
        block_f = p.sb("block_f", [P, TT, 2])
        row_f = p.sb("row_f", [P, TT, 2])
        weight = p.sb("weight", [P, TT, 2])
        token_no = p.sb("token_no", [P, TT])
        spare_no = p.sb("spare_no", [P, 1])
        iota_p = p.sb("iota_p", [P, P])
        occupied = p.sb("occupied", [P, MAXB])
        row_pick = keep["stage"][:, D * KD // 2:D * KD // 2 + 2 * TT * P].rearrange("p (t k x) -> p t k x", t=TT, k=2)
        block_pick = keep["stage"][:, D * KD // 2 + 2 * TT * P:D * KD // 2 + 2 * TT * (P + 2 * MAXB)].rearrange("p (t k v x) -> p t k v x", t=TT, k=2, v=2)
        zeros = p.sb("zeros", [P, 128])
        y = [[p.ps(f"y{i}{j}", [P, 512]) for j in range(2)] for i in range(2)]
        turn = [p.ps(f"turn3{i}", [P, 512]) for i in range(2)]
        route = p.ps("route", [P, 512])
        count = p.ps("count", [P, 512])

        r_loaded = p.sem("r_loaded")
        x_loaded = [p.sem(f"x1_loaded{i}") for i in range(3)]
        consts = p.sem("consts3")
        mixed = p.sem("mixed3")
        mix_hi_made = p.sem("mix_hi_made")
        mix_rest_made = p.sem("mix_rest_made")
        w_out_hi_made = p.sem("w_out_hi_made")
        w_out_rest_made = p.sem("w_out_rest_made")
        added = p.sem("added")
        squared = p.sem("squared3")
        rooted = p.sem("rooted3")
        normed = p.sem("normed3")
        x_stored = [p.sem(f"x_stored{i}") for i in range(3)]
        h_stored = [p.sem(f"h_stored{i}") for i in range(2)]
        turned = p.sem("turned3")
        hT_act = p.sem("hT_act")
        hT_dve = p.sem("hT_dve")
        routed = p.sem("routed")
        dve_step = p.sem("dve_step3")
        shifted = p.sem("shifted")
        g_exped = p.sem("g_exped")
        gapped = p.sem("gapped")
        e_exped = p.sem("e_exped")
        picked = p.sem("picked")
        counted = p.sem("counted")
        slotted = p.sem("slotted")
        slots_summed = p.sem("slots_summed")
        spare_stored = p.sem("spare_stored")

        SPLIT_AFTER = (4, 5)

        block = stack.enter_context(nc.Block())

        @block.sync
        def _(sp):
            for t in range(3):
                sp.dma_start(x1[:, t, :], io["x"][t]).then_inc(x_loaded[t], 16)
            sp.dma_start(norm_g[:, :], io["norm_ffn"].partition_broadcast(P)).then_inc(r_loaded, 16)
            sp.dma_start(w_route[:, :, 0:NG], io["w_group"]).then_inc(r_loaded, 16)
            sp.dma_start(w_route[:, :, NG:], io["w_router"]).then_inc(r_loaded, 16)
            sp.dma_start(b_route[:, 0:NG], io["b_group"].partition_broadcast(P)).then_inc(r_loaded, 16)
            sp.dma_start(b_route[:, NG:], io["b_router"].partition_broadcast(P)).then_inc(r_loaded, 16)
            moe.load(sp, "gate", 0, 0)
            sp.wait_ge(consts, 9)
            sp.dma_start(io["x1"][TOK:, :].rearrange("p (k f) -> p k f", f=P), zeros[:, :].unsqueeze(1).to_broadcast([P, KD, P])).then_inc(spare_stored, 16)
            sp.dma_start(io["h"][TOK:, :].rearrange("p (k f) -> p k f", f=P), zeros[:, :].unsqueeze(1).to_broadcast([P, KD, P])).then_inc(spare_stored, 16)
            for t in range(TT):
                n = tokens(t)
                sp.wait_ge(added, t + 1)
                sp.dma_start(io["x1"][P * t:P * t + n, :], x1[0:n, t % 3, :]).then_inc(x_stored[t % 3], 16)
                sp.wait_ge(normed, t + 1)
                sp.dma_start(io["h"][P * t:P * t + n, :], hn[0:n, t % 2, :]).then_inc(h_stored[t % 2], 16)
                if t + 3 < TT:
                    sp.wait_ge(x_stored[t % 3], 16 * (t // 3 + 1))
                    sp.dma_start(x1[0:tokens(t + 3), t % 3, :], io["x"][t + 3]).then_inc(x_loaded[t % 3], 16)
            sp.wait_ge(mixed, TT)
            moe.load(sp, "up", 0, 0)
            moe.load(sp, "down", 0, 0)
            for which in moe.names:
                moe.load(sp, which, 1, 1)
            for s in range(3):
                sp.wait_ge(x_stored[s], 16 * (TT // 3))
            sp.wait_ge(h_stored[0], 16 * 5)
            sp.wait_ge(h_stored[1], 16 * 4)
            sp.wait_ge(spare_stored, 32)

        @block.gpsimd
        def _(pool):
            exact = {"allow_small_or_imprecise_dtypes": True}
            nc.gpsimd.memset(eps[:, :], EPS).then_inc(consts, 1)
            pool.wait_ge(consts, 1)
            nc.gpsimd.iota(spare_no[:, :], pattern=[[0, 1]], base=TOK + 1, channel_multiplier=1, **exact).then_inc(consts, 1)
            pool.wait_ge(consts, 2)
            nc.gpsimd.iota(token_no[:, :], pattern=[[P, TT]], base=1, channel_multiplier=1, **exact).then_inc(consts, 1)
            pool.wait_ge(consts, 3)
            nc.gpsimd.memset(token_no[NB * NT:P, QT_N:TT], 0.0).then_inc(consts, 1)
            pool.wait_ge(consts, 4)
            nc.gpsimd.iota(iota_f[:, :], pattern=[[1, NE]], base=0, channel_multiplier=0, **exact).then_inc(consts, 1)
            pool.wait_ge(consts, 5)
            nc.gpsimd.iota(iota_p[:, :], pattern=[[1, P]], base=0, channel_multiplier=0, **exact).then_inc(consts, 1)
            pool.wait_ge(consts, 6)
            nc.gpsimd.memset(ones[:, :], 1.0).then_inc(consts, 1)
            pool.wait_ge(consts, 7)
            nc.gpsimd.affine_select(out=below[:, :], in_=ones[:, :], compare_op=ALU.is_gt, fill=0.0, base=0,
                                    pattern=[[1, P]], channel_multiplier=-1).then_inc(consts, 1)
            pool.wait_ge(consts, 8)
            nc.gpsimd.memset(zeros[:, :], 0.0).then_inc(consts, 1)

        @block.scalar
        def _(act):
            def mix_hi_of(t):
                if t >= 2:
                    act.wait_ge(mixed, t - 1)
                n = tokens(t)
                nc.scalar.activation(mix_hi[:, t % 2, :, 0:n], mixT[:, :, P * t:P * t + n], ACT.Copy).then_inc(mix_hi_made, 1)

            act.wait_ge(consts, 1)
            mix_hi_of(0)
            for k in range(KD):
                nc.scalar.activation(w_out_hi[:, k, :], w_out[:, k, :], ACT.Copy).then_inc(w_out_hi_made, 1)
            mix_hi_of(1)
            for t in range(TT):
                n = tokens(t)
                act.wait_ge(added, t + 1)
                if t >= 2:
                    act.wait_ge(h_stored[t % 2], 16 * (t // 2))
                    act.wait_ge(turned, 2 * t - 2)
                nc.scalar.activation(hn[0:n, t % 2, :], x1[0:n, t % 3, :], ACT.Square, accum_out=stats[0:n, t, 0:1]).then_inc(squared, 1)
                act.wait_ge(squared, t + 1)
                nc.scalar.activation(stats[0:n, t, 1:2], stats[0:n, t, 0:1], ACT.Sqrt, bias=eps[0:n, :], scale=1.0 / D).then_inc(rooted, 1)
                if t + 2 < TT:
                    mix_hi_of(t + 2)
                act.wait_ge(turned, 2 * t + 1)
                if t >= 2:
                    act.wait_ge(routed, t - 1)
                nc.scalar.activation(hT[:, t % 2, 0:4, 0:n], turn[0][:, :].rearrange("p (k c) -> p k c", k=4)[:, :, 0:n], ACT.Copy).then_inc(hT_act, 1)
                if t in SPLIT_AFTER:
                    moe.split_hi(act, "gate", 0, 0, SPLIT_AFTER.index(t))
            act.wait_ge(shifted, 1)
            nc.scalar.activation(g_exp[:, :, :], g_shift[:, :, :], ACT.Exp).then_inc(g_exped, 1)
            act.wait_ge(gapped, 1)
            nc.scalar.activation(e_exp[:, :], e_gap[:, :], ACT.Exp).then_inc(e_exped, 1)
            for c in range(2):
                moe.split_hi(act, "up", 0, 0, c)

        @block.vector
        def _(dve):
            step = stepper(dve, dve_step)
            step(nc.vector.memset(logits[:, :, :], 0.0))
            step(nc.vector.memset(g_pad[:, :, :], MASK))

            def mix_rest_of(t):
                n = tokens(t)
                dve.wait_ge(mix_hi_made, t + 1)
                nc.vector.tensor_tensor(mix_rest[:, t % 2, :, 0:n], mixT[:, :, P * t:P * t + n], mix_hi[:, t % 2, :, 0:n].bitcast(F32),
                                        ALU.subtract).then_inc(mix_rest_made, 1)

            mix_rest_of(0)
            for k in range(KD):
                dve.wait_ge(w_out_hi_made, k + 1)
                nc.vector.tensor_tensor(w_out_rest[:, k, :], w_out[:, k, :], w_out_hi[:, k, :].bitcast(F32), ALU.subtract).then_inc(w_out_rest_made, 1)
            mix_rest_of(1)
            dve.wait_ge(r_loaded, 80)

            def after_route(t):
                n = tokens(t)
                dve.wait_ge(routed, t + 1)
                step(nc.vector.tensor_tensor(logits[0:n, t, :], route[0:n, 32 * t:32 * t + NG + NE], b_route[0:n, :], ALU.add))

            for t in range(TT):
                n = tokens(t)
                dve.wait_ge(x_loaded[t % 3], 16 * (t // 3 + 1))
                dve.wait_ge(mixed, t + 1)
                for j in range(2):
                    xs = x1[0:n, t % 3, 512 * j:512 * j + 512]
                    ins = nc.vector.tensor_tensor(xs, y[t % 2][j][0:n, :], xs, ALU.add)
                ins.then_inc(added, 1)
                dve.wait_ge(rooted, t + 1)
                step(nc.vector.reciprocal(stats[0:n, t, 2:3], stats[0:n, t, 1:2]))
                if t >= 2:
                    dve.wait_ge(h_stored[t % 2], 16 * (t // 2))
                    dve.wait_ge(turned, 2 * t - 2)
                nc.vector.scalar_tensor_tensor(out=hn[0:n, t % 2, :], in0=x1[0:n, t % 3, :], scalar=stats[0:n, t, 2:3],
                                               in1=norm_g[0:n, :], op0=ALU.mult, op1=ALU.mult).then_inc(normed, 1)
                if t + 2 < TT:
                    mix_rest_of(t + 2)
                if t:
                    after_route(t - 1)
                dve.wait_ge(turned, 2 * t + 2)
                if t >= 2:
                    dve.wait_ge(routed, t - 1)
                nc.vector.tensor_copy(hT[:, t % 2, 4:8, 0:n], turn[1][:, :].rearrange("p (k c) -> p k c", k=4)[:, :, 0:n]).then_inc(hT_dve, 1)
                if t in SPLIT_AFTER:
                    moe.split_rest(dve, "gate", 0, 0, SPLIT_AFTER.index(t))
            after_route(TT - 1)

            step(nc.vector.tensor_copy(g_pad[:, :, 0:NG], logits[:, :, 0:NG]))
            for t in range(TT):
                ins = nc.vector.max(g_top[:, t, :], g_pad[:, t, :])
            step(ins)
            for t in range(TT):
                ins = nc.vector.max_index(g_index[:, t, :], g_top[:, t, :], g_pad[:, t, :])
            step(ins)
            nc.vector.tensor_tensor(g_shift[:, :, :], logits[:, :, 0:NG], g_top[:, :, 0:1].to_broadcast([P, TT, NG]), ALU.subtract).then_inc(shifted, 1)
            step(nc.vector.tensor_copy(g_index_f[:, :], g_index[:, :, 0]))
            dve.wait_ge(consts, 8)
            step(nc.vector.tensor_tensor(chosen[:, :, :], iota_f[:, 0:NG].unsqueeze(1).to_broadcast([P, TT, NG]),
                                         g_index_f[:, :].unsqueeze(2).to_broadcast([P, TT, NG]), ALU.is_equal))
            step(nc.vector.tensor_scalar(chosen[:, :, :], chosen[:, :, :], -1.0, -MASK, ALU.add, ALU.mult))
            for g in range(NG):
                ins = nc.vector.tensor_tensor(e_in[:, :, EPG * g:EPG * g + EPG], logits[:, :, NG + EPG * g:NG + EPG * g + EPG],
                                              chosen[:, :, g:g + 1].to_broadcast([P, TT, EPG]), ALU.add)
            step(ins)
            for t in range(TT):
                ins = nc.vector.max(e_top[:, t, :], e_in[:, t, :])
            step(ins)
            for t in range(TT):
                ins = nc.vector.max_index(e_index[:, t, :], e_top[:, t, :], e_in[:, t, :])
            nc.vector.tensor_tensor(e_gap[:, :], e_top[:, :, 1], e_top[:, :, 0], ALU.subtract).then_inc(gapped, 1)
            step(ins)
            step(nc.vector.tensor_copy(e_index_f[:, :, :], e_index[:, :, 0:2]))
            for k in range(2):
                ins = nc.vector.tensor_tensor(pick[:, k, :, :], iota_f[:, :].unsqueeze(1).to_broadcast([P, TT, NE]),
                                              e_index_f[:, :, k:k + 1].to_broadcast([P, TT, NE]), ALU.is_equal)
            step(ins)
            step(nc.vector.memset(pick[NB * NT:P, :, QT_N, :], 0.0))
            nc.vector.tensor_tensor(picks[:, :, :], pick[:, 0, :, :], pick[:, 1, :, :], ALU.add).then_inc(picked, 1)
            dve.wait_ge(g_exped, 1)
            step(nc.vector.tensor_reduce(g_sum[:, :], g_exp[:, :, :], AX.X, ALU.add))
            step(nc.vector.reciprocal(g_weight[:, :], g_sum[:, :]))
            dve.wait_ge(e_exped, 1)
            step(nc.vector.tensor_scalar(e_norm[:, :], e_exp[:, :], 1.0, None, ALU.add))
            step(nc.vector.reciprocal(e_norm[:, :], e_norm[:, :]))
            step(nc.vector.tensor_tensor(weight[:, :, 0], e_norm[:, :], g_weight[:, :], ALU.mult))
            step(nc.vector.tensor_tensor(weight[:, :, 1], weight[:, :, 0], e_exp[:, :], ALU.mult))
            step(nc.vector.memset(weight[NB * NT:P, QT_N, :], 0.0))
            dve.wait_ge(counted, 1)
            step(nc.vector.tensor_scalar(blocks[:, :], count[:, 256:256 + NE], float(P - 1), None, ALU.add))
            step(nc.vector.tensor_copy(blocks_i[:, :], blocks[:, :]))
            step(nc.vector.tensor_scalar(blocks_i[:, :], blocks_i[:, :], 7, None, ALU.arith_shift_right))
            step(nc.vector.tensor_copy(blocks[:, :], blocks_i[:, :]))
            step(nc.vector.tensor_scalar(scan[:, 0, :], blocks[:, :], 1.0, None, ALU.max))
            for i in range(4):
                d = 1 << i
                nc.vector.tensor_copy(scan[:, i + 1, 0:d], scan[:, i, 0:d])
                step(nc.vector.tensor_tensor(scan[:, i + 1, d:NE], scan[:, i, d:NE], scan[:, i, 0:NE - d], ALU.add))
            step(nc.vector.memset(ends_f[:, 0:1], 0.0))
            step(nc.vector.tensor_copy(ends_f[:, 1:NE + 1], scan[:, 4, :]))
            step(nc.vector.tensor_copy(ends[:, :], ends_f[:, :]))
            step(nc.vector.tensor_scalar(blocks[:, :], ends_f[:, 0:NE], float(P), None, ALU.mult))
            step(nc.vector.tensor_tensor(place[:, :, :], count[:, 0:TT * NE].rearrange("p (t e) -> p t e", e=NE),
                                         blocks[:, :].unsqueeze(1).to_broadcast([P, TT, NE]), ALU.add))
            for k in range(2):
                step(nc.vector.tensor_tensor(pick[:, k, :, :], pick[:, k, :, :], place[:, :, :], ALU.mult))
                step(nc.vector.tensor_reduce(slot_f[:, :, k], pick[:, k, :, :], AX.X, ALU.add))
            step(nc.vector.tensor_copy(slot_i[:, :, :], slot_f[:, :, :]))
            step(nc.vector.tensor_scalar(slot_i[:, :, :], slot_i[:, :, :], 7, None, ALU.arith_shift_right))
            step(nc.vector.tensor_copy(block_f[:, :, :], slot_i[:, :, :]))
            step(nc.vector.scalar_tensor_tensor(out=row_f[:, :, :], in0=block_f[:, :, :], scalar=-float(P), in1=slot_f[:, :, :],
                                                op0=ALU.mult, op1=ALU.add))
            all_slots = [P, TT, 2, MAXB]
            step(nc.vector.tensor_tensor(block_pick[:, :, :, 0, :], iota_p[:, 0:MAXB].unsqueeze(1).unsqueeze(1).to_broadcast(all_slots),
                                         block_f[:, :, :].unsqueeze(3).to_broadcast(all_slots), ALU.is_equal))
            step(nc.vector.tensor_tensor(block_pick[:, :, :, 1, :], block_pick[:, :, :, 0, :],
                                         weight[:, :, :].unsqueeze(3).to_broadcast(all_slots), ALU.mult))
            step(nc.vector.tensor_tensor(block_pick[:, :, :, 0, :], block_pick[:, :, :, 0, :],
                                         token_no[:, :].unsqueeze(2).unsqueeze(2).to_broadcast(all_slots), ALU.mult))
            for t in range(0, TT, 3):
                part = [P, 3, 2, P]
                nc.vector.tensor_tensor(row_pick[:, t:t + 3, :, :], iota_p[:, :].unsqueeze(1).unsqueeze(1).to_broadcast(part),
                                        row_f[:, t:t + 3, :].unsqueeze(3).to_broadcast(part), ALU.is_equal).then_inc(slotted, 1)
            for c in range(2):
                moe.split_rest(dve, "up", 0, 0, c)
            dve.wait_ge(slots_summed, 1)
            numbers = y[0][0][:, 0:MAXB]
            step(nc.vector.tensor_copy(slot_w[:, :], y[0][0][:, MAXB:2 * MAXB]))
            step(nc.vector.tensor_scalar(occupied[:, :], numbers, 1.0, None, ALU.min))
            step(nc.vector.tensor_scalar(occupied[:, :], occupied[:, :], -1.0, 1.0, ALU.mult, ALU.add))
            step(nc.vector.scalar_tensor_tensor(out=occupied[:, :], in0=occupied[:, :], scalar=spare_no[:, 0:1], in1=numbers,
                                                op0=ALU.mult, op1=ALU.add))
            step(nc.vector.memset(slot_ids[:, MAXB:], 0))
            step(nc.vector.tensor_scalar(slot_ids[:, 0:MAXB], occupied[:, :], -1.0, None, ALU.add))

        @block.tensor
        def _(pe):
            def mix(t):
                n = tokens(t)
                if t >= 2:
                    pe.wait_ge(added, t - 1)
                pe.wait_ge(mix_rest_made, t + 1)
                for k in range(KD):
                    if t == 0:
                        pe.wait_ge(w_out_rest_made, k + 1)
                    for x, (rows, wt) in enumerate(((mix_hi, w_out_hi), (mix_hi, w_out_rest), (mix_rest, w_out_hi))):
                        for j in range(2):
                            ins = nc.tensor.matmul(y[t % 2][j][0:n, :], rows[:, t % 2, k, 0:n], wt[:, k, 512 * j:512 * j + 512],
                                                   start=(k == 0 and x == 0), stop=(k == KD - 1 and x == 2))
                ins.then_inc(mixed, 1)

            def turn_h(t):
                n = tokens(t)
                pe.wait_ge(normed, t + 1)
                if t:
                    pe.wait_ge(hT_act, t)
                    pe.wait_ge(hT_dve, t)
                for k in range(KD):
                    ins = nc.tensor.transpose(turn[k // 4][:, P * (k % 4):P * (k % 4) + n], hn[0:n, t % 2, P * k:P * k + P], ident[0:n, 0:n])
                    if k == 3:
                        ins.then_inc(turned, 1)
                ins.then_inc(turned, 1)

            def router(t):
                n = tokens(t)
                pe.wait_ge(hT_act, t + 1)
                pe.wait_ge(hT_dve, t + 1)
                if t:
                    pe.wait_ge(dve_step, 3 + 2 * t)
                for k in range(KD):
                    ins = nc.tensor.matmul(route[0:n, 32 * t:32 * t + NG + NE], hT[:, t % 2, k, 0:n], w_route[:, k, :],
                                           start=(k == 0), stop=(k == KD - 1))
                ins.then_inc(routed, 1)

            mix(0)
            mix(1)
            pe.wait_ge(r_loaded, 80)
            for t in range(TT):
                turn_h(t)
                if t + 2 < TT:
                    mix(t + 2)
                router(t)
            pe.wait_ge(consts, 8)
            pe.wait_ge(picked, 1)
            flat = picks[:, :, :].rearrange("p t e -> p (t e)")
            for t in range(TT):
                nc.tensor.matmul(count[:, 256:256 + NE], ones[:, :], flat[:, NE * t:NE * t + NE], start=(t == 0), stop=(t == TT - 1))
            nc.tensor.matmul(count[:, 0:TT * NE], below[:, :], flat, start=True, stop=False)
            for d in range(1, TT):
                ins = nc.tensor.matmul(count[:, NE * d:TT * NE], ones[:, :], flat[:, 0:NE * (TT - d)], start=False, stop=(d == TT - 1))
            ins.then_inc(counted, 1)
            for t in range(TT):
                if t % 3 == 0:
                    pe.wait_ge(slotted, t // 3 + 1)
                for k in range(2):
                    for rows in (slice(0, P // 2), slice(P // 2, P)):
                        ins = nc.tensor.matmul(y[0][0][rows, 0:2 * MAXB], row_pick[:, t, k, rows],
                                               block_pick[:, t, k, :, :].rearrange("p v x -> p (v x)"),
                                               start=(t == 0 and k == 0), stop=(t == TT - 1 and k == 1))
            ins.then_inc(slots_summed, 1)


class ExpertWeights:

    names = ("gate", "up", "down")
    steps = [(which, c) for which in names for c in range(2)]

    def __init__(self, nc, io, p):
        self.nc, self.io = nc, io
        tiles = {"gate": KD, "up": KD, "down": FT}
        self.shape = {n: [P, tiles[n], KD * FF // tiles[n]] for n in self.names}
        self.half_tiles = {n: tiles[n] // 2 for n in self.names}
        self.raw, self.rest, self.hi = ({n: [None, None] for n in self.names} for _ in range(3))
        self.loaded = {n: [p.sem(f"{n}_loaded{i}") for i in range(2)] for n in self.names}
        self.hi_made, self.rest_made = p.sem("weights_hi"), p.sem("weights_rest")

    def place(self, p, half):
        with ExitStack() as freed:
            q = Pools(self.nc, freed)
            self.raw["gate"][half] = q.sb(f"w_gate{half}", self.shape["gate"])
            if half == 0:
                with ExitStack() as before:
                    self.w_out_hi = Pools(self.nc, before).sb("w_out_hi", [P, KD, D], F32R)
            for n in ("up", "down"):
                self.raw[n][half] = q.sb(f"w_{n}{half}", self.shape[n])
        for n in self.names:
            self.rest[n][half] = p.sb(f"{n}_rest{half}", self.shape[n], F32R)

    def place_hi(self, p, which, half):
        self.hi[which][half] = p.sb(f"{which}_hi{half}", self.shape[which], F32R)

    def load(self, sp, which, e, half):
        src = self.io["w_" + which]
        src = src[e:e + 1] if type(e) is int else src[bass.ds(e, 1)]
        sp.dma_start(self.raw[which][half][:, :, :], src.rearrange("o (k p) f -> p (o k) f", p=P)).then_inc(self.loaded[which][half], 16)

    def rows(self, which, c):
        return slice(self.half_tiles[which] * c, self.half_tiles[which] * (c + 1))

    def split_hi(self, act, which, pair, half, c):
        if c == 0:
            act.wait_ge(self.loaded[which][half], 16 * pair + 16)
        k = self.rows(which, c)
        self.nc.scalar.activation(self.hi[which][half][:, k, :], self.raw[which][half][:, k, :], ACT.Copy).then_inc(self.hi_made, 1)

    def split_rest(self, dve, which, pair, half, c):
        dve.wait_ge(self.hi_made, 12 * pair + 6 * half + self.steps.index((which, c)) + 1)
        k = self.rows(which, c)
        self.nc.vector.tensor_tensor(self.rest[which][half][:, k, :], self.raw[which][half][:, k, :],
                                     self.hi[which][half][:, k, :].bitcast(F32), ALU.subtract).then_inc(self.rest_made, 1)


def experts(nc, io, keep):
    ident, ends, slot_ids, slot_w = keep["ident"], keep["ends"], keep["slot_ids"], keep["slot_w"]
    moe = keep["moe"]
    FIRST = 0
    with ExitStack() as stack:
        p = Pools(nc, stack)
        landing = p.sb("landing", [P, D])
        rows = p.sb("rows", [P, D])
        row_id = p.sb("row_id", [P, 1], I32)
        out_id = p.sb("out_id", [P, 1], I32)
        rowsT_hi = p.sb("rowsT_hi", [P, KD, P], F32R)
        rowsT_lo = p.sb("rowsT_lo", [P, KD, P], F32R)
        moe.place_hi(p, "down", 0)
        moe.hi["down"][1] = moe.hi["down"][0]
        moe.place_hi(p, "up", 1)
        silu = keep["silu"]
        hid = p.sb("hid", [P, FF])
        hidT_hi = p.sb("hidT_hi", [P, FT, P], F32R)
        hidT_lo = p.sb("hidT_lo", [P, FT, P], F32R)
        y_out = p.sb("y_out", [P, D])
        turn = [p.ps(f"turn5{i}", [P, 512]) for i in range(2)]
        gate = p.ps("gate", [P, FF])
        up = p.ps("up", [P, FF])
        hturn = p.ps("hturn", [P, 512])
        y = [p.ps(f"y5{i}", [P, 512]) for i in range(2)]

        rows_ready = p.sem("rows_ready")
        gathered = p.sem("gathered")
        gather_id = p.sem("gather_id")
        id_copied = p.sem("id_copied")
        turned = p.sem("turned5")
        rowsT_hi_made = p.sem("rowsT_hi_made")
        rowsT_lo_made = p.sem("rowsT_lo_made")
        gated = p.sem("gated")
        silued = p.sem("silued")
        upped = p.sem("upped")
        hid_ready = p.sem("hid_ready")
        hid_turned = p.sem("hid_turned")
        hidT_hi_made = p.sem("hidT_hi_made")
        hidT_lo_made = p.sem("hidT_lo_made")
        downed = p.sem("downed")
        y_act = p.sem("y_act")
        y_dve = p.sem("y_dve")
        y_stored = p.sem("y_stored")
        gather_begun = p.sem("gather_begun")
        add_begun = p.sem("add_begun")
        expert_begun = p.sem("expert_begun")

        def expert_loops(eng, block_step):
            def one(pair, half, last):
                e = 2 * pair + half if pair is not FIRST or half else FIRST
                here = (pair, half)
                following = None if last else ((pair, 1) if half == 0 else (pair + 1, 0))
                first = eng.value_load(ends[0:1, bass.ds(e, 1)], min_val=0, max_val=MAXB - 1)
                after = eng.value_load(ends[0:1, bass.ds(e + 1, 1)], min_val=1, max_val=MAXB)
                block_step(FIRST if e is FIRST else first, here, following)
                with eng.If(first + 1 < after):
                    with eng.Fori(first + 1, after) as b:
                        block_step(b)

            one(0, 0, False)
            one(0, 1, False)
            with eng.Fori(1, NE // 2 - 1) as pair:
                one(pair, 0, False)
                one(pair, 1, False)
            one(NE // 2 - 1, 0, False)
            one(NE // 2 - 1, 1, True)

        block = stack.enter_context(nc.Block())

        @block.sync
        def _(sp):
            with sp.Fori(1, NE // 2) as pair:
                for half in range(2):
                    end = sp.value_load(ends[0:1, bass.ds(2 * pair + half - 1, 1)], min_val=1, max_val=MAXB)
                    sp.wait_ge(gated, end)
                    moe.load(sp, "gate", 2 * pair + half, half)
                    sp.wait_ge(upped, end)
                    moe.load(sp, "up", 2 * pair + half, half)
                    sp.wait_ge(downed, end)
                    moe.load(sp, "down", 2 * pair + half, half)

        @block.gpsimd
        def _(pool):
            def gather(b):
                if b is not FIRST:
                    pool.wait_ge(rows_ready, b)
                nc.gpsimd.tensor_copy(row_id[:, :], slot_ids[:, bass.ds(b, 1)]).then_inc(gather_id, 1)
                pool.wait_ge(gather_id, b + 1)
                nc.gpsimd.sem_inc(gather_begun, 1)
                nc.gpsimd.indirect_dma_start(out=landing[:, :], out_offset=None, in_=io["h"],
                                             in_offset=bass.IndirectOffsetOnAxis(ap=row_id[:, :], axis=0)).then_inc(gathered, 16)

            gather(FIRST)
            gather(1)
            gather(2)
            total = pool.value_load(ends[0:1, NE:NE + 1], min_val=NE, max_val=MAXB)

            def block_step(b):
                if b is not FIRST:
                    pool.wait_ge(y_stored, 16 * b)
                nc.gpsimd.tensor_copy(out_id[:, :], slot_ids[:, bass.ds(b, 1)]).then_inc(id_copied, 1)
                pool.wait_ge(id_copied, b + 1)
                pool.wait_ge(y_act, b + 1)
                pool.wait_ge(y_dve, b + 1)
                nc.gpsimd.sem_inc(add_begun, 1)
                nc.gpsimd.indirect_dma_start(out=io["x1"], out_offset=bass.IndirectOffsetOnAxis(ap=out_id[:, :], axis=0),
                                             in_=y_out[:, :], in_offset=None, compute_op=ALU.add).then_inc(y_stored, 16)
                gather(b + 3)

            block_step(FIRST)
            with pool.Fori(1, total) as b:
                block_step(b)
            pool.wait_ge(y_stored, 16 * total)
            pool.wait_ge(gathered, 16 * total + 48)

        @block.scalar
        def _(act):
            def rows_hi(b, c):
                act.wait_ge(turned, 2 * b + c + 1)
                nc.scalar.activation(rowsT_hi[:, 4 * c:4 * c + 4, :], turn[c][:, :].rearrange("p (k c) -> p k c", k=4), ACT.Copy).then_inc(rowsT_hi_made, 1)

            def block_step(b, here=None, following=None):
                if here:
                    if b is not FIRST:
                        act.wait_ge(downed, b)
                    moe.split_hi(act, "down", *here, 0)
                    moe.split_hi(act, "down", *here, 1)
                if following:
                    moe.split_hi(act, "gate", *following, 0)
                act.wait_ge(gated, b + 1)
                nc.scalar.activation(silu[:, :], gate[:, :], ACT.Silu).then_inc(silued, 1)
                if following:
                    moe.split_hi(act, "gate", *following, 1)
                    moe.split_hi(act, "up", *following, 0)
                rows_hi(b + 1, 0)
                act.wait_ge(hid_turned, b + 1)
                nc.scalar.activation(hidT_hi[:, :, :], hturn[:, :].rearrange("p (k c) -> p k c", k=FT), ACT.Copy).then_inc(hidT_hi_made, 1)
                rows_hi(b + 1, 1)
                if following:
                    moe.split_hi(act, "up", *following, 1)
                act.wait_ge(downed, b + 1)
                if b is not FIRST:
                    act.wait_ge(y_stored, 16 * b)
                nc.scalar.activation(y_out[:, 0:512], y[0][:, :], ACT.Copy, scale=slot_w[:, bass.ds(b, 1)]).then_inc(y_act, 1)

            rows_hi(FIRST, 0)
            rows_hi(FIRST, 1)
            expert_loops(act, block_step)

        @block.vector
        def _(dve):
            def fetch(b):
                if b is not FIRST:
                    dve.wait_ge(turned, 2 * b)
                dve.wait_ge(gathered, 16 * b + 16)
                nc.vector.tensor_copy(rows[:, :], landing[:, :]).then_inc(rows_ready, 1)

            def rows_lo(b, c):
                dve.wait_ge(rowsT_hi_made, 2 * b + c + 1)
                hi = rowsT_hi[:, 4 * c:4 * c + 4, :]
                nc.vector.tensor_tensor(rowsT_lo[:, 4 * c:4 * c + 4, :], turn[c][:, :].rearrange("p (k c) -> p k c", k=4),
                                        hi.bitcast(F32), ALU.subtract).then_inc(rowsT_lo_made, 1)

            def block_step(b, here=None, following=None):
                if here:
                    moe.split_rest(dve, "down", *here, 0)
                    moe.split_rest(dve, "down", *here, 1)
                if following:
                    moe.split_rest(dve, "gate", *following, 0)
                dve.wait_ge(silued, b + 1)
                dve.wait_ge(upped, b + 1)
                nc.vector.tensor_tensor(hid[:, :], up[:, :], silu[:, :], ALU.mult).then_inc(hid_ready, 1)
                rows_lo(b + 1, 0)
                dve.wait_ge(hidT_hi_made, b + 1)
                nc.vector.tensor_tensor(hidT_lo[:, :, :], hturn[:, :].rearrange("p (k c) -> p k c", k=FT),
                                        hidT_hi[:, :, :].bitcast(F32), ALU.subtract).then_inc(hidT_lo_made, 1)
                rows_lo(b + 1, 1)
                if following:
                    moe.split_rest(dve, "gate", *following, 1)
                    moe.split_rest(dve, "up", *following, 0)
                    moe.split_rest(dve, "up", *following, 1)
                dve.wait_ge(downed, b + 1)
                if b is not FIRST:
                    dve.wait_ge(y_stored, 16 * b)
                nc.vector.tensor_scalar(y_out[:, 512:D], y[1][:, :], slot_w[:, bass.ds(b, 1)], None, ALU.mult).then_inc(y_dve, 1)
                fetch(b + 2)

            fetch(FIRST)
            rows_lo(FIRST, 0)
            rows_lo(FIRST, 1)
            fetch(1)
            expert_loops(dve, block_step)

        @block.tensor
        def _(pe):
            def turn_rows(c):
                for k in range(4):
                    ins = nc.tensor.transpose(turn[c][:, P * k:P * k + P], rows[:, P * (4 * c + k):P * (4 * c + k + 1)], ident[:, :])
                ins.then_inc(turned, 1)

            def project(out, b, hi, rest, made):
                pe.wait_ge(rowsT_hi_made, 2 * b + 2)
                pe.wait_ge(moe.rest_made, made)
                for k in range(KD):
                    nc.tensor.matmul(out[:, :], rowsT_hi[:, k, :], hi[:, k, :], start=(k == 0), stop=False)
                    nc.tensor.matmul(out[:, :], rowsT_hi[:, k, :], rest[:, k, :], start=False, stop=False)
                pe.wait_ge(rowsT_lo_made, 2 * b + 2)
                for k in range(KD):
                    ins = nc.tensor.matmul(out[:, :], rowsT_lo[:, k, :], hi[:, k, :], start=False, stop=(k == KD - 1))
                return ins

            pe.wait_ge(rows_ready, 1)
            turn_rows(0)
            turn_rows(1)
            with pe.Fori(0, NE // 2) as pair:
                for half in range(2):
                    first = pe.value_load(ends[0:1, bass.ds(2 * pair + half, 1)], min_val=0, max_val=MAXB - 1)
                    after = pe.value_load(ends[0:1, bass.ds(2 * pair + half + 1, 1)], min_val=1, max_val=MAXB)
                    done = 12 * pair + 6 * half
                    pe.wait_ge(moe.rest_made, done + 2)
                    nc.tensor.sem_inc(expert_begun, 1)
                    with pe.Fori(first, after) as b:
                        project(gate, b, moe.hi["gate"][half], moe.rest["gate"][half], done + 2).then_inc(gated, 1)
                        project(up, b, moe.hi["up"][half], moe.rest["up"][half], done + 4).then_inc(upped, 1)
                        pe.wait_ge(rows_ready, b + 2)
                        turn_rows(0)
                        pe.wait_ge(hid_ready, b + 1)
                        for k in range(FT):
                            ins = nc.tensor.transpose(hturn[:, P * k:P * k + P], hid[:, P * k:P * k + P], ident[:, :])
                        ins.then_inc(hid_turned, 1)
                        turn_rows(1)
                        pe.wait_ge(hidT_hi_made, b + 1)
                        pe.wait_ge(moe.rest_made, done + 6)
                        for k in range(FT):
                            for j in range(2):
                                cols = slice(512 * j, 512 * j + 512)
                                nc.tensor.matmul(y[j][:, :], hidT_hi[:, k, :], moe.hi["down"][half][:, k, cols], start=(k == 0), stop=False)
                                nc.tensor.matmul(y[j][:, :], hidT_hi[:, k, :], moe.rest["down"][half][:, k, cols], start=False, stop=False)
                        pe.wait_ge(hidT_lo_made, b + 1)
                        for k in range(FT):
                            for j in range(2):
                                ins = nc.tensor.matmul(y[j][:, :], hidT_lo[:, k, :], moe.hi["down"][half][:, k, 512 * j:512 * j + 512],
                                                       start=False, stop=(k == FT - 1))
                        ins.then_inc(downed, 1)


def finish(nc, io, keep):
    with ExitStack() as stack:
        p = Pools(nc, stack)
        x1 = p.sb("x1f", [P, TT, D])
        squares = p.sb("squaresf", [P, D])
        norm_g = p.sb("norm_gf", [P, D])
        stats = p.sb("statsf", [P, TT, 3])
        eps = p.sb("epsf", [P, 1])
        eps_set = p.sem("eps_setf")
        g_loaded = p.sem("g_loadedf")
        x_loaded = [p.sem(f"x_loadedf{t}") for t in range(TT)]
        y_stored = p.sem("y_storedf")
        squared = p.sem("squaredf")
        rooted = p.sem("rootedf")
        dve_step = p.sem("dve_stepf")
        scaled = p.sem("scaledf")
        block = stack.enter_context(nc.Block())

        @block.sync
        def _(sp):
            for t in range(TT):
                n = tokens(t)
                sp.dma_start(x1[0:n, t, :], io["x1"][P * t:P * t + n, :]).then_inc(x_loaded[t], 16)
                if t == 0:
                    sp.dma_start(norm_g[:, :], io["norm_final"].partition_broadcast(P)).then_inc(g_loaded, 16)
            for t in range(TT):
                sp.wait_ge(scaled, t + 1)
                sp.dma_start(io["y"][t], x1[0:tokens(t), t, :]).then_inc(y_stored, 16)
            sp.wait_ge(y_stored, 16 * TT)

        @block.scalar
        def _(act):
            act.wait_ge(eps_set, 1)
            for t in range(TT):
                n = tokens(t)
                act.wait_ge(x_loaded[t], 16)
                if t:
                    act.wait_ge(squared, t)
                nc.scalar.activation(squares[0:n, :], x1[0:n, t, :], ACT.Square, accum_out=stats[0:n, t, 0:1]).then_inc(squared, 1)
                act.wait_ge(squared, t + 1)
                nc.scalar.activation(stats[0:n, t, 1:2], stats[0:n, t, 0:1], ACT.Sqrt, bias=eps[0:n, :], scale=1.0 / D).then_inc(rooted, 1)

        @block.vector
        def _(dve):
            step = stepper(dve, dve_step)
            nc.vector.memset(eps[:, :], EPS).then_inc(eps_set, 1)
            dve.wait_ge(g_loaded, 16)

            for t in range(TT):
                n = tokens(t)
                x = x1[0:n, t, :]
                dve.wait_ge(rooted, t + 1)
                step(nc.vector.reciprocal(stats[0:n, t, 2:3], stats[0:n, t, 1:2]))
                nc.vector.scalar_tensor_tensor(out=x, in0=x, scalar=stats[0:n, t, 2:3], in1=norm_g[0:n, :],
                                               op0=ALU.mult, op1=ALU.mult).then_inc(scaled, 1)


def constants():
    return {"bias_rows": bias_rows(), "sink_pick": np.tile(np.eye(A_H, dtype=np.float32), (1, P // A_H))}


def program(nc, ins, outs, upto=9):
    io = {k: ins[k] for k in ("norm_mix", "norm_ffn", "norm_final", "bias_rows")}
    xp = ins["x_prompt"].rearrange("o (t p) d -> (o t) p d", p=P)
    xs = ins["x_sample"].rearrange("b t d -> (b t) d")
    io["x"] = [xp[t] for t in range(QT_N)] + [xs]
    io["table"] = ins["rel_bias_table"]
    io["w_in"] = ins["w_in"].rearrange("l (k p) c -> p (l k) c", p=P)
    io["state_conv"] = ins["state_conv"].rearrange("l b s c -> (l b s) c")
    io["conv_w"] = ins["conv_w"].rearrange("l s c -> (l s) c")
    io["norm_mix"] = ins["norm_mix"].rearrange("l d -> (l d)")
    io["a_k_prompt"] = outs["a_k_prompt"].rearrange("l b t h d -> (l b t) (h d)")
    io["a_v_prompt"] = outs["a_v_prompt"].rearrange("l b t h d -> (l b t) (h d)")
    for n in "kv":
        rows = outs[f"b_{n}_prompt"].rearrange("l b (t p) h d -> (l b t) p (h d)", p=P)
        io[f"b_{n}_prompt"] = [rows[t] for t in range(QT_N)]
        io[f"a_{n}_sample"] = outs[f"a_{n}_sample"].rearrange("l b t h d -> (l b t) (h d)")
        io[f"b_{n}_sample"] = outs[f"b_{n}_sample"].rearrange("l b t h d -> (l b t) (h d)")
    io["conv_prompt"] = outs["conv_prompt"].rearrange("l b s c -> (l b s) c")
    io["conv_sample"] = outs["conv_sample"].rearrange("l b s c -> (l b s) c")
    bias = nc.dram_tensor("bias_scratch", (A_H + B_H, P * GW + P), F32, kind="Internal").ap()
    io["bias"] = [bias[h, 0:P * GW].rearrange("(p y) -> p y", p=P) for h in range(A_H + B_H)]
    io["bias_skewed"] = bias[:, P + 7:P + 7 + P * GPITCH].rearrange("h (p y) -> p h y", p=P)
    io["bias_row"] = bias
    io["sinks"] = ins["attn_sinks"].rearrange("l h -> (l h)")
    io["sink_pick"] = ins["sink_pick"]
    for n in "kv":
        io[f"cache_a_{n}"] = ins[f"cache_a_{n}"].rearrange("l b t h d -> t (l b) (h d)")
        rows = ins[f"cache_b_{n}"].rearrange("l b t h d -> (l b) t (h d)")
        io[f"cache_b_{n}_far"] = [[rows[b, 256 * k:256 * k + 256].rearrange("(a r) c -> a r c", r=16)[:, 0:NT, :]
                                   for k in range(2)] for b in range(NB)]
        io[f"cache_b_{n}_near"] = [rows[b, SEQ // 2:SEQ].rearrange("(k p) c -> p k c", p=P) for b in range(NB)]
    io["a_v_new"] = outs["a_v_sample"].rearrange("l b t h d -> t (l b) (h d)")
    vn = outs["b_v_sample"].rearrange("l b t h d -> (l b) t (h d)")
    io["b_v_new"] = [vn[b] for b in range(NB)]
    io["w_out"] = ins["w_out"].rearrange("l r c -> (l r) c")
    for n in ("norm_ffn", "b_group", "b_router"):
        io[n] = ins[n].rearrange("l d -> (l d)")
    for n in ("w_group", "w_router"):
        io[n] = ins[n].rearrange("l (k p) c -> p (l k) c", p=P)
    for n in ("w_gate", "w_up", "w_down"):
        io[n] = ins[n].rearrange("l e r c -> (l e) r c")
    yp = outs["y_prompt"].rearrange("o (t p) d -> (o t) p d", p=P)
    io["y"] = [yp[t] for t in range(QT_N)] + [outs["y_sample"].rearrange("b t d -> (b t) d")]
    io["x1"] = nc.dram_tensor("x1_rows", (TOK + P, D), F32, kind="Internal").ap()
    io["h"] = nc.dram_tensor("h_rows", (TOK + P, D), F32, kind="Internal").ap()
    with ExitStack() as stack:
        p = Pools(nc, stack)
        keep = {"ident": p.sb("ident", [P, P]), 
                "ends": p.sb("ends", [P, NE + 1], I32), "slot_ids": p.sb("slot_ids", [P, MAXB + 3], I32),
                "slot_w": p.sb("slot_w", [P, MAXB])}
        moe = keep["moe"] = ExpertWeights(nc, io, p)
        with ExitStack() as later:
            q = Pools(nc, later)
            moe.place(q, 1)
            moe.place_hi(q, "gate", 1)
            keep["silu"] = q.sb("silu", [P, FF])
        keep["mixT"] = p.sb("mixT", [P, 8, TOK])
        with ExitStack() as before:
            keep["w_rest"] = Pools(nc, before).sb("w_rest", [P, 2, KD * VW], F32R)
        keep["stage"] = p.sb("stage", [P, KD * D])
        with ExitStack() as heads:
            r = Pools(nc, heads)
            keep["KT"] = r.sb("KT", [P, 4, TOK])
            keep["V"] = r.sb("V", [P, TT, VW])
            project_in(nc, io, keep)
            if upto >= 2:
                attend(nc, io, keep)
        moe.place(p, 0)
        keep["w_out_hi"] = moe.w_out_hi
        moe.place_hi(p, "gate", 0)
        moe.place_hi(p, "up", 0)
        if upto >= 3:
            mix_out(nc, io, keep)
        if upto >= 5:
            experts(nc, io, keep)
            finish(nc, io, keep)


_OUTS = [("y_prompt", (1, SEQ, D)), ("y_sample", (NB, NT, D)),
         ("a_k_prompt", (1, 1, A_WIN, 2, DH)), ("a_v_prompt", (1, 1, A_WIN, 2, DH)),
         ("b_k_prompt", (1, 1, SEQ, B_H, DH)), ("b_v_prompt", (1, 1, SEQ, B_H, DH)),
         ("conv_prompt", (1, 1, 2, BW)),
         ("a_k_sample", (1, NB, NT, 2, DH)), ("a_v_sample", (1, NB, NT, 2, DH)),
         ("b_k_sample", (1, NB, NT, B_H, DH)), ("b_v_sample", (1, NB, NT, B_H, DH)),
         ("conv_sample", (1, NB, 2, BW))]
_INS = ["x_prompt", "x_sample", "cache_a_k", "cache_a_v", "cache_b_k", "cache_b_v", "state_conv", "rel_bias_table",
        "w_in", "w_out", "conv_w", "attn_sinks", "norm_mix", "norm_ffn", "w_group", "b_group", "w_router", "b_router",
        "w_gate", "w_up", "w_down", "norm_final"]


def kernel(**inputs):
    import numpy as _np
    import concourse.bacc as _bacc
    from concourse import mybir as _mybir
    from concourse.bass_utils import run_bass_kernel_spmd as _run

    nc = _bacc.Bacc("TRN2", target_bir_lowering=False, num_devices=1)
    arrays = {name: _np.ascontiguousarray(inputs[name]) for name in _INS}
    arrays |= constants()
    ins = {n: nc.dram_tensor(f"in_{n}", a.shape, _mybir.dt.from_np(a.dtype), kind="ExternalInput").ap()
           for n, a in arrays.items()}
    outs = {n: nc.dram_tensor(f"out_{n}", shape, _mybir.dt.float32, kind="ExternalOutput").ap() for n, shape in _OUTS}
    program(nc, ins, outs)
    r = _run(nc, [{f"in_{n}": a for n, a in arrays.items()}], core_ids=[0])
    return tuple(r.results[0][f"out_{n}"] for n, _ in _OUTS)
```
